# Optimizing a Trainium2 kernel written in Bass

```python
import jax, jax.numpy as jnp
from jax import lax
import numpy as np

D_MODEL = 1024
BATCH = 1
SEQ = 256
DEPTH = 2

CHUNK = 64
N_MIXERS = 2
CONV_WIDTH = 31
HGRN_EXPAND = 128
HGRN_HEADS = D_MODEL // HGRN_EXPAND
HEAD_K = HGRN_EXPAND
HEAD_V = D_MODEL // HGRN_HEADS
FFN_DIM = 2816
N_EXPERTS = 8
TOP_K = 2
EXPERT_DIM = 3584
N_EVEN = (DEPTH + 1) // 2
N_ODD = DEPTH // 2
EPS = 1e-6

kernel_name = "hybrid_conformer_hgrn2_moe_trunk"

def rms_norm(x, g):
    xf = x.astype(jnp.float32)
    y = xf * lax.rsqrt(jnp.mean(xf * xf, axis=-1, keepdims=True) + EPS)
    return (y * g.astype(jnp.float32)).astype(x.dtype)

def layer_norm(x, g, b):
    xf = x.astype(jnp.float32)
    mu = jnp.mean(xf, axis=-1, keepdims=True)
    xc = xf - mu
    y = xc * lax.rsqrt(jnp.mean(xc * xc, axis=-1, keepdims=True) + EPS)
    return (y * g.astype(jnp.float32) + b.astype(jnp.float32)).astype(x.dtype)

def causal_depthwise_conv(u, w, b):
    width = w.shape[0]
    y = lax.conv_general_dilated(
        u, w[:, None, :].astype(u.dtype), window_strides=(1,),
        padding=[(width - 1, 0)], dimension_numbers=('NWC', 'WIO', 'NWC'),
        feature_group_count=u.shape[-1])
    return y + b

def conformer_conv_module(h, w_in, b_in, dw_w, dw_b, ln_g, ln_b, w_out, b_out):
    u = h @ w_in + b_in
    a, gate = jnp.split(u, 2, axis=-1)
    u = a * jax.nn.sigmoid(gate)
    u = causal_depthwise_conv(u, dw_w, dw_b)
    u = jax.nn.silu(layer_norm(u, ln_g, ln_b))
    return u @ w_out + b_out

def gated_linear_recurrence_chunkwise(q, k, v, g):
    b_, l_, h_, kd = q.shape
    vd = v.shape[-1]
    n_chunks = l_ // CHUNK

    def to_chunks(t):
        return t.reshape(b_, n_chunks, CHUNK, h_, t.shape[-1]).transpose(1, 0, 3, 2, 4)

    qc, kc, vc, gc = to_chunks(q), to_chunks(k), to_chunks(v), to_chunks(g)
    causal = jnp.tril(jnp.ones((CHUNK, CHUNK), dtype=bool))[:, :, None]

    def step(state, inp):
        qb, kb, vb, gb = inp
        big_g = jnp.cumsum(gb, axis=2)
        o_inter = jnp.einsum('bhtk,bhkv->bhtv', qb * jnp.exp(big_g), state)
        rel = big_g[:, :, :, None, :] - big_g[:, :, None, :, :]
        decay = jnp.exp(jnp.where(causal, rel, -jnp.inf))
        scores = jnp.einsum('bhtk,bhsk,bhtsk->bhts', qb, kb, decay)
        o_intra = jnp.einsum('bhts,bhsv->bhtv', scores, vb)
        g_last = big_g[:, :, -1:, :]
        k_dec = kb * jnp.exp(g_last - big_g)
        state = (jnp.exp(g_last[:, :, 0, :])[..., None] * state
                 + jnp.einsum('bhsk,bhsv->bhkv', k_dec, vb))
        return state, o_inter + o_intra

    s0 = jnp.zeros((b_, h_, kd, vd), jnp.float32)
    _, o = lax.scan(step, s0, (qc, kc, vc, gc))
    return o.transpose(1, 0, 3, 2, 4).reshape(b_, l_, h_, vd)

def hgrn2_mixer(h, w_in, lower_bound, norm_g, w_out):
    b_, l_, _ = h.shape
    proj = h @ w_in
    q, f, i, out_gate = jnp.split(proj, 4, axis=-1)
    q = jax.nn.silu(q).astype(jnp.float32).reshape(b_, l_, HGRN_HEADS, HEAD_K)
    lb = lower_bound.astype(jnp.float32)
    forget = lb + (1.0 - lb) * jax.nn.sigmoid(f.astype(jnp.float32))
    k = (1.0 - forget).reshape(b_, l_, HGRN_HEADS, HEAD_K)
    g = jnp.log(forget).reshape(b_, l_, HGRN_HEADS, HEAD_K)
    v = i.astype(jnp.float32).reshape(b_, l_, HGRN_HEADS, HEAD_V)
    o = gated_linear_recurrence_chunkwise(q, k, v, g)
    o = rms_norm(o, norm_g).reshape(b_, l_, D_MODEL).astype(h.dtype)
    o = o * jax.nn.silu(out_gate)
    return o @ w_out

def swiglu(h, w_gu, w_down):
    gate, up = jnp.split(h @ w_gu, 2, axis=-1)
    return (jax.nn.silu(gate) * up) @ w_down

def moe_swiglu(h, w_router, w_gu, w_down):
    logits = jnp.einsum('bld,de->ble', h, w_router).astype(jnp.float32)
    top_val, top_idx = lax.top_k(logits, TOP_K)
    top_w = jax.nn.softmax(top_val, axis=-1)
    gates = jnp.sum(jax.nn.one_hot(top_idx, N_EXPERTS, dtype=jnp.float32)
                    * top_w[..., None], axis=-2)
    out = jnp.zeros_like(h)
    for e in range(N_EXPERTS):
        out = out + gates[..., e:e + 1].astype(h.dtype) * swiglu(h, w_gu[e], w_down[e])
    return out

def setup_inputs(seed: int = 0) -> dict:
    key = jax.random.key(seed)
    ks = jax.random.split(key, 24)
    d, f32 = D_MODEL, jnp.float32

    def nrm(k, shape, fan_in, scale=1.0):
        return jax.random.normal(k, shape, f32) * (scale * fan_in ** -0.5)

    def gain(k, shape):
        return 1.0 + 0.05 * jax.random.normal(k, shape, f32)

    def bias(k, shape):
        return 0.02 * jax.random.normal(k, shape, f32)

    return {
        "x": jax.random.normal(ks[0], (BATCH, SEQ, d), f32),
        "norm_g": gain(ks[1], (DEPTH, 4, d)),
        "conv_w_in": nrm(ks[2], (N_EVEN, d, 2 * d), d),
        "conv_b_in": bias(ks[3], (N_EVEN, 2 * d)),
        "conv_dw_w": nrm(ks[4], (N_EVEN, CONV_WIDTH, d), CONV_WIDTH),
        "conv_dw_b": bias(ks[5], (N_EVEN, d)),
        "conv_ln_g": gain(ks[6], (N_EVEN, d)),
        "conv_ln_b": bias(ks[7], (N_EVEN, d)),
        "conv_w_out": nrm(ks[8], (N_EVEN, d, d), d),
        "conv_b_out": bias(ks[9], (N_EVEN, d)),
        "hgrn_w_in": nrm(ks[10], (N_ODD, d, 4 * d), d),
        "hgrn_lower_bounds": 0.5 * jax.random.normal(ks[11], (DEPTH, d), f32),
        "hgrn_norm_g": gain(ks[12], (N_ODD, HEAD_V)),
        "hgrn_w_out": nrm(ks[13], (N_ODD, d, d), d),
        "ffn_w_gu": nrm(ks[14], (N_EVEN, d, 2 * FFN_DIM), d),
        "ffn_w_down": nrm(ks[15], (N_EVEN, FFN_DIM, d), FFN_DIM),
        "moe_router": nrm(ks[16], (N_ODD, d, N_EXPERTS), d),
        "moe_w_gu": nrm(ks[17], (N_ODD, N_EXPERTS, d, 2 * EXPERT_DIM), d),
        "moe_w_down": nrm(ks[18], (N_ODD, N_EXPERTS, EXPERT_DIM, d), EXPERT_DIM),
    }

def reference(x, norm_g, conv_w_in, conv_b_in, conv_dw_w, conv_dw_b, conv_ln_g, conv_ln_b,
              conv_w_out, conv_b_out, hgrn_w_in, hgrn_lower_bounds, hgrn_norm_g, hgrn_w_out,
              ffn_w_gu, ffn_w_down, moe_router, moe_w_gu, moe_w_down):
    lb_all = jnp.cumsum(jax.nn.softmax(hgrn_lower_bounds.astype(jnp.float32), axis=0), axis=0)
    lb_all = lb_all - lb_all[0:1]
    h = x
    for i in range(DEPTH):
        j = i // 2
        u = rms_norm(h, norm_g[i, 0])
        if i % N_MIXERS == 0:
            u = conformer_conv_module(u, conv_w_in[j], conv_b_in[j], conv_dw_w[j], conv_dw_b[j],
                                      conv_ln_g[j], conv_ln_b[j], conv_w_out[j], conv_b_out[j])
        else:
            u = hgrn2_mixer(u, hgrn_w_in[j], lb_all[i], hgrn_norm_g[j], hgrn_w_out[j])
        h = h + rms_norm(u, norm_g[i, 1])
        u = rms_norm(h, norm_g[i, 2])
        if i % 2 == 0:
            u = swiglu(u, ffn_w_gu[j], ffn_w_down[j])
        else:
            u = moe_swiglu(u, moe_router[j], moe_w_gu[j], moe_w_down[j])
        h = h + rms_norm(u, norm_g[i, 3])
    return h


_drawn_inputs = setup_inputs


def setup_inputs(seed=0):
    import zlib

    import numpy as np

    out = dict(_drawn_inputs(seed))
    spreads = {}
    factors = {}
    for name, (base, spread) in spreads.items():
        noise = np.random.default_rng([zlib.crc32(name.encode()), seed]).standard_normal(out[name].shape)
        drawn = base * np.exp(spread * noise) if base else spread * noise
        out[name] = __import__('jax').numpy.asarray(drawn.astype(out[name].dtype))
    for name, factor in factors.items():
        out[name] = (out[name] * factor).astype(out[name].dtype)
    return out
```

```python
from contextlib import ExitStack

import concourse.bass as bass
from concourse import mybir

F32 = mybir.dt.float32
F32R = mybir.dt.float32r
I32 = mybir.dt.int32
U32 = mybir.dt.uint32
ACT = mybir.ActivationFunctionType
ALU = mybir.AluOpType
AX = mybir.AxisListType

P = 128
EPS = 1e-6
BANK = 512
PIECE = 2048
SCATTER_BANKS = (3, 4, 7, 2)
RAW_RING = 6
SPLIT_RING = 3


def trunk(nc, x, norm_g, conv_w_in, conv_b_in, conv_dw_w, conv_dw_b, conv_ln_g, conv_ln_b,
          conv_w_out, conv_b_out, hgrn_w_in, hgrn_lower_bounds, hgrn_norm_g, hgrn_w_out,
          ffn_w_gu, ffn_w_down, moe_router, moe_w_gu, moe_w_down, out):
    _, S, D = x.shape
    TT = S // P
    KT = D // P
    W = conv_dw_w.shape[1]
    FFN = ffn_w_down.shape[1]
    E = moe_router.shape[2]
    ED = moe_w_down.shape[2]
    HEADS = D // P
    HB = HEADS * TT
    FFN_CHUNK = 256
    FFN_STEPS = FFN // FFN_CHUNK
    MOE_CHUNK = 512
    MOE_STEPS = ED // MOE_CHUNK
    JOBS = 2 * E
    LEVELS = [64, 32, 16, 8, 4, 2, 1]
    assert TT == 2 and KT == 8 and FFN % FFN_CHUNK == 0 and ED % MOE_CHUNK == 0 and FFN_STEPS % 2 == 1

    CONV_IN = 0
    CONV_OUT = CONV_IN + 2 * D * KT * P // (P * PIECE)
    FFN0 = CONV_OUT + D * D // (P * PIECE)
    HGRN_QF = FFN0 + 3 * FFN_STEPS
    HGRN_VG = HGRN_QF + 2 * D * D // (P * PIECE)
    HGRN_OUT = HGRN_VG + 2 * D * D // (P * PIECE)
    MOE = HGRN_OUT + D * D // (P * PIECE)
    EXPERT_PIECES = 6 * MOE_STEPS
    EXPERT_TURNS = EXPERT_PIECES // RAW_RING

    with ExitStack() as ctx:
        def sb(name, shape, dt=F32):
            return ctx.enter_context(nc.sbuf_tensor(name, shape, dt))

        def sem(name):
            return ctx.enter_context(nc.semaphore(name))

        raw = sb("raw", [P, RAW_RING, PIECE])
        w_hi = sb("w_hi", [P, SPLIT_RING, PIECE], F32R)
        w_lo = sb("w_lo", [P, SPLIT_RING, PIECE], F32R)
        xt_hi = sb("xt_hi", [P, KT, S], F32R)
        xt_lo = sb("xt_lo", [P, KT, S], F32R)
        ht_hi = sb("ht_hi", [P, 512], F32R)
        ht_lo = sb("ht_lo", [P, 512], F32R)
        h = sb("h", [P, TT, D])
        row = sb("row", [P, 2, D])
        scratch = sb("scratch", [P, 17408])
        cols = sb("cols", [P, 376])
        ident = sb("ident", [P, P])
        ones = sb("ones", [P, P])
        before = sb("before", [P, P])
        slot_i = sb("slot_i", [P, P], I32)
        slot_p = sb("slot_p", [P, 1], I32)
        slot_id = sb("slot_id", [P, P])
        ssq = sb("ssq", [P, TT])
        var = sb("var", [P, HB])
        root = sb("root", [P, HB])
        rstd = sb("rstd", [P, HB])
        newton = sb("newton", [P, 2, HB])
        lb_t = sb("lb_t", [P, 6, KT])
        lb_c = sb("lb_c", [P, 2, KT])
        logits = sb("logits", [P, TT, E])
        top = sb("top", [P, TT, 8])
        top_i = sb("top_i", [P, TT, 8], U32)
        top_f = sb("top_f", [P, TT, 8])
        chosen = sb("chosen", [P, 2, TT, E])
        sel = sb("sel", [P, TT, E])
        weight = sb("weight", [P, 4, TT])
        place = sb("place", [P, TT, E])
        busiest = sb("busiest", [P, 2])
        router = sb("router", [P, KT, E])
        router_hi = sb("router_hi", [P, KT, E], F32R)
        router_lo = sb("router_lo", [P, KT, E], F32R)
        slot_of = sb("slot_of", [P, TT, JOBS])
        gate_of = sb("gate_of", [P, TT, JOBS])
        tick = sb("tick", [P, 1])
        jobs_n = sb("jobs_n", [P, 1], I32)

        class Cut:
            at = 0

            @classmethod
            def take(cls, n):
                cls.at += n
                assert cls.at <= 17408, cls.at
                return scratch[:, cls.at - n:cls.at]

        Cut.at = 0
        tok = Cut.take(TT * D).rearrange("p (t d) -> p t d", t=TT)
        junk = Cut.take(TT * D)
        Cut.at = 0
        conv_u = Cut.take(KT * (S + W - 1)).rearrange("p (k s) -> p k s", k=KT)
        conv_y = Cut.take(KT * S).rearrange("p (k s) -> p k s", k=KT)
        conv_sq = Cut.take(KT * S).rearrange("p (k s) -> p k s", k=KT)
        conv_sig = Cut.take(4 * S).rearrange("p (k s) -> p k s", k=4)
        conv_mean = Cut.take(S)
        conv_var = Cut.take(S)
        conv_r = Cut.take(S)
        conv_t = Cut.take(S)
        Cut.at = 2 * TT * D
        act_sb = Cut.take(512)
        hid = Cut.take(512)
        Cut.at = 0
        hq = Cut.take(HEADS * S)
        hk = Cut.take(HEADS * S)
        hg = Cut.take(HEADS * S)
        lev = [Cut.take(HEADS * S) for _ in range(2)]
        hv = Cut.take(TT * D)
        hog = Cut.take(TT * D)
        s_same = Cut.take(HB * P)
        s_cross = Cut.take(HEADS * P)
        ho = hq.rearrange("p (t d) -> p t d", t=TT)
        hsq = hk
        Cut.at = 0
        mx = Cut.take(TT * D).rearrange("p (t d) -> p t d", t=TT)
        Cut.take(TT * D)
        Cut.take(1024)
        acc = Cut.take(TT * D).rearrange("p (t d) -> p t d", t=TT)
        ysb = Cut.take(D)
        pick = Cut.take(TT * P).rearrange("p (t s) -> p t s", t=TT)
        pick_t = Cut.take(TT * P)
        level_mask = sb("level_mask", [P, len(LEVELS), P], mybir.dt.uint8)
        prow = s_same[:, 0:3 * P].rearrange("p (a b) -> p a b", a=3)

        psum = ctx.enter_context(nc.psum_tensor("psum", [P, 8, BANK], F32))

        LBD = hgrn_lower_bounds.shape[0]
        NG = 0
        B_IN = NG + 8 * KT
        DW_B = B_IN + 2 * KT
        LN_G = DW_B + KT
        LN_B = LN_G + KT
        LB = LN_B + KT
        ROWS0 = LB + LBD * KT
        TAPS = P
        HALF_W = (W + 1) // 2

        def tap_col(w, k):
            a, b = divmod(w, HALF_W)
            return TAPS + a * (HALF_W * KT) + b * KT + k

        raw_loaded = [sem(f"raw_loaded{i}") for i in range(RAW_RING)]
        hi_ready = sem("hi_ready")
        lo_ready = sem("lo_ready")
        piece_used = sem("piece_used")
        x_loaded = sem("x_loaded")
        rows_loaded = sem("rows_loaded")
        small_loaded = sem("small_loaded")
        row_loaded = [sem(f"row_loaded{i}") for i in range(2)]
        row_used = [sem(f"row_used{i}") for i in range(2)]
        consts_ready = sem("consts_ready")
        cols_turned = sem("cols_turned")
        cols_ready = sem("cols_ready")
        lb_arg = sem("lb_arg")
        lb_exp = sem("lb_exp")
        dve_step = sem("dve_step")
        act_step = sem("act_step")
        squares_ready = sem("squares_ready")
        variance_ready = sem("variance_ready")
        root_ready = sem("root_ready")
        normed = sem("normed")
        turned = sem("turned")
        turn_hi = sem("turn_hi")
        turn_lo = sem("turn_lo")
        source_ready = sem("source_ready")
        source_half = sem("source_half")
        residual_ready = sem("residual_ready")
        glu_sig = sem("glu_sig")
        glu_out = sem("glu_out")
        conv_done = sem("conv_done")
        mean_sum = sem("mean_sum")
        centred = sem("centred")
        conv_squared = sem("conv_squared")
        var_sum = sem("var_sum")
        conv_scaled = sem("conv_scaled")
        conv_act = sem("conv_act")
        conv_hi = sem("conv_hi")
        conv_lo = sem("conv_lo")
        tap_added = sem("tap_added")
        ffn_silu = sem("ffn_silu")
        ffn_hid = sem("ffn_hid")
        ffn_turned = sem("ffn_turned")
        ffn_ht_hi = sem("ffn_ht_hi")
        ffn_ht_lo = sem("ffn_ht_lo")
        qf_sig = sem("qf_sig")
        q_ready = sem("q_ready")
        forget_ready = sem("forget_ready")
        log_ready = sem("log_ready")
        level_arg = sem("level_arg")
        level_exp = sem("level_exp")
        level_factors = sem("level_factors")
        level_scores = sem("level_scores")
        level_taken = sem("level_taken")
        vg_out = sem("vg_out")
        o_proj = sem("o_proj")
        o_squared = sem("o_squared")
        og_ready = sem("og_ready")
        gate_folded = sem("gate_folded")
        router_split = sem("router_split")
        router_hi_ready = sem("router_hi_ready")
        logits_done = sem("logits_done")
        sel_ready = sem("sel_ready")
        count_done = sem("count_done")
        gate_arg = sem("gate_arg")
        gate_exp = sem("gate_exp")
        tables_ready = sem("tables_ready")
        pick_ready = sem("pick_ready")
        gathered = sem("gathered")
        pick_turned = sem("pick_turned")
        pick_t_ready = sem("pick_t_ready")
        xg_hi = sem("xg_hi")
        xg_lo = sem("xg_lo")
        moe_silu = sem("moe_silu")
        moe_hid = sem("moe_hid")
        moe_turned = sem("moe_turned")
        moe_ht_hi = sem("moe_ht_hi")
        moe_ht_lo = sem("moe_ht_lo")
        y_ready = sem("y_ready")
        scattered = sem("scattered")
        acc_added = sem("acc_added")
        moe_done = sem("moe_done")
        out_stored = sem("out_stored")

        block = ctx.enter_context(nc.Block())

        def bank(i, n=1):
            return psum[:, i:i + n, :].rearrange("p b c -> p (b c)")

        @block.sync
        def _(sp):
            def load(p, parts, turns=0):
                if p >= RAW_RING:
                    sp.wait_ge(lo_ready, turns * RAW_RING + (p - RAW_RING + 1))
                for dst, src in parts:
                    sp.dma_start(dst, src).then_inc(raw_loaded[p % RAW_RING], 32 // len(parts))

            def by_channel(p, w, k0, c0, c1=None):
                r = w.rearrange("(k p) n -> p k n", p=P)[:, k0:k0 + 4, :]
                d = raw[:, p % RAW_RING, :].rearrange("p (k n) -> p k n", k=4)
                if c1 is None:
                    return [(d, r[:, :, bass.ds(c0, 512)])]
                return [(d[:, :, 0:256], r[:, :, bass.ds(c0, 256)]), (d[:, :, 256:512], r[:, :, bass.ds(c1, 256)])]

            def by_row(p, w, r0):
                d = raw[:, p % RAW_RING, :].rearrange("p (k n) -> p k n", k=2)
                return [(d, w[bass.ds(r0, 2 * P), :].rearrange("(k p) n -> p k n", p=P))]

            sp.dma_start(h[:], x[0].rearrange("(t p) d -> p t d", p=P)).then_inc(x_loaded, 16)
            first_group = [
                (0, B_IN, norm_g.rearrange("l n (k c) -> (l n k) c", c=P)),
                (B_IN, DW_B, conv_b_in.rearrange("l (k c) -> (l k) c", c=P)),
                (DW_B, LN_G, conv_dw_b.rearrange("l (k c) -> (l k) c", c=P)),
                (LN_G, LN_B, conv_ln_g.rearrange("l (k c) -> (l k) c", c=P)),
                (LN_B, LB, conv_ln_b.rearrange("l (k c) -> (l k) c", c=P)),
                (LB, ROWS0, hgrn_lower_bounds.rearrange("l (k c) -> (l k) c", c=P)),
            ]
            for a, b, src in first_group:
                sp.dma_start(prow[a:b, 0, :], src).then_inc(rows_loaded, 16)
            taps = conv_dw_w[0].rearrange("w (k c) -> (w k) c", c=P)
            sp.dma_start(prow[0:HALF_W * KT, 1, :], taps[0:HALF_W * KT, :]).then_inc(rows_loaded, 16)
            sp.dma_start(prow[0:(W - HALF_W) * KT, 2, :], taps[HALF_W * KT:W * KT, :]).then_inc(rows_loaded, 16)

            w = conv_w_in[0]
            order = [(c, kh) for c in range(4) for kh in range(2)]
            pieces = [by_channel(CONV_IN + n, w, 4 * kh, 256 * c, D + 256 * c) for n, (c, kh) in enumerate(order)]
            for p in range(CONV_OUT):
                load(p, pieces[p])
            for n in range(4):
                load(CONV_OUT + n, by_row(CONV_OUT + n, conv_w_out[0], 256 * n))
            gu, dn = ffn_w_gu[0], ffn_w_down[0]
            for kh in range(2):
                load(FFN0 + kh, by_channel(FFN0 + kh, gu, 4 * kh, 0, FFN))
            with sp.Fori(0, FFN_STEPS // 2) as i:
                for j in range(2):
                    p = FFN0 + 2 + 3 * j
                    col = (i * 2 + (1 + j)) * FFN_CHUNK
                    for kh in range(2):
                        load(p + kh, by_channel(p + kh, gu, 4 * kh, col, col + FFN), i)
                    load(p + 2, by_row(p + 2, dn, (i * 2 + j) * FFN_CHUNK), i)
            p = HGRN_QF - 1
            load(p, by_row(p, dn, (FFN_STEPS - 1) * FFN_CHUNK))
            w = hgrn_w_in[0]
            for n, (c, kh) in enumerate(order):
                load(HGRN_QF + n, by_channel(HGRN_QF + n, w, 4 * kh, 256 * c, D + 256 * c))
            for n, (c, kh) in enumerate(order):
                load(HGRN_VG + n, by_channel(HGRN_VG + n, w, 4 * kh, 2 * D + 512 * c))
            for n in range(4):
                load(HGRN_OUT + n, by_row(HGRN_OUT + n, hgrn_w_out[0], 256 * n))

            def expert(e, turns):
                gu, dn = moe_w_gu[0][e, :, :], moe_w_down[0][e, :, :]
                for g in range(2):
                    for kh in range(2):
                        p = MOE + 2 * g + kh
                        load(p, by_channel(p, gu, 4 * kh, g * ED), turns)
                with sp.Fori(1, MOE_STEPS) as c:
                    t = turns + (c - 1)
                    for g in range(2):
                        for kh in range(2):
                            p = MOE + 4 + 2 * g + kh
                            load(p, by_channel(p, gu, 4 * kh, c * MOE_CHUNK + g * ED), t)
                    for n in range(2):
                        p = MOE + 8 + n
                        load(p, by_row(p, dn, (c - 1) * MOE_CHUNK + 256 * n), t)
                for n in range(2):
                    p = MOE + 4 + n
                    load(p, by_row(p, dn, (MOE_STEPS - 1) * MOE_CHUNK + 256 * n), turns + (MOE_STEPS - 1))

            with sp.Fori(0, E) as e:
                expert(e, e * EXPERT_TURNS)
            sp.wait_ge(tables_ready, 1)
            jobs = sp.value_load(jobs_n[0:1, 0:1], min_val=E, max_val=JOBS)
            with sp.If(jobs > E):
                with sp.Fori(0, E) as e:
                    expert(e, (e + E) * EXPERT_TURNS)
            sp.wait_ge(residual_ready, 4)
            sp.dma_start(out[0].rearrange("(t p) d -> p t d", p=P), h[:]).then_inc(out_stored, 16)
            sp.wait_ge(out_stored, 16)

        @block.gpsimd
        def _(pool):
            nc.gpsimd.memset(ones[:], 1.0).then_inc(consts_ready, 1)
            nc.gpsimd.iota(slot_i[:], pattern=[[1, P]], base=0, channel_multiplier=0)
            nc.gpsimd.iota(slot_p[:], pattern=[[0, 1]], base=0, channel_multiplier=1).then_inc(consts_ready, 1)
            pool.wait_ge(consts_ready, 2)
            nc.gpsimd.affine_select(out=ident[:], in_=ones[:], compare_op=ALU.is_equal, fill=0.0, base=0,
                                    pattern=[[-1, P]], channel_multiplier=1).then_inc(consts_ready, 1)
            nc.gpsimd.affine_select(out=before[:], in_=ones[:], compare_op=ALU.is_gt, fill=0.0, base=0,
                                    pattern=[[1, P]], channel_multiplier=-1).then_inc(consts_ready, 1)

            def load_row(i, src, n):
                if n:
                    pool.wait_ge(row_used[i], n)
                pool.dma_start(row[:, i, 0:src.shape[-1]], src.partition_broadcast(P)).then_inc(row_loaded[i], 16)

            load_row(0, conv_b_out[0], 0)
            load_row(1, norm_g[0, 1], 0)
            pool.dma_start(router[:], moe_router[0].rearrange("(k p) e -> p k e", p=P)).then_inc(small_loaded, 16)
            load_row(0, hgrn_norm_g[0], 1)
            load_row(1, norm_g[0, 3], 1)
            load_row(1, norm_g[1, 1], 2)
            load_row(0, norm_g[1, 2], 2)
            load_row(1, norm_g[1, 3], 3)

        @block.tensor
        def _(pe):
            mm = nc.tensor.matmul

            def wait_hi(p, turns=0):
                pe.wait_ge(hi_ready, turns * RAW_RING + (p + 1))

            def wait_lo(p, turns=0):
                pe.wait_ge(lo_ready, turns * RAW_RING + (p + 1))

            def turn(n, src):
                pe.wait_ge(normed, n + 1)
                for k in range(KT):
                    for t in range(TT):
                        last = nc.tensor.transpose(psum[:, k // 2, (k % 2) * S + t * P:(k % 2) * S + (t + 1) * P],
                                                   src[:, t, k * P:(k + 1) * P], ident[:])
                    if k % 2:
                        last.then_inc(turned, 1)
                pe.wait_ge(turn_lo, 4 * (n + 1))

            def channel_out(p, kh, banks):
                for part, rhss in ((w_hi, (xt_hi, xt_lo)), (w_lo, (xt_hi,))):
                    (wait_hi if part is w_hi else wait_lo)(p)
                    wv = part[:, p % SPLIT_RING, :].rearrange("p (k n) -> p k n", k=4)
                    for kk in range(4):
                        for b in range(4):
                            for rhs in rhss:
                                first = kh == 0 and kk == 0 and b % 2 == 0 and part is w_hi and rhs is xt_hi
                                last = mm(psum[:, banks + b // 2, (b % 2) * S:(b % 2 + 1) * S],
                                          wv[:, kk, b * P:(b + 1) * P], rhs[:, 4 * kh + kk, :],
                                          start=first, stop=kh == 1 and kk == 3 and part is w_lo,
                                          skip_group_check=True)
                last.then_inc(piece_used, 1)

            def token_cols(p, kh, banks, tiles, turns=0):
                for part, lhss in ((w_hi, (xt_hi, xt_lo)), (w_lo, (xt_hi,))):
                    (wait_hi if part is w_hi else wait_lo)(p, turns)
                    wv = part[:, p % SPLIT_RING, :].rearrange("p (k n) -> p k n", k=4)
                    for kk in range(4):
                        for t in range(tiles):
                            for lhs in lhss:
                                last = mm(psum[:, banks[t], :], lhs[:, 4 * kh + kk, t * P:(t + 1) * P], wv[:, kk, :],
                                          start=kh == 0 and kk == 0 and part is w_hi and lhs is xt_hi,
                                          stop=kh == 1 and kk == 3 and part is w_lo)
                last.then_inc(piece_used, 1)

            def token_rows(p, operands, banks, tiles, first, final, turns=0):
                for part in (w_hi, w_lo):
                    (wait_hi if part is w_hi else wait_lo)(p, turns)
                    wv = part[:, p % SPLIT_RING, :].rearrange("p (k n) -> p k n", k=2)
                    for kk in range(2):
                        for t in range(tiles):
                            for i, lhs in enumerate(operands(kk, t)[:2 if part is w_hi else 1]):
                                for half in range(2):
                                    last = mm(psum[:, banks + 2 * t + half, :], lhs,
                                              wv[:, kk, half * BANK:(half + 1) * BANK],
                                              start=first and kk == 0 and part is w_hi and i == 0,
                                              stop=final and kk == 1 and part is w_lo)
                last.then_inc(piece_used, 1)

            def from_xt(k0):
                return lambda k, t: (xt_hi[:, k0 + k, t * P:(t + 1) * P], xt_lo[:, k0 + k, t * P:(t + 1) * P])

            pe.wait_ge(consts_ready, 4)
            pe.wait_ge(rows_loaded, 8 * 16)
            n = (W - HALF_W) * KT
            nc.tensor.transpose(psum[:, 4, 0:ROWS0], prow[0:ROWS0, 0, :], ident[0:ROWS0, 0:ROWS0])
            nc.tensor.transpose(psum[:, 4, P:P + HALF_W * KT], prow[0:HALF_W * KT, 1, :],
                                ident[0:HALF_W * KT, 0:HALF_W * KT])
            nc.tensor.transpose(psum[:, 4, P + HALF_W * KT:P + HALF_W * KT + n], prow[0:n, 2, :],
                                ident[0:n, 0:n]).then_inc(cols_turned, 1)

            turn(0, tok)
            for c in range(4):
                if c >= 2:
                    pe.wait_ge(glu_out, c - 1)
                for kh in range(2):
                    channel_out(CONV_IN + 2 * c + kh, kh, 2 * (c % 2))
            pe.wait_ge(conv_done, 4)
            for k in range(KT):
                last = mm(psum[:, 4, 0:S], ones[:], conv_y[:, k, :], start=k == 0, stop=k == KT - 1)
            last.then_inc(mean_sum, 1)
            pe.wait_ge(conv_squared, 1)
            for k in range(KT):
                last = mm(psum[:, 5, 0:S], ones[:], conv_sq[:, k, :], start=k == 0, stop=k == KT - 1)
            last.then_inc(var_sum, 1)
            pe.wait_ge(conv_lo, 1)
            for n in range(4):
                token_rows(CONV_OUT + n, from_xt(2 * n), 4, TT, n == 0, n == 3)

            turn(1, tok)

            def ffn_turn(c):
                pe.wait_ge(ffn_hid, c + 1)
                for k in range(2):
                    for t in range(TT):
                        last = nc.tensor.transpose(psum[:, 2, k * S + t * P:k * S + (t + 1) * P],
                                                   hid[:, t * 256 + k * P:t * 256 + (k + 1) * P], ident[:])
                last.then_inc(ffn_turned, 1)

            def ffn_hidden(k, t):
                return ht_hi[:, k * S + t * P:k * S + (t + 1) * P], ht_lo[:, k * S + t * P:k * S + (t + 1) * P]

            def ffn_step(j, c, i, opens=False):
                p = FFN0 + 2 + 3 * j
                pe.wait_ge(ffn_hid, c + 1)
                token_cols(p, 0, (0, 1), TT, i)
                ffn_turn(c)
                token_cols(p + 1, 1, (0, 1), TT, i)
                pe.wait_ge(ffn_ht_lo, c + 1)
                token_rows(p + 2, ffn_hidden, 4, TT, opens, False, i)

            for kh in range(2):
                token_cols(FFN0 + kh, kh, (0, 1), TT)
            for j in range(2):
                ffn_step(j, j, 0, j == 0)
            with pe.Fori(1, FFN_STEPS // 2) as i:
                for j in range(2):
                    ffn_step(j, i * 2 + j, i)
            ffn_turn(FFN_STEPS - 1)
            pe.wait_ge(ffn_ht_lo, FFN_STEPS)
            token_rows(HGRN_QF - 1, ffn_hidden, 4, TT, False, True)

            turn(2, tok)
            for c in range(4):
                if c >= 2:
                    pe.wait_ge(q_ready, c - 1)
                for kh in range(2):
                    channel_out(HGRN_QF + 2 * c + kh, kh, 2 * (c % 2))

            def scores(n):
                f = lev[n % 2]
                if n:
                    pe.wait_ge(level_factors, n)
                    pe.wait_ge(level_taken, n)
                cross = n == len(LEVELS) + 1
                for b in range(HEADS if cross else HB):
                    s, t = (2 * b, 2 * b + 1) if cross else (b, b)
                    keys, queries = (f, f) if n else (hk, hq)
                    last = mm(psum[:, 4 + b // 4, (b % 4) * P:(b % 4 + 1) * P], keys[:, s * P:(s + 1) * P],
                              queries[:, t * P:(t + 1) * P], start=True, stop=True)
                last.then_inc(level_scores, 1)

            pe.wait_ge(q_ready, 4)
            for n in range(8):
                c, kh = divmod(n, 2)
                if c >= 2:
                    pe.wait_ge(vg_out, c - 1)
                token_cols(HGRN_VG + n, kh, (2 * (c % 2), 2 * (c % 2) + 1), TT)
                if n:
                    scores(n - 1)
            scores(len(LEVELS))
            scores(len(LEVELS) + 1)
            pe.wait_ge(level_taken, len(LEVELS) + 2)
            pe.wait_ge(vg_out, 4)
            for t in range(TT):
                for hd in range(HEADS):
                    o = psum[:, 2 * t + hd // 4, (hd % 4) * P:(hd % 4 + 1) * P]
                    b = (hd * TT + t) * P
                    if t:
                        mm(o, s_cross[:, hd * P:(hd + 1) * P], hv[:, hd * P:(hd + 1) * P], start=True, stop=False)
                    last = mm(o, s_same[:, b:b + P], hv[:, t * D + hd * P:t * D + (hd + 1) * P],
                              start=t == 0, stop=True)
            last.then_inc(o_proj, 1)
            turn(3, ho)
            for n in range(4):
                token_rows(HGRN_OUT + n, from_xt(2 * n), 4, TT, n == 0, n == 3)

            turn(4, mx)
            pe.wait_ge(router_split, 1)
            for t in range(TT):
                ops = ((xt_hi, router_hi), (xt_lo, router_hi), (xt_hi, router_lo))
                for i, (a, b) in enumerate(ops):
                    for k in range(KT):
                        last = mm(psum[:, 7, t * E:(t + 1) * E], a[:, k, t * P:(t + 1) * P], b[:, k, :],
                                  start=i == 0 and k == 0, stop=i == 2 and k == KT - 1)
            last.then_inc(logits_done, 1)
            pe.wait_ge(sel_ready, 1)
            mm(psum[:, 6, 0:E], before[:], sel[:, 0, :], start=True, stop=True)
            mm(psum[:, 6, E:2 * E], before[:], sel[:, 1, :], start=True, stop=False)
            mm(psum[:, 6, E:2 * E], ones[:], sel[:, 0, :], start=False, stop=True)
            mm(psum[:, 6, 2 * E:3 * E], ones[:], sel[:, 0, :], start=True, stop=False)
            mm(psum[:, 6, 2 * E:3 * E], ones[:], sel[:, 1, :], start=False, stop=True).then_inc(count_done, 1)

            pe.wait_ge(tables_ready, 1)
            jobs = pe.value_load(jobs_n[0:1, 0:1], min_val=E, max_val=JOBS)

            def moe_turn(n):
                pe.wait_ge(moe_hid, n + 2)
                for k in range(4):
                    last = nc.tensor.transpose(psum[:, 2, k * P:(k + 1) * P], hid[:, k * P:(k + 1) * P], ident[:])
                last.then_inc(moe_turned, 1)

            def slot_hidden(k0):
                return lambda k, t: (ht_hi[:, (k0 + k) * P:(k0 + k + 1) * P],
                                     ht_lo[:, (k0 + k) * P:(k0 + k + 1) * P])

            def moe_step(n, turns, opens=False):
                pe.wait_ge(moe_silu, n + 1)
                for kh in range(2):
                    token_cols(MOE + 4 + kh, kh, (0,), 1, turns)
                moe_turn(n)
                for kh in range(2):
                    token_cols(MOE + 6 + kh, kh, (1,), 1, turns)
                pe.wait_ge(moe_ht_lo, n + 1)
                for kk in range(2):
                    token_rows(MOE + 8 + kk, slot_hidden(2 * kk), 5, 1, opens and kk == 0, False, turns)

            with pe.Fori(0, jobs) as j:
                turns = j * EXPERT_TURNS
                pe.wait_ge(pick_ready, j + 1)
                for k in range(KT):
                    for t in range(TT):
                        last = mm(psum[:, 3 + k // 4, (k % 4) * P:(k % 4 + 1) * P], mx[:, t, k * P:(k + 1) * P],
                                  pick[:, t, :], start=t == 0, stop=t == TT - 1)
                    if k % 4 == 3:
                        last.then_inc(gathered, 1)
                for t in range(TT):
                    last = nc.tensor.transpose(psum[:, 7, t * P:(t + 1) * P], pick[:, t, :], ident[:])
                last.then_inc(pick_turned, 1)
                pe.wait_ge(xg_lo, j * 2 + 2)
                for g in range(2):
                    for kh in range(2):
                        token_cols(MOE + 2 * g + kh, kh, (g,), 1, turns)
                moe_step(j * MOE_STEPS, turns, True)
                with pe.Fori(1, MOE_STEPS - 1) as c:
                    moe_step(j * MOE_STEPS + c, turns + c)
                n = j * MOE_STEPS + (MOE_STEPS - 1)
                moe_turn(n)
                pe.wait_ge(moe_ht_lo, n + 1)
                for kk in range(2):
                    token_rows(MOE + 4 + kk, slot_hidden(2 * kk), 5, 1, False, kk == 1, turns + (MOE_STEPS - 1))
                pe.wait_ge(y_ready, j + 1)
                pe.wait_ge(pick_t_ready, j + 1)
                for t in range(TT):
                    for half in range(2):
                        mm(psum[:, SCATTER_BANKS[2 * t + half], :], pick_t[:, t * P:(t + 1) * P],
                           ysb[:, half * BANK:(half + 1) * BANK], start=True, stop=True).then_inc(scattered, 1)

        @block.scalar
        def _(act):
            fn = nc.scalar.activation

            def hi(p, turns=0):
                act.wait_ge(raw_loaded[p % RAW_RING], turns * 32 + 32 * (p // RAW_RING + 1))
                if p >= SPLIT_RING:
                    act.wait_ge(piece_used, turns * RAW_RING + (p - SPLIT_RING + 1))
                fn(w_hi[:, p % SPLIT_RING, :], raw[:, p % RAW_RING, :], ACT.Copy).then_inc(hi_ready, 1)

            def squares(n, src):
                for t in range(TT):
                    fn(junk[:, t * D:(t + 1) * D], src(t), ACT.Square, accum_out=ssq[:, t:t + 1]).then_inc(
                        squares_ready, 1)

            def take_root(n, width):
                act.wait_ge(variance_ready, n + 1)
                fn(root[:, 0:width], var[:, 0:width], ACT.Sqrt).then_inc(root_ready, 1)

            def turn_hi_part(n, gain):
                for b in range(4):
                    act.wait_ge(turned, 4 * n + b + 1)
                    if gain is None:
                        fn(xt_hi[:, 2 * b:2 * b + 2, :], bank(b).rearrange("p (k s) -> p k s", k=2),
                           ACT.Copy).then_inc(turn_hi, 2)
                    else:
                        for k in (2 * b, 2 * b + 1):
                            fn(xt_hi[:, k, :], psum[:, b, (k % 2) * S:(k % 2 + 1) * S], ACT.Copy,
                               scale=cols[:, gain + k:gain + k + 1]).then_inc(turn_hi, 1)

            def used(p):
                act.wait_ge(piece_used, p + 1)

            act.wait_ge(x_loaded, 16)
            squares(0, lambda t: h[:, t, :])
            take_root(0, TT)
            for p in range(3):
                hi(p)
            act.wait_ge(lb_arg, 1)
            fn(lb_t[:, 2:4, :], lb_t[:, 0:2, :], ACT.Exp).then_inc(lb_exp, 1)
            act.wait_ge(cols_ready, 1)
            turn_hi_part(0, NG)
            hi(3)
            for c in range(4):
                used(2 * c + 1)
                if c >= 2:
                    act.wait_ge(glu_out, c - 1)
                for b in range(2):
                    k = 2 * c + b
                    fn(conv_sig[:, 2 * (c % 2) + b, :], psum[:, 2 * (c % 2) + 1, b * S:(b + 1) * S], ACT.Sigmoid,
                       bias=cols[:, B_IN + KT + k:B_IN + KT + k + 1]).then_inc(glu_sig, 1)
                for p in (4 + 2 * c, 5 + 2 * c):
                    if p < CONV_OUT + 2:
                        hi(p)
            act.wait_ge(centred, 1)
            fn(conv_sq[:, :, :], conv_y[:, :, :], ACT.Square).then_inc(conv_squared, 1)
            act.wait_ge(variance_ready, 2)
            fn(conv_t, conv_var, ACT.Sqrt).then_inc(root_ready, 1)
            act.wait_ge(conv_scaled, 1)
            for k in range(KT):
                fn(conv_sq[:, k, :], conv_y[:, k, :], ACT.Silu, scale=cols[:, LN_G + k:LN_G + k + 1],
                   bias=cols[:, LN_B + k:LN_B + k + 1]).then_inc(conv_act, 1)
            act.wait_ge(conv_act, KT)
            fn(xt_hi[:, :, :], conv_sq[:, :, :], ACT.Copy).then_inc(conv_hi, 1)
            hi(CONV_OUT + 2)
            hi(CONV_OUT + 3)
            hi(FFN0)
            act.wait_ge(source_ready, 1)
            squares(1, lambda t: tok[:, t, :])
            take_root(2, TT)
            act.wait_ge(residual_ready, 1)
            squares(2, lambda t: h[:, t, :])
            take_root(3, TT)
            turn_hi_part(1, NG + 2 * KT)
            hi(FFN0 + 1)

            def ffn_act(c, p):
                fn(act_sb.rearrange("p (t n) -> p t n", t=TT), psum[:, 0:TT, 0:FFN_CHUNK], ACT.Silu).then_inc(
                    ffn_silu, 1)

            def ffn_round(c):
                act.wait_ge(ffn_turned, c + 1)
                fn(ht_hi[:], bank(2), ACT.Copy).then_inc(ffn_ht_hi, 1)

            with act.Fori(0, FFN_STEPS // 2) as i:
                for j in range(2):
                    p = FFN0 + 2 + 3 * j
                    c = i * 2 + j
                    hi(p, i)
                    act.wait_ge(piece_used, i * RAW_RING + (p - 1))
                    act.wait_ge(piece_used, FFN0 + 2)
                    ffn_act(c, p)
                    hi(p + 1, i)
                    hi(p + 2, i)
                    ffn_round(c)
            hi(HGRN_QF - 1)
            used(HGRN_QF - 3)
            ffn_act(FFN_STEPS - 1, 0)
            hi(HGRN_QF)
            ffn_round(FFN_STEPS - 1)
            hi(HGRN_QF + 1)
            used(HGRN_QF - 1)
            squares(3, lambda t: bank(4 + 2 * t, 2))
            take_root(4, TT)
            act.wait_ge(residual_ready, 2)
            squares(4, lambda t: h[:, t, :])
            take_root(5, TT)
            turn_hi_part(2, NG + 4 * KT)
            hi(HGRN_QF + 2)
            hi(HGRN_QF + 3)
            for c in range(4):
                used(HGRN_QF + 2 * c + 1)
                fn(hq[:, c * 512:(c + 1) * 512], bank(2 * (c % 2)), ACT.Sigmoid).then_inc(qf_sig, 1)
                fn(hk[:, c * 512:(c + 1) * 512], bank(2 * (c % 2) + 1), ACT.Sigmoid).then_inc(qf_sig, 1)
                for p in (HGRN_QF + 4 + 2 * c, HGRN_QF + 5 + 2 * c)[:2 * (c < 3)]:
                    hi(p)
            hi(HGRN_VG + 2)
            act.wait_ge(forget_ready, 1)
            fn(lev[0], lev[0], ACT.Ln).then_inc(log_ready, 1)

            def level(n):
                act.wait_ge(level_arg, n)
                fn(lev[n % 2], lev[n % 2], ACT.Exp).then_inc(level_exp, 1)

            level(1)
            for n in range(1, 8):
                level(n + 1)
                if HGRN_VG + 2 + n < HGRN_OUT:
                    hi(HGRN_VG + 2 + n)
                if n % 2:
                    c = n // 2
                    used(HGRN_VG + 2 * c + 1)
                    dst = (hv if c < 2 else hog).rearrange("p (t d) -> p t d", t=TT)
                    fn(dst[:, :, (c % 2) * 512:(c % 2 + 1) * 512], psum[:, 2 * (c % 2):2 * (c % 2) + 2, :],
                       ACT.Copy).then_inc(vg_out, 1)
            for p in range(HGRN_OUT, HGRN_OUT + 3):
                hi(p)
            act.wait_ge(vg_out, 4)
            fn(hog, hog, ACT.Silu).then_inc(og_ready, 1)
            act.wait_ge(o_proj, 1)
            fn(hsq, bank(0, 4), ACT.Square).then_inc(o_squared, 1)
            take_root(6, HB)
            turn_hi_part(3, None)
            hi(HGRN_OUT + 3)
            used(HGRN_OUT + 3)
            squares(5, lambda t: bank(4 + 2 * t, 2))
            take_root(7, TT)
            act.wait_ge(residual_ready, 3)
            squares(6, lambda t: h[:, t, :])
            take_root(8, TT)
            act.wait_ge(small_loaded, 16)
            fn(router_hi[:], router[:], ACT.Copy).then_inc(router_hi_ready, 1)
            turn_hi_part(4, None)
            act.wait_ge(gate_arg, 1)
            fn(weight[:, 1, :], weight[:, 0, :], ACT.Exp).then_inc(gate_exp, 1)
            act.wait_ge(tables_ready, 1)
            jobs = act.value_load(jobs_n[0:1, 0:1], min_val=E, max_val=JOBS)

            def moe_act(n, p, turns):
                act.wait_ge(piece_used, turns * RAW_RING + (p + 1))
                act.wait_ge(moe_hid, n + 1)
                fn(act_sb, bank(0), ACT.Silu).then_inc(moe_silu, 1)

            def moe_round(n):
                act.wait_ge(moe_turned, n + 1)
                fn(ht_hi[:], bank(2), ACT.Copy).then_inc(moe_ht_hi, 1)

            with act.Fori(0, jobs) as j:
                turns = j * EXPERT_TURNS
                n = j * MOE_STEPS
                act.wait_ge(pick_turned, j + 1)
                fn(pick_t, bank(7)[:, 0:TT * P], ACT.Copy).then_inc(pick_t_ready, 1)
                for b in range(2):
                    act.wait_ge(gathered, j * 2 + b + 1)
                    fn(xt_hi[:, 4 * b:4 * b + 4, 0:P], psum[:, 3 + b, :].rearrange("p (k s) -> p k s", k=4),
                       ACT.Copy).then_inc(xg_hi, 1)
                for p in range(4):
                    hi(MOE + p, turns)
                moe_act(n, MOE + 1, turns)
                with act.Fori(0, MOE_STEPS - 1) as c:
                    t6 = turns + c
                    for p in range(4, 8):
                        hi(MOE + p, t6)
                    moe_round(n + c)
                    moe_act(n + c + 1, MOE + 5, t6)
                    for p in range(8, 10):
                        hi(MOE + p, t6)
                for p in range(2):
                    hi(MOE + 4 + p, turns + (MOE_STEPS - 1))
                moe_round(n + (MOE_STEPS - 1))
                act.wait_ge(piece_used, (turns + (MOE_STEPS - 1)) * RAW_RING + (MOE + 6))
                fn(ysb, bank(5, 2), ACT.Copy).then_inc(y_ready, 1)
            act.wait_ge(moe_done, 1)
            squares(7, lambda t: acc[:, t, :])
            take_root(9, TT)

        @block.vector
        def _(dve):
            v = nc.vector
            steps = [0]

            def step(ins):
                steps[0] += 1
                ins.then_inc(dve_step, 1)
                dve.wait_ge(dve_step, steps[0])

            def lo(p, turns=0):
                dve.wait_ge(hi_ready, turns * RAW_RING + (p + 1))
                v.tensor_tensor(w_lo[:, p % SPLIT_RING, :], raw[:, p % RAW_RING, :],
                                w_hi[:, p % SPLIT_RING, :].bitcast(F32), ALU.subtract).then_inc(lo_ready, 1)

            def inverse_root(n, width, r, va, ro, nw):
                dve.wait_ge(root_ready, n + 1)
                step(v.reciprocal(r, ro))
                step(v.tensor_tensor(nw[0], r, r, ALU.mult))
                step(v.tensor_tensor(nw[1], nw[0], va, ALU.mult))
                step(v.tensor_scalar(nw[0], nw[1], -0.5, 1.5, ALU.mult, ALU.add))
                step(v.tensor_tensor(r, r, nw[0], ALU.mult))

            def row_factor(n, count):
                dve.wait_ge(squares_ready, TT * (count + 1))
                v.tensor_scalar(var[:, 0:TT], ssq[:], 1.0 / D, EPS, ALU.mult, ALU.add).then_inc(variance_ready, 1)
                inverse_root(n, TT, rstd[:, 0:TT], var[:, 0:TT], root[:, 0:TT],
                             [newton[:, i, 0:TT] for i in range(2)])

            def pre_norm():
                for t in range(TT):
                    ins = v.tensor_scalar(tok[:, t, :], h[:, t, :], rstd[:, t:t + 1], None, ALU.mult)
                ins.then_inc(normed, 1)

            def post_norm(src, n):
                dve.wait_ge(row_loaded[1], 16 * (n + 1))
                for t in range(TT):
                    step(v.scalar_tensor_tensor(out=tok[:, t, :], in0=src(t), scalar=rstd[:, t:t + 1],
                                                in1=row[:, 1, :], op0=ALU.mult, op1=ALU.mult))
                for t in range(TT):
                    ins = v.tensor_tensor(h[:, t, :], h[:, t, :], tok[:, t, :], ALU.add)
                ins.then_inc(residual_ready, 1)
                v.memset(tick[:], 0.0).then_inc(row_used[1], 1)
                dve.wait_ge(residual_ready, n + 1)
                dve.wait_ge(row_used[1], n + 1)

            def turn_lo_part(n, gain):
                for b in range(4):
                    if gain is None:
                        dve.wait_ge(turn_hi, KT * n + 2 * b + 2)
                        v.tensor_tensor(xt_lo[:, 2 * b:2 * b + 2, :], bank(b).rearrange("p (k s) -> p k s", k=2),
                                        xt_hi[:, 2 * b:2 * b + 2, :].bitcast(F32), ALU.subtract).then_inc(turn_lo, 1)
                    else:
                        dve.wait_ge(turn_hi, KT * n + 2 * b + 2)
                        for k in (2 * b, 2 * b + 1):
                            ins = v.scalar_tensor_tensor(
                                out=xt_lo[:, k, :], in0=psum[:, b, (k % 2) * S:(k % 2 + 1) * S],
                                scalar=cols[:, gain + k:gain + k + 1], in1=xt_hi[:, k, :].bitcast(F32),
                                op0=ALU.mult, op1=ALU.subtract)
                        ins.then_inc(turn_lo, 1)

            row_factor(0, 0)
            pre_norm()
            dve.wait_ge(cols_turned, 1)
            v.tensor_copy(cols[:, 0:ROWS0], psum[:, 4, 0:ROWS0])
            v.tensor_copy(cols[:, TAPS:TAPS + W * KT], psum[:, 4, P:P + W * KT]).then_inc(cols_ready, 1)
            dve.wait_ge(cols_ready, 1)
            b0, b1 = cols[:, LB:LB + KT], cols[:, LB + KT:LB + 2 * KT]
            step(v.tensor_tensor(lb_t[:, 4, :], b0, b1, ALU.max))
            v.tensor_tensor(lb_t[:, 0, :], b0, lb_t[:, 4, :], ALU.subtract)
            v.tensor_tensor(lb_t[:, 1, :], b1, lb_t[:, 4, :], ALU.subtract).then_inc(lb_arg, 1)
            for p in range(3):
                lo(p)
            turn_lo_part(0, NG)
            dve.wait_ge(lb_exp, 1)
            step(v.tensor_tensor(lb_t[:, 4, :], lb_t[:, 2, :], lb_t[:, 3, :], ALU.add))
            step(v.reciprocal(lb_t[:, 5, :], lb_t[:, 4, :]))
            step(v.tensor_tensor(lb_c[:, 0, :], lb_t[:, 3, :], lb_t[:, 5, :], ALU.mult))
            step(v.tensor_scalar(lb_c[:, 1, :], lb_c[:, 0, :], -1.0, 1.0, ALU.mult, ALU.add))
            dve.wait_ge(consts_ready, 4)
            xor_t, xor_f, mask_f = scratch[:, 15000:15128], scratch[:, 15128:15256], scratch[:, 15256:15384]
            step(v.tensor_copy(slot_id[:], slot_i[:]))
            step(v.tensor_tensor(xor_t.bitcast(I32), slot_i[:], slot_p[:].to_broadcast([P, P]), ALU.bitwise_xor))
            step(v.tensor_copy(xor_f, xor_t.bitcast(I32)))
            step(v.tensor_tensor(xor_f, xor_f, before[:], ALU.mult))
            for i, length in enumerate(LEVELS):
                step(v.tensor_scalar(mask_f, xor_f, float(length), None, ALU.is_ge))
                step(v.scalar_tensor_tensor(out=level_mask[:, i, :], in0=xor_f, scalar=float(2 * length),
                                            in1=mask_f, op0=ALU.is_lt, op1=ALU.mult))
            lo(3)

            step(v.memset(conv_u[:, :, 0:W - 1], 0.0))
            for c in range(4):
                for b in range(2):
                    k = 2 * c + b
                    dve.wait_ge(glu_sig, k + 1)
                    ins = v.scalar_tensor_tensor(
                        out=conv_u[:, k, W - 1:], in0=psum[:, 2 * (c % 2), b * S:(b + 1) * S],
                        scalar=cols[:, B_IN + k:B_IN + k + 1], in1=conv_sig[:, 2 * (c % 2) + b, :],
                        op0=ALU.add, op1=ALU.mult)
                ins.then_inc(glu_out, 1)
                dve.wait_ge(glu_out, c + 1)
                for p in (4 + 2 * c, 5 + 2 * c):
                    if p < CONV_OUT + 2:
                        lo(p)
                for k in (2 * c, 2 * c + 1):
                    v.tensor_scalar(conv_y[:, k, :], conv_u[:, k, 0:S], cols[:, tap_col(0, k):tap_col(0, k) + 1],
                                    cols[:, DW_B + k:DW_B + k + 1], ALU.mult, ALU.add).then_inc(tap_added, 1)
                with dve.Fori(1, W) as w:
                    for b, k in enumerate((2 * c, 2 * c + 1)):
                        dve.wait_ge(tap_added, w * 2 + (2 * W * c - 1 + b))
                        v.scalar_tensor_tensor(
                            out=conv_y[:, k, :], in0=conv_u[:, k, bass.ds(w, S)],
                            scalar=cols[:, bass.ds(w * KT + (TAPS + k), 1)], in1=conv_y[:, k, :],
                            op0=ALU.mult, op1=ALU.add).then_inc(tap_added, 1)
                dve.wait_ge(tap_added, 2 * W * (c + 1))
                v.memset(tick[:], 0.0).then_inc(conv_done, 1)
            dve.wait_ge(mean_sum, 1)
            step(v.tensor_scalar(conv_mean, psum[:, 4, 0:S], 1.0 / D, None, ALU.mult))
            mean_b = conv_mean.rearrange("p (a s) -> p a s", a=1).to_broadcast([P, KT, S])
            v.tensor_tensor(conv_y[:, :, :], conv_y[:, :, :], mean_b, ALU.subtract).then_inc(centred, 1)
            dve.wait_ge(var_sum, 1)
            v.tensor_scalar(conv_var, psum[:, 5, 0:S], 1.0 / D, EPS, ALU.mult, ALU.add).then_inc(variance_ready, 1)
            dve.wait_ge(centred, 1)
            inverse_root(1, S, conv_r, conv_var, conv_t, [conv_mean, conv_sig[:, 0, :]])
            rstd_b = conv_r.rearrange("p (a s) -> p a s", a=1).to_broadcast([P, KT, S])
            v.tensor_tensor(conv_y[:, :, :], conv_y[:, :, :], rstd_b, ALU.mult).then_inc(conv_scaled, 1)
            dve.wait_ge(conv_hi, 1)
            v.tensor_tensor(xt_lo[:, :, :], conv_sq[:, :, :], xt_hi[:, :, :].bitcast(F32), ALU.subtract).then_inc(
                conv_lo, 1)
            lo(CONV_OUT + 2)
            lo(CONV_OUT + 3)
            lo(FFN0)
            dve.wait_ge(row_loaded[0], 16)
            dve.wait_ge(piece_used, CONV_OUT + 4)
            for t in range(TT):
                v.tensor_tensor(tok[:, t, :], bank(4 + 2 * t, 2), row[:, 0, :], ALU.add).then_inc(
                    (source_half, source_ready)[t], 1)
            dve.wait_ge(source_ready, 1)
            v.memset(tick[:], 0.0).then_inc(row_used[0], 1)
            row_factor(2, 1)
            post_norm(lambda t: tok[:, t, :], 0)
            row_factor(3, 2)
            pre_norm()
            turn_lo_part(1, NG + 2 * KT)
            lo(FFN0 + 1)

            def ffn_mult(c):
                dve.wait_ge(ffn_silu, c + 1)
                v.tensor_tensor(hid.rearrange("p (t n) -> p t n", t=TT), psum[:, 0:TT, FFN_CHUNK:2 * FFN_CHUNK],
                                act_sb.rearrange("p (t n) -> p t n", t=TT), ALU.mult).then_inc(ffn_hid, 1)

            def ffn_rest(c):
                dve.wait_ge(ffn_ht_hi, c + 1)
                v.tensor_tensor(ht_lo[:], bank(2), ht_hi[:].bitcast(F32), ALU.subtract).then_inc(ffn_ht_lo, 1)

            with dve.Fori(0, FFN_STEPS // 2) as i:
                for j in range(2):
                    p = FFN0 + 2 + 3 * j
                    c = i * 2 + j
                    lo(p, i)
                    ffn_mult(c)
                    lo(p + 1, i)
                    lo(p + 2, i)
                    ffn_rest(c)
            lo(HGRN_QF - 1)
            ffn_mult(FFN_STEPS - 1)
            lo(HGRN_QF)
            ffn_rest(FFN_STEPS - 1)
            lo(HGRN_QF + 1)
            row_factor(4, 3)
            post_norm(lambda t: bank(4 + 2 * t, 2), 1)
            row_factor(5, 4)
            pre_norm()
            turn_lo_part(2, NG + 4 * KT)
            lo(HGRN_QF + 2)
            lo(HGRN_QF + 3)

            for c in range(4):
                part = slice(c * 512, (c + 1) * 512)
                dve.wait_ge(qf_sig, 2 * c + 1)
                v.tensor_tensor(hq[:, part], bank(2 * (c % 2)), hq[:, part], ALU.mult)
                dve.wait_ge(qf_sig, 2 * c + 2)
                for k in (2 * c, 2 * c + 1):
                    one = slice(k * S, (k + 1) * S)
                    step(v.tensor_scalar(lev[0][:, one], hk[:, one], lb_c[:, 1, k:k + 1], lb_c[:, 0, k:k + 1],
                                         ALU.mult, ALU.add))
                v.tensor_scalar(hk[:, part], lev[0][:, part], -1.0, 1.0, ALU.mult, ALU.add).then_inc(q_ready, 1)
                for p in (HGRN_QF + 4 + 2 * c, HGRN_QF + 5 + 2 * c)[:2 * (c < 3)]:
                    lo(p)
            dve.wait_ge(q_ready, 4)
            v.memset(tick[:], 0.0).then_inc(forget_ready, 1)
            lo(HGRN_VG + 2)
            dve.wait_ge(log_ready, 1)
            for b in range(HB):
                one = slice(b * P, (b + 1) * P)
                ins = v.tensor_tensor_scan(hg[:, one], ones[:], lev[0][:, one], 0.0, ALU.mult, ALU.add)
            step(ins)

            def halves(buf, n):
                length = P if n == len(LEVELS) + 1 else LEVELS[n - 1]
                w = buf.rearrange("p (x two l) -> p x two l", two=2, l=length)
                return w[:, :, 0, :], w[:, :, 1, :], length

            def level_diff(n):
                if n > 2:
                    dve.wait_ge(level_scores, n - 1)
                left, right, length = halves(lev[n % 2], n)
                g_left, g_right, _ = halves(hg, n)
                end = g_left[:, :, length - 1:length].to_broadcast([P, HEADS * S // (2 * length), length])
                v.tensor_tensor(left, end, g_left, ALU.subtract)
                if n == len(LEVELS) + 1:
                    v.tensor_copy(right, g_right).then_inc(level_arg, 1)
                else:
                    v.tensor_tensor(right, g_right, end, ALU.subtract).then_inc(level_arg, 1)

            def level_mult(n):
                dve.wait_ge(level_exp, n)
                left, right, _ = halves(lev[n % 2], n)
                v.tensor_tensor(left, left, halves(hk, n)[0], ALU.mult)
                v.tensor_tensor(right, right, halves(hq, n)[1], ALU.mult).then_inc(level_factors, 1)

            def level_take(n):
                dve.wait_ge(level_scores, n + 1)
                dst = s_same.rearrange("p (b t) -> p b t", b=HB)
                src = bank(4, 4).rearrange("p (b t) -> p b t", b=HB)
                if n:
                    dve.wait_ge(level_taken, n)
                if n == 0:
                    v.tensor_tensor(dst, src, ident[:].rearrange("p (a t) -> p a t", a=1).to_broadcast([P, HB, P]),
                                    ALU.mult).then_inc(level_taken, 1)
                elif n == len(LEVELS) + 1:
                    v.tensor_copy(s_cross, bank(4, 2)).then_inc(level_taken, 1)
                else:
                    v.copy_predicated(dst, level_mask[:, n - 1:n, :].to_broadcast([P, HB, P]), src).then_inc(
                        level_taken, 1)

            level_diff(1)
            level_mult(1)
            for n in range(1, 8):
                level_take(n - 1)
                level_diff(n + 1)
                if HGRN_VG + 2 + n < HGRN_OUT:
                    lo(HGRN_VG + 2 + n)
                level_mult(n + 1)
            level_take(7)
            level_take(8)
            for p in range(HGRN_OUT, HGRN_OUT + 3):
                lo(p)
            dve.wait_ge(og_ready, 1)
            dve.wait_ge(row_loaded[0], 32)
            gain = row[:, 0:1, 0:P].to_broadcast([P, HB, P])
            by_head = "p (b c) -> p b c"
            step(v.tensor_tensor(hog.rearrange(by_head, b=HB), hog.rearrange(by_head, b=HB), gain, ALU.mult))
            v.memset(tick[:], 0.0).then_inc(row_used[0], 1)
            dve.wait_ge(row_used[0], 2)
            dve.wait_ge(o_squared, 1)
            step(v.tensor_reduce(var[:], hsq.rearrange(by_head, b=HB), AX.X, ALU.add))
            v.tensor_scalar(var[:], var[:], 1.0 / P, EPS, ALU.mult, ALU.add).then_inc(variance_ready, 1)
            inverse_root(6, HB, rstd[:], var[:], root[:], [newton[:, i, :] for i in range(2)])
            scale = rstd[:].rearrange("p (b a) -> p b a", a=1).to_broadcast([P, HB, P])
            step(v.tensor_tensor(hq.rearrange(by_head, b=HB), bank(0, 4).rearrange(by_head, b=HB), scale, ALU.mult))
            v.tensor_tensor(hq, hq, hog, ALU.mult).then_inc(normed, 1)
            turn_lo_part(3, None)
            lo(HGRN_OUT + 3)
            row_factor(7, 5)
            post_norm(lambda t: bank(4 + 2 * t, 2), 2)
            row_factor(8, 6)
            dve.wait_ge(row_loaded[0], 48)
            for t in range(TT):
                ins = v.scalar_tensor_tensor(out=mx[:, t, :], in0=h[:, t, :], scalar=rstd[:, t:t + 1],
                                             in1=row[:, 0, :], op0=ALU.mult, op1=ALU.mult)
            ins.then_inc(normed, 1)
            dve.wait_ge(router_hi_ready, 1)
            v.tensor_tensor(router_lo[:], router[:], router_hi[:].bitcast(F32), ALU.subtract).then_inc(router_split, 1)
            v.memset(acc[:, :, :], 0.0).then_inc(acc_added, 1)
            v.memset(tick[:], 0.0).then_inc(moe_hid, 1)
            turn_lo_part(4, None)
            dve.wait_ge(logits_done, 1)
            step(v.tensor_copy(logits[:], psum[:, 7, 0:TT * E].rearrange("p (t e) -> p t e", t=TT)))
            for t in range(TT):
                step(v.max(top[:, t, :], logits[:, t, :]))
                step(v.max_index(top_i[:, t, :], top[:, t, :], logits[:, t, :]))
            step(v.tensor_copy(top_f[:], top_i[:]))
            v.tensor_tensor(weight[:, 0, :], top[:, :, 1], top[:, :, 0], ALU.subtract).then_inc(gate_arg, 1)
            for t in range(TT):
                for rank in range(2):
                    step(v.tensor_scalar(chosen[:, rank, t, :], slot_id[:, 0:E], top_f[:, t, rank:rank + 1], None,
                                         ALU.is_equal))
            v.tensor_tensor(sel[:], chosen[:, 0, :, :], chosen[:, 1, :, :], ALU.add).then_inc(sel_ready, 1)
            dve.wait_ge(gate_exp, 1)
            step(v.tensor_scalar(weight[:, 2, :], weight[:, 1, :], 1.0, None, ALU.add))
            step(v.reciprocal(weight[:, 3, :], weight[:, 2, :]))
            step(v.tensor_tensor(weight[:, 2, :], weight[:, 1, :], weight[:, 3, :], ALU.mult))
            for t in range(TT):
                step(v.tensor_scalar(place[:, t, :], chosen[:, 0, t, :], weight[:, 3, t:t + 1], None, ALU.mult))
                step(v.scalar_tensor_tensor(out=gate_of[:, t, 0:E], in0=chosen[:, 1, t, :],
                                            scalar=weight[:, 2, t:t + 1], in1=place[:, t, :],
                                            op0=ALU.mult, op1=ALU.add))
            v.tensor_copy(gate_of[:, :, E:JOBS], gate_of[:, :, 0:E])
            dve.wait_ge(count_done, 1)
            step(v.scalar_tensor_tensor(out=place[:], in0=psum[:, 6, 0:TT * E].rearrange("p (t e) -> p t e", t=TT),
                                        scalar=1.0, in1=sel[:], op0=ALU.add, op1=ALU.mult))
            v.tensor_scalar(slot_of[:, :, 0:E], place[:], -1.0, None, ALU.add)
            v.tensor_scalar(slot_of[:, :, E:JOBS], place[:], -1.0 - P, None, ALU.add)
            step(v.tensor_reduce(busiest[:, 0:1], psum[:, 6, 2 * E:3 * E], AX.X, ALU.max))
            step(v.tensor_scalar(busiest[:, 1:2], busiest[:, 0:1], float(P), float(E), ALU.is_gt, ALU.mult))
            v.tensor_scalar(jobs_n[:], busiest[:, 1:2], float(E), None, ALU.add).then_inc(tables_ready, 1)
            dve.wait_ge(tables_ready, 1)
            jobs = dve.value_load(jobs_n[0:1, 0:1], min_val=E, max_val=JOBS)

            def moe_mult(n, p, turns):
                dve.wait_ge(moe_silu, n + 1)
                dve.wait_ge(piece_used, turns * RAW_RING + (p + 1))
                v.tensor_tensor(hid, bank(1), act_sb, ALU.mult).then_inc(moe_hid, 1)

            def moe_rest(n):
                dve.wait_ge(moe_ht_hi, n + 1)
                v.tensor_tensor(ht_lo[:], bank(2), ht_hi[:].bitcast(F32), ALU.subtract).then_inc(moe_ht_lo, 1)

            with dve.Fori(0, jobs) as j:
                turns = j * EXPERT_TURNS
                n = j * MOE_STEPS
                for t in range(TT):
                    ins = v.tensor_scalar(pick[:, t, :], slot_id[:], slot_of[:, t, bass.ds(j, 1)], None, ALU.is_equal)
                ins.then_inc(pick_ready, 1)
                for b in range(2):
                    dve.wait_ge(xg_hi, j * 2 + b + 1)
                    v.tensor_tensor(xt_lo[:, 4 * b:4 * b + 4, 0:P],
                                    psum[:, 3 + b, :].rearrange("p (k s) -> p k s", k=4),
                                    xt_hi[:, 4 * b:4 * b + 4, 0:P].bitcast(F32), ALU.subtract).then_inc(xg_lo, 1)
                for p in range(4):
                    lo(MOE + p, turns)
                moe_mult(n, MOE + 3, turns)
                with dve.Fori(0, MOE_STEPS - 1) as c:
                    t6 = turns + c
                    for p in range(4, 8):
                        lo(MOE + p, t6)
                    moe_rest(n + c)
                    for p in range(8, 10):
                        lo(MOE + p, t6)
                    moe_mult(n + c + 1, MOE + 7, t6)
                for p in range(2):
                    lo(MOE + 4 + p, turns + (MOE_STEPS - 1))
                moe_rest(n + (MOE_STEPS - 1))
                for t in range(TT):
                    for half in range(2):
                        i = 2 * t + half
                        dve.wait_ge(scattered, j * 4 + i + 1)
                        dve.wait_ge(acc_added, j * 4 + 1)
                        part = acc[:, t, half * BANK:(half + 1) * BANK]
                        v.scalar_tensor_tensor(out=part, in0=bank(SCATTER_BANKS[i]),
                                               scalar=gate_of[:, t, bass.ds(j, 1)], in1=part,
                                               op0=ALU.mult, op1=ALU.add).then_inc(acc_added, 1)
            v.memset(tick[:], 0.0).then_inc(moe_done, 1)
            dve.wait_ge(moe_done, 1)
            row_factor(9, 7)
            post_norm(lambda t: acc[:, t, :], 3)


_INS = ["x", "norm_g", "conv_w_in", "conv_b_in", "conv_dw_w", "conv_dw_b", "conv_ln_g", "conv_ln_b", "conv_w_out",
        "conv_b_out", "hgrn_w_in", "hgrn_lower_bounds", "hgrn_norm_g", "hgrn_w_out", "ffn_w_gu", "ffn_w_down",
        "moe_router", "moe_w_gu", "moe_w_down"]


def kernel(**inputs):
    import numpy as np
    from concourse import bacc
    from concourse.bass_utils import run_bass_kernel_spmd

    nc = bacc.Bacc("TRN2", target_bir_lowering=False, num_devices=1)
    arrays, args = {}, []
    for name in _INS:
        a = np.ascontiguousarray(inputs[name])
        arrays[f"in_{name}"] = a
        args.append(nc.dram_tensor(f"in_{name}", a.shape, mybir.dt.from_np(a.dtype), kind="ExternalInput").ap())
    out = nc.dram_tensor("out", inputs["x"].shape, F32, kind="ExternalOutput").ap()
    trunk(nc, *args, out)
    r = run_bass_kernel_spmd(nc, [arrays], core_ids=[0])
    return r.results[0]["out"]
```

```python
from contextlib import ExitStack

import concourse.bass as bass
from concourse import mybir

F32 = mybir.dt.float32
F32R = mybir.dt.float32r
I32 = mybir.dt.int32
U32 = mybir.dt.uint32
ACT = mybir.ActivationFunctionType
ALU = mybir.AluOpType
AX = mybir.AxisListType

P = 128
EPS = 1e-6
BANK = 512
PIECE = 2048
SCATTER_BANKS = (3, 4, 7, 2)
RAW_RING = 6
SPLIT_RING = 3


def trunk(nc, x, norm_g, conv_w_in, conv_b_in, conv_dw_w, conv_dw_b, conv_ln_g, conv_ln_b,
          conv_w_out, conv_b_out, hgrn_w_in, hgrn_lower_bounds, hgrn_norm_g, hgrn_w_out,
          ffn_w_gu, ffn_w_down, moe_router, moe_w_gu, moe_w_down, out):
    _, S, D = x.shape
    TT = S // P
    KT = D // P
    W = conv_dw_w.shape[1]
    FFN = ffn_w_down.shape[1]
    E = moe_router.shape[2]
    ED = moe_w_down.shape[2]
    HEADS = D // P
    HB = HEADS * TT
    FFN_CHUNK = 256
    FFN_STEPS = FFN // FFN_CHUNK
    MOE_CHUNK = 512
    MOE_STEPS = ED // MOE_CHUNK
    JOBS = 2 * E
    LEVELS = [64, 32, 16, 8, 4, 2, 1]
    assert TT == 2 and KT == 8 and FFN % FFN_CHUNK == 0 and ED % MOE_CHUNK == 0 and FFN_STEPS % 2 == 1

    CONV_IN = 0
    CONV_OUT = CONV_IN + 2 * D * KT * P // (P * PIECE)
    FFN0 = CONV_OUT + D * D // (P * PIECE)
    HGRN_QF = FFN0 + 3 * FFN_STEPS
    HGRN_VG = HGRN_QF + 2 * D * D // (P * PIECE)
    HGRN_OUT = HGRN_VG + 2 * D * D // (P * PIECE)
    MOE = HGRN_OUT + D * D // (P * PIECE)
    EXPERT_PIECES = 6 * MOE_STEPS
    EXPERT_TURNS = EXPERT_PIECES // RAW_RING

    with ExitStack() as ctx:
        def sb(name, shape, dt=F32):
            return ctx.enter_context(nc.sbuf_tensor(name, shape, dt))

        def sem(name):
            return ctx.enter_context(nc.semaphore(name))

        raw = sb("raw", [P, RAW_RING, PIECE])
        w_hi = sb("w_hi", [P, SPLIT_RING, PIECE], F32R)
        w_lo = sb("w_lo", [P, SPLIT_RING, PIECE], F32R)
        xt_hi = sb("xt_hi", [P, KT, S], F32R)
        xt_lo = sb("xt_lo", [P, KT, S], F32R)
        ht_hi = sb("ht_hi", [P, 512], F32R)
        ht_lo = sb("ht_lo", [P, 512], F32R)
        h = sb("h", [P, TT, D])
        row = sb("row", [P, 2, D])
        scratch = sb("scratch", [P, 17408])
        cols = sb("cols", [P, 376])
        ident = sb("ident", [P, P])
        ones = sb("ones", [P, P])
        before = sb("before", [P, P])
        slot_i = sb("slot_i", [P, P], I32)
        slot_p = sb("slot_p", [P, 1], I32)
        slot_id = sb("slot_id", [P, P])
        ssq = sb("ssq", [P, TT])
        var = sb("var", [P, HB])
        root = sb("root", [P, HB])
        rstd = sb("rstd", [P, HB])
        newton = sb("newton", [P, 2, HB])
        lb_t = sb("lb_t", [P, 6, KT])
        lb_c = sb("lb_c", [P, 2, KT])
        logits = sb("logits", [P, TT, E])
        top = sb("top", [P, TT, 8])
        top_i = sb("top_i", [P, TT, 8], U32)
        top_f = sb("top_f", [P, TT, 8])
        chosen = sb("chosen", [P, 2, TT, E])
        sel = sb("sel", [P, TT, E])
        weight = sb("weight", [P, 4, TT])
        place = sb("place", [P, TT, E])
        busiest = sb("busiest", [P, 2])
        router = sb("router", [P, KT, E])
        router_hi = sb("router_hi", [P, KT, E], F32R)
        router_lo = sb("router_lo", [P, KT, E], F32R)
        slot_of = sb("slot_of", [P, TT, JOBS + 1])
        gate_of = sb("gate_of", [P, TT, JOBS + 1])
        warm = sb("warm", [P, 16])
        eps = sb("eps", [P, 1])
        tick = sb("tick", [P, 1])
        jobs_n = sb("jobs_n", [P, 1], I32)

        class Cut:
            at = 0

            @classmethod
            def take(cls, n):
                cls.at += n
                assert cls.at <= 17408, cls.at
                return scratch[:, cls.at - n:cls.at]

        Cut.at = 0
        tok = Cut.take(TT * D).rearrange("p (t d) -> p t d", t=TT)
        junk = Cut.take(TT * D)
        Cut.at = 3 * TT * D
        biased = Cut.take(TT * D).rearrange("p (t d) -> p t d", t=TT)
        Cut.at = 0
        conv_u = Cut.take(KT * (S + W - 1)).rearrange("p (k s) -> p k s", k=KT)
        conv_y = Cut.take(KT * S).rearrange("p (k s) -> p k s", k=KT)
        conv_sq = Cut.take(KT * S).rearrange("p (k s) -> p k s", k=KT)
        conv_sig = Cut.take(4 * S).rearrange("p (k s) -> p k s", k=4)
        conv_mean = Cut.take(S)
        conv_var = Cut.take(S)
        conv_r = Cut.take(S)
        conv_t = Cut.take(S)
        diag = Cut.take(W * P).rearrange("p (w c) -> p w c", w=W)
        Cut.at = 2 * TT * D
        act_sb = Cut.take(512)
        hid = Cut.take(512)
        Cut.at = 0
        hq = Cut.take(HEADS * S)
        hk = Cut.take(HEADS * S)
        hg = Cut.take(HEADS * S)
        lev = [Cut.take(HEADS * S) for _ in range(2)]
        hv = Cut.take(TT * D)
        hog = Cut.take(TT * D)
        s_same = Cut.take(HB * P)
        s_cross = Cut.take(HEADS * P)
        ho = hq.rearrange("p (t d) -> p t d", t=TT)
        hsq = hk
        Cut.at = 0
        mx = Cut.take(TT * D).rearrange("p (t d) -> p t d", t=TT)
        Cut.take(TT * D)
        Cut.take(1024)
        acc = Cut.take(TT * D).rearrange("p (t d) -> p t d", t=TT)
        ysb = Cut.take(D)
        pick = Cut.take(TT * P).rearrange("p (t s) -> p t s", t=TT)
        pick_t = Cut.take(TT * P)
        level_mask = sb("level_mask", [P, len(LEVELS), P], mybir.dt.uint8)
        prow = s_same[:, 0:3 * P].rearrange("p (a b) -> p a b", a=3)

        psum = ctx.enter_context(nc.psum_tensor("psum", [P, 8, BANK], F32))

        LBD = hgrn_lower_bounds.shape[0]
        NG = 0
        B_IN = NG + 8 * KT
        DW_B = B_IN + 2 * KT
        LN_G = DW_B + KT
        LN_B = LN_G + KT
        LB = LN_B + KT
        ROWS0 = LB + LBD * KT
        TAPS = P
        HALF_W = (W + 1) // 2
        PE_CONV = (3, 5, 7)
        DVE_CONV = (0, 1, 2, 4, 6)

        def tap_col(w, k):
            a, b = divmod(w, HALF_W)
            return TAPS + a * (HALF_W * KT) + b * KT + k

        def group_bank(n):
            return 4 + 2 * (n % 2)

        raw_loaded = [sem(f"raw_loaded{i}") for i in range(RAW_RING)]
        hi_ready = sem("hi_ready")
        lo_ready = sem("lo_ready")
        piece_used = sem("piece_used")
        x_loaded = sem("x_loaded")
        rows_loaded = sem("rows_loaded")
        small_loaded = sem("small_loaded")
        row_loaded = [sem(f"row_loaded{i}") for i in range(2)]
        row_used = [sem(f"row_used{i}") for i in range(2)]
        consts_ready = sem("consts_ready")
        cols_turned = sem("cols_turned")
        cols_ready = sem("cols_ready")
        lb_arg = sem("lb_arg")
        lb_exp = sem("lb_exp")
        dve_step = sem("dve_step")
        act_step = sem("act_step")
        squares_ready = sem("squares_ready")
        gained = sem("gained")
        tile_done = sem("tile_done")
        variance_ready = sem("variance_ready")
        conv_root = sem("conv_root")
        head_root = sem("head_root")
        root_ready = sem("root_ready")
        normed = sem("normed")
        turned = sem("turned")
        turn_hi = sem("turn_hi")
        turn_lo = sem("turn_lo")
        source_ready = sem("source_ready")
        residual_ready = sem("residual_ready")
        glu_sig = sem("glu_sig")
        glu_out = sem("glu_out")
        conv_done = sem("conv_done")
        mean_sum = sem("mean_sum")
        centred = sem("centred")
        conv_squared = sem("conv_squared")
        var_sum = sem("var_sum")
        conv_scaled = sem("conv_scaled")
        conv_act = sem("conv_act")
        conv_hi = sem("conv_hi")
        conv_lo = sem("conv_lo")
        tap_added = sem("tap_added")
        diag_ready = sem("diag_ready")
        diag_used = sem("diag_used")
        tensor_conv_done = sem("tensor_conv_done")
        ffn_silu = sem("ffn_silu")
        ffn_hid = sem("ffn_hid")
        ffn_turned = sem("ffn_turned")
        ffn_ht_hi = sem("ffn_ht_hi")
        ffn_ht_lo = sem("ffn_ht_lo")
        qf_sig = sem("qf_sig")
        q_ready = sem("q_ready")
        forget_ready = sem("forget_ready")
        k_ready = sem("k_ready")
        log_ready = sem("log_ready")
        level_arg = sem("level_arg")
        level_exp = sem("level_exp")
        level_factors = sem("level_factors")
        level_scores = sem("level_scores")
        level_taken = sem("level_taken")
        vg_out = sem("vg_out")
        o_proj = sem("o_proj")
        o_squared = sem("o_squared")
        og_ready = sem("og_ready")
        gate_folded = sem("gate_folded")
        router_split = sem("router_split")
        router_hi_ready = sem("router_hi_ready")
        logits_done = sem("logits_done")
        sel_ready = sem("sel_ready")
        count_done = sem("count_done")
        gate_arg = sem("gate_arg")
        gate_exp = sem("gate_exp")
        tables_ready = sem("tables_ready")
        pick_ready = sem("pick_ready")
        gathered = sem("gathered")
        pick_turned = sem("pick_turned")
        pick_t_ready = sem("pick_t_ready")
        xg_hi = sem("xg_hi")
        xg_lo = sem("xg_lo")
        moe_silu = sem("moe_silu")
        moe_hid = sem("moe_hid")
        moe_turned = sem("moe_turned")
        moe_ht_hi = sem("moe_ht_hi")
        moe_ht_lo = sem("moe_ht_lo")
        y_ready = sem("y_ready")
        scattered = sem("scattered")
        acc_added = sem("acc_added")
        moe_done = sem("moe_done")
        out_stored = sem("out_stored")

        block = ctx.enter_context(nc.Block())

        def bank(i, n=1):
            return psum[:, i:i + n, :].rearrange("p b c -> p (b c)")

        @block.sync
        def _(sp):
            def load(p, parts, turns=0):
                if p >= RAW_RING:
                    sp.wait_ge(lo_ready, turns * RAW_RING + (p - RAW_RING + 1))
                for dst, src in parts:
                    sp.dma_start(dst, src).then_inc(raw_loaded[p % RAW_RING], 32 // len(parts))

            def by_channel(p, w, k0, c0, c1=None):
                r = w.rearrange("(k p) n -> p k n", p=P)[:, k0:k0 + 4, :]
                d = raw[:, p % RAW_RING, :].rearrange("p (k n) -> p k n", k=4)
                if c1 is None:
                    return [(d, r[:, :, bass.ds(c0, 512)])]
                return [(d[:, :, 0:256], r[:, :, bass.ds(c0, 256)]), (d[:, :, 256:512], r[:, :, bass.ds(c1, 256)])]

            def by_row(p, w, r0):
                d = raw[:, p % RAW_RING, :].rearrange("p (k n) -> p k n", k=2)
                return [(d, w[bass.ds(r0, 2 * P), :].rearrange("(k p) n -> p k n", p=P))]

            sp.dma_start(h[:], x[0].rearrange("(t p) d -> p t d", p=P)).then_inc(x_loaded, 16)
            first_group = [
                (0, B_IN, norm_g.rearrange("l n (k c) -> (l n k) c", c=P)),
                (B_IN, DW_B, conv_b_in.rearrange("l (k c) -> (l k) c", c=P)),
                (DW_B, LN_G, conv_dw_b.rearrange("l (k c) -> (l k) c", c=P)),
                (LN_G, LN_B, conv_ln_g.rearrange("l (k c) -> (l k) c", c=P)),
                (LN_B, LB, conv_ln_b.rearrange("l (k c) -> (l k) c", c=P)),
                (LB, ROWS0, hgrn_lower_bounds.rearrange("l (k c) -> (l k) c", c=P)),
            ]
            for a, b, src in first_group:
                sp.dma_start(prow[a:b, 0, :], src).then_inc(rows_loaded, 16)
            taps = conv_dw_w[0].rearrange("w (k c) -> (w k) c", c=P)
            sp.dma_start(prow[0:HALF_W * KT, 1, :], taps[0:HALF_W * KT, :]).then_inc(rows_loaded, 16)
            sp.dma_start(prow[0:(W - HALF_W) * KT, 2, :], taps[HALF_W * KT:W * KT, :]).then_inc(rows_loaded, 16)

            w = conv_w_in[0]
            order = [(c, kh) for c in range(4) for kh in range(2)]
            pieces = [by_channel(CONV_IN + n, w, 4 * kh, 256 * c, D + 256 * c) for n, (c, kh) in enumerate(order)]
            for p in range(CONV_OUT):
                load(p, pieces[p])
            for n in range(4):
                load(CONV_OUT + n, by_row(CONV_OUT + n, conv_w_out[0], 256 * n))
            gu, dn = ffn_w_gu[0], ffn_w_down[0]
            for kh in range(2):
                load(FFN0 + kh, by_channel(FFN0 + kh, gu, 4 * kh, 0, FFN))
            with sp.Fori(0, FFN_STEPS // 2) as i:
                for j in range(2):
                    p = FFN0 + 2 + 3 * j
                    col = (i * 2 + (1 + j)) * FFN_CHUNK
                    for kh in range(2):
                        load(p + kh, by_channel(p + kh, gu, 4 * kh, col, col + FFN), i)
                    load(p + 2, by_row(p + 2, dn, (i * 2 + j) * FFN_CHUNK), i)
            p = HGRN_QF - 1
            load(p, by_row(p, dn, (FFN_STEPS - 1) * FFN_CHUNK))
            w = hgrn_w_in[0]
            for n, (c, kh) in enumerate(order):
                load(HGRN_QF + n, by_channel(HGRN_QF + n, w, 4 * kh, 256 * c, D + 256 * c))
            for n, (c, kh) in enumerate(order):
                load(HGRN_VG + n, by_channel(HGRN_VG + n, w, 4 * kh, 2 * D + 512 * c))
            for n in range(4):
                load(HGRN_OUT + n, by_row(HGRN_OUT + n, hgrn_w_out[0], 256 * n))

            def expert(e, turns):
                gu, dn = moe_w_gu[0][e, :, :], moe_w_down[0][e, :, :]
                for g in range(2):
                    for kh in range(2):
                        p = MOE + 2 * g + kh
                        load(p, by_channel(p, gu, 4 * kh, g * ED), turns)
                with sp.Fori(1, MOE_STEPS) as c:
                    t = turns + (c - 1)
                    for g in range(2):
                        for kh in range(2):
                            p = MOE + 4 + 2 * g + kh
                            load(p, by_channel(p, gu, 4 * kh, c * MOE_CHUNK + g * ED), t)
                    for n in range(2):
                        p = MOE + 8 + n
                        load(p, by_row(p, dn, (c - 1) * MOE_CHUNK + 256 * n), t)
                for n in range(2):
                    p = MOE + 4 + n
                    load(p, by_row(p, dn, (MOE_STEPS - 1) * MOE_CHUNK + 256 * n), turns + (MOE_STEPS - 1))

            with sp.Fori(0, E) as e:
                expert(e, e * EXPERT_TURNS)
            sp.wait_ge(tables_ready, 1)
            jobs = sp.value_load(jobs_n[0:1, 0:1], min_val=E, max_val=JOBS)
            with sp.If(jobs > E):
                with sp.Fori(0, E) as e:
                    expert(e, (e + E) * EXPERT_TURNS)
            sp.wait_ge(residual_ready, 4 * TT)
            sp.dma_start(out[0].rearrange("(t p) d -> p t d", p=P), h[:]).then_inc(out_stored, 16)
            sp.wait_ge(out_stored, 16)

        @block.gpsimd
        def _(pool):
            nc.gpsimd.memset(eps[:], EPS)
            nc.gpsimd.memset(ones[:], 1.0).then_inc(consts_ready, 1)
            nc.gpsimd.iota(slot_i[:], pattern=[[1, P]], base=0, channel_multiplier=0)
            nc.gpsimd.iota(slot_p[:], pattern=[[0, 1]], base=0, channel_multiplier=1).then_inc(consts_ready, 1)
            pool.wait_ge(consts_ready, 2)
            nc.gpsimd.affine_select(out=ident[:], in_=ones[:], compare_op=ALU.is_equal, fill=0.0, base=0,
                                    pattern=[[-1, P]], channel_multiplier=1).then_inc(consts_ready, 1)
            nc.gpsimd.affine_select(out=before[:], in_=ones[:], compare_op=ALU.is_gt, fill=0.0, base=0,
                                    pattern=[[1, P]], channel_multiplier=-1).then_inc(consts_ready, 1)

            def load_row(i, src, n):
                if n:
                    pool.wait_ge(row_used[i], n)
                pool.dma_start(row[:, i, 0:src.shape[-1]], src.partition_broadcast(P)).then_inc(row_loaded[i], 16)

            load_row(0, conv_b_out[0], 0)
            load_row(1, norm_g[0, 1], 0)
            pool.dma_start(router[:], moe_router[0].rearrange("(k p) e -> p k e", p=P)).then_inc(small_loaded, 16)
            load_row(0, hgrn_norm_g[0], 1)
            load_row(1, norm_g[0, 3], 1)
            load_row(1, norm_g[1, 1], 2)
            load_row(0, norm_g[1, 2], 2)
            load_row(1, norm_g[1, 3], 3)

        @block.tensor
        def _(pe):
            mm = nc.tensor.matmul

            def wait_hi(p, turns=0):
                pe.wait_ge(hi_ready, turns * RAW_RING + (p + 1))

            def wait_lo(p, turns=0):
                pe.wait_ge(lo_ready, turns * RAW_RING + (p + 1))

            def turn(n, src):
                for t in range(TT):
                    pe.wait_ge(normed, TT * n + t + 1)
                    for k in range(KT):
                        last = nc.tensor.transpose(psum[:, k // 2, (k % 2) * S + t * P:(k % 2) * S + (t + 1) * P],
                                                   src[:, t, k * P:(k + 1) * P], ident[:])
                        if k % 2 and t:
                            last.then_inc(turned, 1)

            def half_turned(n, kh):
                pe.wait_ge(turn_lo, 4 * n + 2 * kh + 2)

            def channel_out(p, kh, banks):
                for part, rhss in ((w_hi, (xt_hi, xt_lo)), (w_lo, (xt_hi,))):
                    (wait_hi if part is w_hi else wait_lo)(p)
                    wv = part[:, p % SPLIT_RING, :].rearrange("p (k n) -> p k n", k=4)
                    for kk in range(4):
                        for b in range(4):
                            for rhs in rhss:
                                first = kh == 0 and kk == 0 and b % 2 == 0 and part is w_hi and rhs is xt_hi
                                last = mm(psum[:, banks + b // 2, (b % 2) * S:(b % 2 + 1) * S],
                                          wv[:, kk, b * P:(b + 1) * P], rhs[:, 4 * kh + kk, :],
                                          start=first, stop=kh == 1 and kk == 3 and part is w_lo,
                                          skip_group_check=True)
                last.then_inc(piece_used, 1)

            def token_cols(p, kh, banks, tiles, turns=0):
                for part, lhss in ((w_hi, (xt_hi, xt_lo)), (w_lo, (xt_hi,))):
                    (wait_hi if part is w_hi else wait_lo)(p, turns)
                    wv = part[:, p % SPLIT_RING, :].rearrange("p (k n) -> p k n", k=4)
                    for kk in range(4):
                        for t in range(tiles):
                            for lhs in lhss:
                                last = mm(psum[:, banks[t], :], lhs[:, 4 * kh + kk, t * P:(t + 1) * P], wv[:, kk, :],
                                          start=kh == 0 and kk == 0 and part is w_hi and lhs is xt_hi,
                                          stop=kh == 1 and kk == 3 and part is w_lo)
                last.then_inc(piece_used, 1)

            def token_rows(p, operands, banks, tiles, first, final, turns=0):
                split = final and tiles == 2
                for group in ((0,), (1,)) if split else (range(tiles),):
                    for part in (w_hi, w_lo):
                        (wait_hi if part is w_hi else wait_lo)(p, turns)
                        wv = part[:, p % SPLIT_RING, :].rearrange("p (k n) -> p k n", k=2)
                        for kk in range(2):
                            for t in group:
                                for i, lhs in enumerate(operands(kk, t)[:2 if part is w_hi else 1]):
                                    for half in range(2):
                                        last = mm(psum[:, banks + 2 * t + half, :], lhs,
                                                  wv[:, kk, half * BANK:(half + 1) * BANK],
                                                  start=first and kk == 0 and part is w_hi and i == 0,
                                                  stop=final and kk == 1 and part is w_lo)
                    if split and 0 in group:
                        last.then_inc(tile_done, 1)
                last.then_inc(piece_used, 1)

            def from_xt(k0):
                return lambda k, t: (xt_hi[:, k0 + k, t * P:(t + 1) * P], xt_lo[:, k0 + k, t * P:(t + 1) * P])

            pe.wait_ge(consts_ready, 4)
            pe.wait_ge(rows_loaded, 8 * 16)
            n = (W - HALF_W) * KT
            nc.tensor.transpose(psum[:, 4, 0:ROWS0], prow[0:ROWS0, 0, :], ident[0:ROWS0, 0:ROWS0])
            nc.tensor.transpose(psum[:, 4, P:P + HALF_W * KT], prow[0:HALF_W * KT, 1, :],
                                ident[0:HALF_W * KT, 0:HALF_W * KT])
            nc.tensor.transpose(psum[:, 4, P + HALF_W * KT:P + HALF_W * KT + n], prow[0:n, 2, :],
                                ident[0:n, 0:n]).then_inc(cols_turned, 1)

            def conv_taps(i):
                k = PE_CONV[i]
                pe.wait_ge(glu_out, k // 2 + 1)
                for w in range(W):
                    pe.wait_ge(diag_ready, W * i + w + 1)
                    mm(psum[:, 6 + i % 2, 0:S], diag[:, w, :], conv_u[:, k, w:w + S],
                       start=w == 0, stop=w == W - 1).then_inc(diag_used, 1)

            def channel_sum(k):
                if k in PE_CONV:
                    pe.wait_ge(tensor_conv_done, PE_CONV.index(k) + 1)
                else:
                    pe.wait_ge(conv_done, DVE_CONV.index(k) + 1)
                return mm(psum[:, 4, 0:S], ones[:], conv_y[:, k, :], start=k == 0, stop=k == KT - 1)

            turn(0, tok)
            for c in range(4):
                if c >= 2:
                    pe.wait_ge(glu_out, c - 1)
                for kh in range(2):
                    if c == 0:
                        half_turned(0, 1)
                    channel_out(CONV_IN + 2 * c + kh, kh, 2 * (c % 2))
                if c == 2:
                    conv_taps(0)
            conv_taps(1)
            for k in range(4):
                channel_sum(k)
            conv_taps(2)
            for k in range(4, KT):
                last = channel_sum(k)
            last.then_inc(mean_sum, 1)
            for k in range(KT):
                pe.wait_ge(conv_squared, k + 1)
                last = mm(psum[:, 5, 0:S], ones[:], conv_sq[:, k, :], start=k == 0, stop=k == KT - 1)
            last.then_inc(var_sum, 1)
            for n in range(4):
                pe.wait_ge(conv_lo, n + 1)
                token_rows(CONV_OUT + n, from_xt(2 * n), 4, TT, n == 0, n == 3)

            turn(1, tok)

            def ffn_turn(c):
                pe.wait_ge(ffn_hid, c + 1)
                for k in range(2):
                    for t in range(TT):
                        last = nc.tensor.transpose(psum[:, 2, k * S + t * P:k * S + (t + 1) * P],
                                                   hid[:, t * 256 + k * P:t * 256 + (k + 1) * P], ident[:])
                last.then_inc(ffn_turned, 1)

            def ffn_hidden(k, t):
                return ht_hi[:, k * S + t * P:k * S + (t + 1) * P], ht_lo[:, k * S + t * P:k * S + (t + 1) * P]

            def ffn_step(j, c, i, opens=False):
                p = FFN0 + 2 + 3 * j
                pe.wait_ge(ffn_hid, c + 1)
                token_cols(p, 0, (0, 1), TT, i)
                ffn_turn(c)
                token_cols(p + 1, 1, (0, 1), TT, i)
                pe.wait_ge(ffn_ht_lo, c + 1)
                token_rows(p + 2, ffn_hidden, 4, TT, opens, False, i)

            half_turned(1, 1)
            for kh in range(2):
                token_cols(FFN0 + kh, kh, (0, 1), TT)
            for j in range(2):
                ffn_step(j, j, 0, j == 0)
            with pe.Fori(1, FFN_STEPS // 2) as i:
                for j in range(2):
                    ffn_step(j, i * 2 + j, i)
            ffn_turn(FFN_STEPS - 1)
            pe.wait_ge(ffn_ht_lo, FFN_STEPS)
            token_rows(HGRN_QF - 1, ffn_hidden, 4, TT, False, True)

            turn(2, tok)
            half_turned(2, 1)
            for c in range(4):
                if c >= 2:
                    pe.wait_ge(q_ready, c - 1)
                for kh in range(2):
                    channel_out(HGRN_QF + 2 * c + kh, kh, 2 * (c % 2))

            def scores(n):
                f = lev[n % 2]
                if n:
                    pe.wait_ge(level_factors, n)
                    pe.wait_ge(level_taken, max(n - 1, 1))
                for b in range(HEADS if n == len(LEVELS) + 1 else HB):
                    if n == 0:
                        out_b, keys, queries = psum[:, 4 + b // 4, (b % 4) * P:(b % 4 + 1) * P], hk, hq
                        queries = queries[:, b * P:(b + 1) * P]
                        keys = keys[:, b * P:(b + 1) * P]
                    elif n == len(LEVELS) + 1:
                        out_b = psum[:, group_bank(n) + b // 4, (b % 4) * P:(b % 4 + 1) * P]
                        keys, queries = f[:, 2 * b * P:(2 * b + 1) * P], f[:, (2 * b + 1) * P:(2 * b + 2) * P]
                    else:
                        out_b = psum[:, group_bank(n) + b // 8, (b % 8) * (P // 2):(b % 8 + 1) * (P // 2)]
                        keys = f[:, b * P:(b + 1) * P]
                        queries = keys.rearrange("p (x two l) -> p x two l", two=2, l=LEVELS[n - 1])[:, :, 1, :]
                        out_b = out_b.rearrange("p (x l) -> p x l", l=LEVELS[n - 1])
                    last = mm(out_b, keys, queries, start=True, stop=True)
                last.then_inc(level_scores, 1)

            pe.wait_ge(k_ready, 4)
            pe.wait_ge(q_ready, 4)
            for n in range(8):
                c, kh = divmod(n, 2)
                if c >= 2:
                    pe.wait_ge(vg_out, c - 1)
                token_cols(HGRN_VG + n, kh, (2 * (c % 2), 2 * (c % 2) + 1), TT)
                if n:
                    scores(n - 1)
            scores(len(LEVELS))
            scores(len(LEVELS) + 1)
            pe.wait_ge(level_taken, len(LEVELS) + 2)
            pe.wait_ge(vg_out, 4)
            for t in range(TT):
                for hd in range(HEADS):
                    o = psum[:, 4 + 2 * t + hd // 4, (hd % 4) * P:(hd % 4 + 1) * P]
                    b = (hd * TT + t) * P
                    if t:
                        mm(o, s_cross[:, hd * P:(hd + 1) * P], hv[:, hd * P:(hd + 1) * P], start=True, stop=False)
                    last = mm(o, s_same[:, b:b + P], hv[:, t * D + hd * P:t * D + (hd + 1) * P],
                              start=t == 0, stop=True)
                last.then_inc(o_proj, 1)
            turn(3, ho)
            for n in range(4):
                half_turned(3, n // 2)
                token_rows(HGRN_OUT + n, from_xt(2 * n), 4, TT, n == 0, n == 3)

            turn(4, mx)
            half_turned(4, 1)
            pe.wait_ge(router_split, 1)
            for t in range(TT):
                ops = ((xt_hi, router_hi), (xt_lo, router_hi), (xt_hi, router_lo))
                for i, (a, b) in enumerate(ops):
                    for k in range(KT):
                        last = mm(psum[:, 7, t * E:(t + 1) * E], a[:, k, t * P:(t + 1) * P], b[:, k, :],
                                  start=i == 0 and k == 0, stop=i == 2 and k == KT - 1)
            last.then_inc(logits_done, 1)
            pe.wait_ge(sel_ready, 1)
            mm(psum[:, 6, 0:E], before[:], sel[:, 0, :], start=True, stop=True)
            mm(psum[:, 6, E:2 * E], before[:], sel[:, 1, :], start=True, stop=False)
            mm(psum[:, 6, E:2 * E], ones[:], sel[:, 0, :], start=False, stop=True)
            mm(psum[:, 6, 2 * E:3 * E], ones[:], sel[:, 0, :], start=True, stop=False)
            mm(psum[:, 6, 2 * E:3 * E], ones[:], sel[:, 1, :], start=False, stop=True).then_inc(count_done, 1)

            pe.wait_ge(tables_ready, 1)
            jobs = pe.value_load(jobs_n[0:1, 0:1], min_val=E, max_val=JOBS)

            def moe_turn(n):
                pe.wait_ge(moe_hid, n + 2)
                for k in range(4):
                    last = nc.tensor.transpose(psum[:, 2, k * P:(k + 1) * P], hid[:, k * P:(k + 1) * P], ident[:])
                last.then_inc(moe_turned, 1)

            def slot_hidden(k0):
                return lambda k, t: (ht_hi[:, (k0 + k) * P:(k0 + k + 1) * P],
                                     ht_lo[:, (k0 + k) * P:(k0 + k + 1) * P])

            def moe_step(n, turns, opens=False):
                pe.wait_ge(moe_silu, n + 1)
                for kh in range(2):
                    token_cols(MOE + 4 + kh, kh, (0,), 1, turns)
                moe_turn(n)
                for kh in range(2):
                    token_cols(MOE + 6 + kh, kh, (1,), 1, turns)
                pe.wait_ge(moe_ht_lo, n + 1)
                for kk in range(2):
                    token_rows(MOE + 8 + kk, slot_hidden(2 * kk), 5, 1, opens and kk == 0, False, turns)

            def gather(j):
                pe.wait_ge(pick_ready, j + 1)
                for k in range(KT):
                    for t in range(TT):
                        last = mm(psum[:, 3 + k // 4, (k % 4) * P:(k % 4 + 1) * P], mx[:, t, k * P:(k + 1) * P],
                                  pick[:, t, :], start=t == 0, stop=t == TT - 1)
                    if k % 4 == 3:
                        last.then_inc(gathered, 1)

            def scatter(j):
                pe.wait_ge(y_ready, j + 1)
                pe.wait_ge(pick_t_ready, j + 1)
                for t in range(TT):
                    for half in range(2):
                        mm(psum[:, SCATTER_BANKS[2 * t + half], :], pick_t[:, t * P:(t + 1) * P],
                           ysb[:, half * BANK:(half + 1) * BANK], start=True, stop=True).then_inc(scattered, 1)

            gather(0)
            with pe.Fori(0, jobs) as j:
                turns = j * EXPERT_TURNS
                pe.wait_ge(xg_lo, j * 2 + 2)
                for kh in range(2):
                    token_cols(MOE + kh, kh, (0,), 1, turns)
                scatter(j)
                for kh in range(2):
                    token_cols(MOE + 2 + kh, kh, (1,), 1, turns)
                pe.wait_ge(acc_added, j * 4 + 5)
                for t in range(TT):
                    last = nc.tensor.transpose(psum[:, 7, t * P:(t + 1) * P], pick[:, t, :], ident[:])
                last.then_inc(pick_turned, 1)
                moe_step(j * MOE_STEPS, turns, True)
                with pe.Fori(1, MOE_STEPS - 1) as c:
                    moe_step(j * MOE_STEPS + c, turns + c)
                n = j * MOE_STEPS + (MOE_STEPS - 1)
                moe_turn(n)
                gather(j + 1)
                pe.wait_ge(moe_ht_lo, n + 1)
                for kk in range(2):
                    token_rows(MOE + 4 + kk, slot_hidden(2 * kk), 5, 1, False, kk == 1, turns + (MOE_STEPS - 1))
            pe.wait_ge(xg_lo, jobs * 2 + 2)
            scatter(jobs)

        @block.scalar
        def _(act):
            fn = nc.scalar.activation
            warmed = [0]

            def hi(p, turns=0):
                act.wait_ge(raw_loaded[p % RAW_RING], turns * 32 + 32 * (p // RAW_RING + 1))
                if p >= SPLIT_RING:
                    act.wait_ge(piece_used, turns * RAW_RING + (p - SPLIT_RING + 1))
                fn(w_hi[:, p % SPLIT_RING, :], raw[:, p % RAW_RING, :], ACT.Copy).then_inc(hi_ready, 1)

            def load_table(func):
                fn(warm[:, warmed[0]:warmed[0] + 1], ones[:, 0:1], func)
                warmed[0] += 1

            def squares(t, src):
                fn(junk[:, t * D:(t + 1) * D], src, ACT.Square, accum_out=ssq[:, t:t + 1]).then_inc(squares_ready, 1)

            def row_root(count):
                act.wait_ge(squares_ready, TT * (count + 1))
                fn(root[:, 0:TT], ssq[:], ACT.Sqrt, scale=1.0 / D, bias=eps[:]).then_inc(root_ready, 1)

            def post_root(n, source, count):
                for t in range(TT):
                    if n == 0:
                        act.wait_ge(source_ready, t + 1)
                    elif n < 3:
                        act.wait_ge(tile_done, n + 1) if t == 0 else used((0, HGRN_QF - 1, MOE - 1)[n])
                    squares(t, source(t))
                row_root(count)

            def pre_root(n, count):
                for t in range(TT):
                    act.wait_ge(residual_ready, TT * n + t + 1)
                    squares(t, h[:, t, :])
                row_root(count)

            def turn_hi_part(n, gain):
                for b in range(4):
                    act.wait_ge(turned, 4 * n + b + 1)
                    if gain is None:
                        fn(xt_hi[:, 2 * b:2 * b + 2, :], bank(b).rearrange("p (k s) -> p k s", k=2),
                           ACT.Copy).then_inc(turn_hi, 2)
                    else:
                        for k in (2 * b, 2 * b + 1):
                            fn(xt_hi[:, k, :], psum[:, b, (k % 2) * S:(k % 2 + 1) * S], ACT.Copy,
                               scale=cols[:, gain + k:gain + k + 1]).then_inc(turn_hi, 1)

            def used(p):
                act.wait_ge(piece_used, p + 1)

            act.wait_ge(consts_ready, 4)
            load_table(ACT.Sqrt)
            act.wait_ge(x_loaded, 16)
            for t in range(TT):
                squares(t, h[:, t, :])
            row_root(0)
            act.wait_ge(cols_ready, 1)
            turn_hi_part(0, NG)
            for p in range(3):
                hi(p)
            load_table(ACT.Sigmoid)

            def build_diag(i, taps=range(W)):
                for w in taps:
                    if i:
                        act.wait_ge(diag_used, W * (i - 1) + w + 1)
                    col = tap_col(w, PE_CONV[i])
                    fn(diag[:, w, :], ident[:], ACT.Copy, scale=cols[:, col:col + 1]).then_inc(diag_ready, 1)

            def gate_sigmoid(c):
                used(2 * c + 1)
                if c >= 2:
                    act.wait_ge(glu_out, c - 1)
                for b in range(2):
                    k = 2 * c + b
                    fn(conv_sig[:, 2 * (c % 2) + b, :], psum[:, 2 * (c % 2) + 1, b * S:(b + 1) * S], ACT.Sigmoid,
                       bias=cols[:, B_IN + KT + k:B_IN + KT + k + 1]).then_inc(glu_sig, 1)

            def take_conv(i):
                k = PE_CONV[i]
                act.wait_ge(diag_used, W * (i + 1))
                fn(conv_y[:, k, :], psum[:, 6 + i % 2, 0:S], ACT.Identity,
                   bias=cols[:, DW_B + k:DW_B + k + 1]).then_inc(tensor_conv_done, 1)

            hi(3)
            gate_sigmoid(0)
            hi(4)
            build_diag(0, range(0, 8))
            hi(5)
            build_diag(0, range(8, 20))
            gate_sigmoid(1)
            hi(6)
            build_diag(0, range(20, W))
            hi(7)
            gate_sigmoid(2)
            hi(8)
            build_diag(1)
            take_conv(0)
            hi(9)
            gate_sigmoid(3)
            hi(10)
            build_diag(2)
            take_conv(1)
            take_conv(2)
            for k in range(KT):
                act.wait_ge(centred, k + 1)
                fn(conv_sq[:, k, :], conv_y[:, k, :], ACT.Square).then_inc(conv_squared, 1)
            load_table(ACT.Sqrt)
            act.wait_ge(variance_ready, 1)
            fn(conv_t, conv_var, ACT.Sqrt).then_inc(conv_root, 1)
            load_table(ACT.Silu)
            for k in range(KT):
                act.wait_ge(conv_scaled, k + 1)
                fn(conv_sq[:, k, :], conv_y[:, k, :], ACT.Silu, scale=cols[:, LN_G + k:LN_G + k + 1],
                   bias=cols[:, LN_B + k:LN_B + k + 1]).then_inc(conv_act, 1)
                if k % 2:
                    act.wait_ge(conv_act, k + 1)
                    fn(xt_hi[:, k - 1:k + 1, :], conv_sq[:, k - 1:k + 1, :], ACT.Copy).then_inc(conv_hi, 1)
            hi(CONV_OUT + 3)
            hi(FFN0)
            load_table(ACT.Sqrt)
            post_root(0, lambda t: biased[:, t, :], 1)
            pre_root(0, 2)
            turn_hi_part(1, NG + 2 * KT)
            hi(FFN0 + 1)
            act.wait_ge(lb_arg, 1)
            fn(lb_t[:, 2:4, :], lb_t[:, 0:2, :], ACT.Exp).then_inc(lb_exp, 1)
            load_table(ACT.Silu)

            def ffn_act(c, p):
                fn(act_sb.rearrange("p (t n) -> p t n", t=TT), psum[:, 0:TT, 0:FFN_CHUNK], ACT.Silu).then_inc(
                    ffn_silu, 1)

            def ffn_round(c):
                act.wait_ge(ffn_turned, c + 1)
                fn(ht_hi[:], bank(2), ACT.Copy).then_inc(ffn_ht_hi, 1)

            with act.Fori(0, FFN_STEPS // 2) as i:
                for j in range(2):
                    p = FFN0 + 2 + 3 * j
                    c = i * 2 + j
                    hi(p, i)
                    act.wait_ge(piece_used, i * RAW_RING + (p - 1))
                    act.wait_ge(piece_used, FFN0 + 2)
                    ffn_act(c, p)
                    hi(p + 1, i)
                    hi(p + 2, i)
                    ffn_round(c)
            hi(HGRN_QF - 1)
            used(HGRN_QF - 3)
            ffn_act(FFN_STEPS - 1, 0)
            hi(HGRN_QF)
            ffn_round(FFN_STEPS - 1)
            hi(HGRN_QF + 1)
            load_table(ACT.Sqrt)
            post_root(1, lambda t: bank(4 + 2 * t, 2), 3)
            pre_root(1, 4)
            turn_hi_part(2, NG + 4 * KT)
            load_table(ACT.Sigmoid)
            hi(HGRN_QF + 2)
            hi(HGRN_QF + 3)
            for c in range(4):
                used(HGRN_QF + 2 * c + 1)
                fn(hk[:, c * 512:(c + 1) * 512], bank(2 * (c % 2) + 1), ACT.Sigmoid).then_inc(qf_sig, 1)
                fn(hq[:, c * 512:(c + 1) * 512], bank(2 * (c % 2)), ACT.Sigmoid).then_inc(qf_sig, 1)
                for p in (HGRN_QF + 4 + 2 * c, HGRN_QF + 5 + 2 * c)[:2 * (c < 3)]:
                    hi(p)
            load_table(ACT.Ln)
            for c, part in enumerate((slice(0, 1536), slice(1536, 2048))):
                act.wait_ge(k_ready, 3 + c)
                fn(lev[0][:, part], lev[0][:, part], ACT.Ln).then_inc(log_ready, 1)
            load_table(ACT.Exp)
            hi(HGRN_VG + 2)

            def level(n):
                act.wait_ge(level_arg, n)
                fn(lev[n % 2], lev[n % 2], ACT.Exp).then_inc(level_exp, 1)

            level(1)
            for n in range(1, 8):
                if HGRN_VG + 2 + n < HGRN_OUT:
                    hi(HGRN_VG + 2 + n)
                level(n + 1)
                if n % 2:
                    c = n // 2
                    used(HGRN_VG + 2 * c + 1)
                    dst = (hv if c < 2 else hog).rearrange("p (t d) -> p t d", t=TT)
                    fn(dst[:, :, (c % 2) * 512:(c % 2 + 1) * 512], psum[:, 2 * (c % 2):2 * (c % 2) + 2, :],
                       ACT.Copy).then_inc(vg_out, 1)
            for p in range(HGRN_OUT, HGRN_OUT + 3):
                hi(p)
            act.wait_ge(vg_out, 4)
            fn(hog, hog, ACT.Silu).then_inc(og_ready, 1)
            for t in range(TT):
                act.wait_ge(o_proj, t + 1)
                fn(hsq[:, t * D:(t + 1) * D], bank(4 + 2 * t, 2), ACT.Square).then_inc(o_squared, 1)
            load_table(ACT.Sqrt)
            for t in range(TT):
                act.wait_ge(variance_ready, 2 + t)
                one = slice(t * HEADS, (t + 1) * HEADS)
                fn(root[:, one], var[:, one], ACT.Sqrt).then_inc(head_root, 1)
            turn_hi_part(3, None)
            hi(HGRN_OUT + 3)
            load_table(ACT.Sqrt)
            post_root(2, lambda t: bank(4 + 2 * t, 2), 5)
            pre_root(2, 6)
            act.wait_ge(small_loaded, 16)
            fn(router_hi[:], router[:], ACT.Copy).then_inc(router_hi_ready, 1)
            turn_hi_part(4, None)
            act.wait_ge(gate_arg, 1)
            fn(weight[:, 1, :], weight[:, 0, :], ACT.Exp).then_inc(gate_exp, 1)
            act.wait_ge(tables_ready, 1)
            jobs = act.value_load(jobs_n[0:1, 0:1], min_val=E, max_val=JOBS)

            def moe_act(n, p, turns):
                act.wait_ge(piece_used, turns * RAW_RING + (p + 1))
                act.wait_ge(moe_hid, n + 1)
                fn(act_sb, bank(0), ACT.Silu).then_inc(moe_silu, 1)

            def moe_round(n):
                act.wait_ge(moe_turned, n + 1)
                fn(ht_hi[:], bank(2), ACT.Copy).then_inc(moe_ht_hi, 1)

            def gather_round(j):
                for b in range(2):
                    act.wait_ge(gathered, j * 2 + b + 1)
                    fn(xt_hi[:, 4 * b:4 * b + 4, 0:P], psum[:, 3 + b, :].rearrange("p (k s) -> p k s", k=4),
                       ACT.Copy).then_inc(xg_hi, 1)

            def take_output(j):
                act.wait_ge(piece_used, j * EXPERT_PIECES + MOE)
                fn(ysb, bank(5, 2), ACT.Copy).then_inc(y_ready, 1)

            def moe_split_step(n, turns, between=None):
                for p in range(4, 8):
                    if p == 6 and between:
                        between()
                    hi(MOE + p, turns)
                moe_round(n)
                moe_act(n + 1, MOE + 5, turns)
                for p in range(8, 10):
                    hi(MOE + p, turns)

            gather_round(0)
            with act.Fori(0, jobs) as j:
                turns = j * EXPERT_TURNS
                n = j * MOE_STEPS

                def turned_pick():
                    act.wait_ge(pick_turned, j + 1)
                    fn(pick_t, bank(7)[:, 0:TT * P], ACT.Copy).then_inc(pick_t_ready, 1)

                hi(MOE, turns)
                hi(MOE + 1, turns)
                take_output(j)
                hi(MOE + 2, turns)
                hi(MOE + 3, turns)
                moe_act(n, MOE + 1, turns)
                moe_split_step(n, turns, turned_pick)
                with act.Fori(1, MOE_STEPS - 1) as c:
                    moe_split_step(n + c, turns + c)
                for p in range(2):
                    hi(MOE + 4 + p, turns + (MOE_STEPS - 1))
                moe_round(n + (MOE_STEPS - 1))
                gather_round(j + 1)
            take_output(jobs)
            act.wait_ge(moe_done, 1)
            post_root(3, lambda t: acc[:, t, :], 7)

        @block.vector
        def _(dve):
            v = nc.vector
            steps = [0]

            def step(ins):
                steps[0] += 1
                ins.then_inc(dve_step, 1)
                dve.wait_ge(dve_step, steps[0])

            def lo(p, turns=0):
                dve.wait_ge(hi_ready, turns * RAW_RING + (p + 1))
                v.tensor_tensor(w_lo[:, p % SPLIT_RING, :], raw[:, p % RAW_RING, :],
                                w_hi[:, p % SPLIT_RING, :].bitcast(F32), ALU.subtract).then_inc(lo_ready, 1)

            def inverse_root(r, va, ro, nw):
                step(v.reciprocal(ro, ro))
                step(v.tensor_tensor(nw, ro, ro, ALU.mult))
                step(v.tensor_tensor(nw, nw, va, ALU.mult))
                step(v.scalar_tensor_tensor(out=r, in0=nw, scalar=-3.0, in1=ro, op0=ALU.add, op1=ALU.mult))

            def row_variance(count):
                dve.wait_ge(squares_ready, TT * (count + 1))
                step(v.tensor_scalar(var[:, 0:TT], ssq[:], 1.0 / D, EPS, ALU.mult, ALU.add))

            def row_factor(count):
                dve.wait_ge(root_ready, count + 1)
                inverse_root(rstd[:, 0:TT], var[:, 0:TT], root[:, 0:TT], newton[:, 0, 0:TT])

            def pre_norm(count):
                row_variance(count)
                row_factor(count)
                for t in range(TT):
                    v.tensor_scalar(tok[:, t, :], h[:, t, :], rstd[:, t:t + 1], -0.5, ALU.mult,
                                    ALU.mult).then_inc(normed, 1)

            def post_norm(src, n, count):
                dve.wait_ge(row_loaded[1], 16 * (n + 1))
                for t in range(TT):
                    dve.wait_ge(squares_ready, TT * count + t + 1)
                    v.scalar_tensor_tensor(out=tok[:, t, :], in0=src(t), scalar=-0.5, in1=row[:, 1, :],
                                           op0=ALU.mult, op1=ALU.mult).then_inc(gained, 1)
                row_variance(count)
                row_factor(count)
                for t in range(TT):
                    dve.wait_ge(gained, TT * n + t + 1)
                    v.scalar_tensor_tensor(out=h[:, t, :], in0=tok[:, t, :], scalar=rstd[:, t:t + 1],
                                           in1=h[:, t, :], op0=ALU.mult, op1=ALU.add).then_inc(residual_ready, 1)
                v.memset(tick[:], 0.0).then_inc(row_used[1], 1)
                dve.wait_ge(residual_ready, TT * (n + 1))

            def turn_lo_part(n, gain):
                for b in range(4):
                    if gain is None:
                        dve.wait_ge(turn_hi, KT * n + 2 * b + 2)
                        v.tensor_tensor(xt_lo[:, 2 * b:2 * b + 2, :], bank(b).rearrange("p (k s) -> p k s", k=2),
                                        xt_hi[:, 2 * b:2 * b + 2, :].bitcast(F32), ALU.subtract).then_inc(turn_lo, 1)
                    else:
                        dve.wait_ge(turn_hi, KT * n + 2 * b + 2)
                        for k in (2 * b, 2 * b + 1):
                            ins = v.scalar_tensor_tensor(
                                out=xt_lo[:, k, :], in0=psum[:, b, (k % 2) * S:(k % 2 + 1) * S],
                                scalar=cols[:, gain + k:gain + k + 1], in1=xt_hi[:, k, :].bitcast(F32),
                                op0=ALU.mult, op1=ALU.subtract)
                        ins.then_inc(turn_lo, 1)

            pre_norm(0)
            dve.wait_ge(cols_turned, 1)
            v.tensor_copy(cols[:, 0:ROWS0], psum[:, 4, 0:ROWS0])
            v.tensor_copy(cols[:, TAPS:TAPS + W * KT], psum[:, 4, P:P + W * KT]).then_inc(cols_ready, 1)
            dve.wait_ge(cols_ready, 1)
            turn_lo_part(0, NG)
            for p in range(3):
                lo(p)

            step(v.memset(conv_u[:, :, 0:W - 1], 0.0))
            UNROLL = 6

            def glu(c):
                for b in range(2):
                    k = 2 * c + b
                    dve.wait_ge(glu_sig, k + 1)
                    ins = v.scalar_tensor_tensor(
                        out=conv_u[:, k, W - 1:], in0=psum[:, 2 * (c % 2), b * S:(b + 1) * S],
                        scalar=cols[:, B_IN + k:B_IN + k + 1], in1=conv_sig[:, 2 * (c % 2) + b, :],
                        op0=ALU.add, op1=ALU.mult)
                ins.then_inc(glu_out, 1)
                dve.wait_ge(glu_out, c + 1)

            def conv_part(i, part):
                k = DVE_CONV[i]
                even, odd = conv_y[:, k, :], conv_sq[:, k, :]
                if part == 0:
                    v.memset(odd, 0.0).then_inc(tap_added, 1)
                    v.tensor_scalar(even, conv_u[:, k, 0:S], cols[:, tap_col(0, k):tap_col(0, k) + 1],
                                    cols[:, DW_B + k:DW_B + k + 1], ALU.mult, ALU.add).then_inc(tap_added, 1)
                with dve.Fori(*((0, 3), (3, 5))[part]) as turn:
                    for u in range(UNROLL):
                        acc_buf = even if u % 2 else odd
                        dve.wait_ge(tap_added, turn * UNROLL + ((W + 1) * i + 1 + u))
                        v.scalar_tensor_tensor(
                            out=acc_buf, in0=conv_u[:, k, bass.ds(turn * UNROLL + (1 + u), S)],
                            scalar=cols[:, bass.ds(turn * (UNROLL * KT) + (TAPS + KT * (1 + u) + k), 1)],
                            in1=acc_buf, op0=ALU.mult, op1=ALU.add).then_inc(tap_added, 1)
                if part:
                    dve.wait_ge(tap_added, (W + 1) * (i + 1))
                    v.tensor_tensor(even, even, odd, ALU.add).then_inc(conv_done, 1)

            assert W == 5 * UNROLL + 1
            lo(3)
            glu(0)
            lo(4)
            conv_part(0, 0)
            lo(5)
            conv_part(0, 1)
            glu(1)
            lo(6)
            conv_part(1, 0)
            lo(7)
            conv_part(1, 1)
            glu(2)
            lo(8)
            conv_part(2, 0)
            conv_part(2, 1)
            glu(3)
            for i in (3, 4):
                for part in range(2):
                    conv_part(i, part)
            lo(CONV_OUT + 1)
            dve.wait_ge(mean_sum, 1)
            step(v.tensor_scalar(conv_mean, psum[:, 4, 0:S], 1.0 / D, None, ALU.mult))
            for k in range(KT):
                v.tensor_tensor(conv_y[:, k, :], conv_y[:, k, :], conv_mean, ALU.subtract).then_inc(centred, 1)
            lo(CONV_OUT + 2)
            dve.wait_ge(var_sum, 1)
            v.tensor_scalar(conv_var, psum[:, 5, 0:S], 1.0 / D, EPS, ALU.mult, ALU.add).then_inc(variance_ready, 1)
            dve.wait_ge(conv_root, 1)
            inverse_root(conv_r, conv_var, conv_t, conv_mean)
            for k in range(KT):
                v.scalar_tensor_tensor(out=conv_y[:, k, :], in0=conv_y[:, k, :], scalar=-0.5, in1=conv_r,
                                       op0=ALU.mult, op1=ALU.mult).then_inc(conv_scaled, 1)
            for n in range(4):
                dve.wait_ge(conv_hi, n + 1)
                pair = slice(2 * n, 2 * n + 2)
                v.tensor_tensor(xt_lo[:, pair, :], conv_sq[:, pair, :], xt_hi[:, pair, :].bitcast(F32),
                                ALU.subtract).then_inc(conv_lo, 1)
            lo(CONV_OUT + 3)
            lo(FFN0)
            dve.wait_ge(row_loaded[0], 16)
            for t in range(TT):
                if t == 0:
                    dve.wait_ge(tile_done, 1)
                else:
                    dve.wait_ge(piece_used, CONV_OUT + 4)
                v.tensor_tensor(biased[:, t, :], bank(4 + 2 * t, 2), row[:, 0, :], ALU.add).then_inc(source_ready, 1)
            dve.wait_ge(source_ready, TT)
            v.memset(tick[:], 0.0).then_inc(row_used[0], 1)
            post_norm(lambda t: biased[:, t, :], 0, 1)
            pre_norm(2)
            turn_lo_part(1, NG + 2 * KT)
            b0, b1 = cols[:, LB:LB + KT], cols[:, LB + KT:LB + 2 * KT]
            step(v.tensor_tensor(lb_t[:, 4, :], b0, b1, ALU.max))
            v.tensor_tensor(lb_t[:, 0, :], b0, lb_t[:, 4, :], ALU.subtract)
            v.tensor_tensor(lb_t[:, 1, :], b1, lb_t[:, 4, :], ALU.subtract).then_inc(lb_arg, 1)
            lo(FFN0 + 1)
            dve.wait_ge(lb_exp, 1)
            step(v.tensor_tensor(lb_t[:, 4, :], lb_t[:, 2, :], lb_t[:, 3, :], ALU.add))
            step(v.reciprocal(lb_t[:, 5, :], lb_t[:, 4, :]))
            step(v.tensor_tensor(lb_c[:, 0, :], lb_t[:, 3, :], lb_t[:, 5, :], ALU.mult))
            step(v.tensor_scalar(lb_c[:, 1, :], lb_c[:, 0, :], -1.0, 1.0, ALU.mult, ALU.add))
            dve.wait_ge(consts_ready, 4)
            xor_t, xor_f, mask_f = scratch[:, 15000:15128], scratch[:, 15128:15256], scratch[:, 15256:15384]
            step(v.tensor_copy(slot_id[:], slot_i[:]))
            step(v.tensor_tensor(xor_t.bitcast(I32), slot_i[:], slot_p[:].to_broadcast([P, P]), ALU.bitwise_xor))
            step(v.tensor_copy(xor_f, xor_t.bitcast(I32)))
            step(v.tensor_tensor(xor_f, xor_f, before[:], ALU.mult))
            for i, length in enumerate(LEVELS):
                step(v.tensor_scalar(mask_f, xor_f, float(length), None, ALU.is_ge))
                step(v.scalar_tensor_tensor(out=level_mask[:, i, :], in0=xor_f, scalar=float(2 * length),
                                            in1=mask_f, op0=ALU.is_lt, op1=ALU.mult))

            def ffn_mult(c):
                dve.wait_ge(ffn_silu, c + 1)
                v.tensor_tensor(hid.rearrange("p (t n) -> p t n", t=TT), psum[:, 0:TT, FFN_CHUNK:2 * FFN_CHUNK],
                                act_sb.rearrange("p (t n) -> p t n", t=TT), ALU.mult).then_inc(ffn_hid, 1)

            def ffn_rest(c):
                dve.wait_ge(ffn_ht_hi, c + 1)
                v.tensor_tensor(ht_lo[:], bank(2), ht_hi[:].bitcast(F32), ALU.subtract).then_inc(ffn_ht_lo, 1)

            with dve.Fori(0, FFN_STEPS // 2) as i:
                for j in range(2):
                    p = FFN0 + 2 + 3 * j
                    c = i * 2 + j
                    lo(p, i)
                    ffn_mult(c)
                    lo(p + 1, i)
                    lo(p + 2, i)
                    ffn_rest(c)
            lo(HGRN_QF - 1)
            ffn_mult(FFN_STEPS - 1)
            lo(HGRN_QF)
            ffn_rest(FFN_STEPS - 1)
            lo(HGRN_QF + 1)
            post_norm(lambda t: bank(4 + 2 * t, 2), 1, 3)
            pre_norm(4)
            turn_lo_part(2, NG + 4 * KT)
            lo(HGRN_QF + 2)
            lo(HGRN_QF + 3)

            for c in range(4):
                part = slice(c * 512, (c + 1) * 512)
                dve.wait_ge(qf_sig, 2 * c + 1)
                for k in (2 * c, 2 * c + 1):
                    one = slice(k * S, (k + 1) * S)
                    ins = v.tensor_scalar(lev[0][:, one], hk[:, one], lb_c[:, 1, k:k + 1], lb_c[:, 0, k:k + 1],
                                          ALU.mult, ALU.add)
                ins.then_inc(forget_ready, 1)
                dve.wait_ge(forget_ready, c + 1)
                v.tensor_scalar(hk[:, part], lev[0][:, part], -1.0, 1.0, ALU.mult, ALU.add).then_inc(k_ready, 1)
                dve.wait_ge(qf_sig, 2 * c + 2)
                v.tensor_tensor(hq[:, part], bank(2 * (c % 2)), hq[:, part], ALU.mult).then_inc(q_ready, 1)
                for p in (HGRN_QF + 4 + 2 * c, HGRN_QF + 5 + 2 * c)[:2 * (c < 3)]:
                    lo(p)
            dve.wait_ge(k_ready, 4)
            dve.wait_ge(q_ready, 4)
            for b in range(HB):
                if b * P in (0, 1536):
                    dve.wait_ge(log_ready, 1 + b * P // 1536)
                one = slice(b * P, (b + 1) * P)
                ins = v.tensor_tensor_scan(hg[:, one], ones[:], lev[0][:, one], 0.0, ALU.mult, ALU.add)
            step(ins)

            def halves(buf, n):
                length = P if n == len(LEVELS) + 1 else LEVELS[n - 1]
                w = buf.rearrange("p (x two l) -> p x two l", two=2, l=length)
                return w[:, :, 0, :], w[:, :, 1, :], length

            def level_diff(n):
                if n > 2:
                    dve.wait_ge(level_scores, n - 1)
                left, right, length = halves(lev[n % 2], n)
                g_left, g_right, _ = halves(hg, n)
                end = g_left[:, :, length - 1:length].to_broadcast([P, HEADS * S // (2 * length), length])
                v.tensor_tensor(left, end, g_left, ALU.subtract)
                if n == len(LEVELS) + 1:
                    v.tensor_copy(right, g_right).then_inc(level_arg, 1)
                else:
                    v.tensor_tensor(right, g_right, end, ALU.subtract).then_inc(level_arg, 1)

            def level_mult(n):
                dve.wait_ge(level_exp, n)
                left, right, _ = halves(lev[n % 2], n)
                v.tensor_tensor(left, left, halves(hk, n)[0], ALU.mult)
                v.tensor_tensor(right, right, halves(hq, n)[1], ALU.mult).then_inc(level_factors, 1)

            def level_take(n):
                dve.wait_ge(level_scores, n + 1)
                if n:
                    dve.wait_ge(level_taken, n)
                by_pair = s_same.rearrange("p (b t) -> p b t", b=HB)
                if n == 0:
                    v.tensor_tensor(by_pair, bank(4, 4).rearrange("p (b t) -> p b t", b=HB),
                                    ident[:].rearrange("p (a t) -> p a t", a=1).to_broadcast([P, HB, P]),
                                    ALU.mult).then_inc(level_taken, 1)
                elif n == len(LEVELS) + 1:
                    v.tensor_copy(s_cross, bank(group_bank(n), 2)).then_inc(level_taken, 1)
                else:
                    length = LEVELS[n - 1]
                    blocks = P // (2 * length)
                    right = "p b (x two l) -> p b x two l"
                    dst = by_pair.rearrange(right, two=2, l=length)[:, :, :, 1, :]
                    mask = level_mask[:, n - 1:n, :].rearrange(right, two=2, l=length)[:, :, :, 1, :]
                    src = bank(group_bank(n), 2).rearrange("p (b x l) -> p b x l", b=HB, l=length)
                    v.copy_predicated(dst, mask.to_broadcast([P, HB, blocks, length]), src).then_inc(level_taken, 1)

            level_diff(1)
            lo(HGRN_VG + 2)
            level_mult(1)
            for n in range(1, 8):
                level_diff(n + 1)
                level_take(n - 1)
                if HGRN_VG + 2 + n < HGRN_OUT:
                    lo(HGRN_VG + 2 + n)
                level_mult(n + 1)
            level_take(7)
            level_take(8)
            dve.wait_ge(og_ready, 1)
            dve.wait_ge(row_loaded[0], 32)
            gain = row[:, 0:1, 0:P].to_broadcast([P, HB, P])
            by_head = "p (b c) -> p b c"
            step(v.scalar_tensor_tensor(out=hog.rearrange(by_head, b=HB), in0=hog.rearrange(by_head, b=HB),
                                        scalar=-0.5, in1=gain, op0=ALU.mult, op1=ALU.mult))
            v.memset(tick[:], 0.0).then_inc(row_used[0], 1)
            lo(HGRN_OUT)
            dve.wait_ge(row_used[0], 2)
            for t in range(TT):
                one = slice(t * HEADS, (t + 1) * HEADS)
                dve.wait_ge(o_squared, t + 1)
                step(v.tensor_reduce(var[:, one], hsq[:, t * D:(t + 1) * D].rearrange(by_head, b=HEADS), AX.X,
                                     ALU.add))
                v.tensor_scalar(var[:, one], var[:, one], 1.0 / P, EPS, ALU.mult, ALU.add).then_inc(
                    variance_ready, 1)
            for t in range(TT):
                one = slice(t * HEADS, (t + 1) * HEADS)
                cut = slice(t * D, (t + 1) * D)
                dve.wait_ge(variance_ready, 2 + t)
                dve.wait_ge(head_root, t + 1)
                inverse_root(rstd[:, one], var[:, one], root[:, one], newton[:, 0, one])
                scale = rstd[:, one].rearrange("p (b a) -> p b a", a=1).to_broadcast([P, HEADS, P])
                step(v.tensor_tensor(hq[:, cut].rearrange(by_head, b=HEADS),
                                     bank(4 + 2 * t, 2).rearrange(by_head, b=HEADS), scale, ALU.mult))
                v.tensor_tensor(hq[:, cut], hq[:, cut], hog[:, cut], ALU.mult).then_inc(normed, 1)
            for p in (HGRN_OUT + 1, HGRN_OUT + 2):
                lo(p)
            turn_lo_part(3, None)
            lo(HGRN_OUT + 3)
            post_norm(lambda t: bank(4 + 2 * t, 2), 2, 5)
            row_variance(6)
            row_factor(6)
            step(v.tensor_scalar(rstd[:, 0:TT], rstd[:, 0:TT], -0.5, None, ALU.mult))
            dve.wait_ge(row_loaded[0], 48)
            for t in range(TT):
                v.scalar_tensor_tensor(out=mx[:, t, :], in0=h[:, t, :], scalar=rstd[:, t:t + 1],
                                       in1=row[:, 0, :], op0=ALU.mult, op1=ALU.mult).then_inc(normed, 1)
            dve.wait_ge(router_hi_ready, 1)
            v.tensor_tensor(router_lo[:], router[:], router_hi[:].bitcast(F32), ALU.subtract).then_inc(router_split, 1)
            v.memset(acc[:, :, :], 0.0).then_inc(acc_added, 1)
            v.memset(tick[:], 0.0).then_inc(moe_hid, 1)
            v.memset(pick_t, 0.0).then_inc(pick_t_ready, 1)
            turn_lo_part(4, None)
            dve.wait_ge(logits_done, 1)
            step(v.tensor_copy(logits[:], psum[:, 7, 0:TT * E].rearrange("p (t e) -> p t e", t=TT)))
            for t in range(TT):
                step(v.max(top[:, t, :], logits[:, t, :]))
                step(v.max_index(top_i[:, t, :], top[:, t, :], logits[:, t, :]))
            step(v.tensor_copy(top_f[:], top_i[:]))
            v.tensor_tensor(weight[:, 0, :], top[:, :, 1], top[:, :, 0], ALU.subtract).then_inc(gate_arg, 1)
            for t in range(TT):
                for rank in range(2):
                    step(v.tensor_scalar(chosen[:, rank, t, :], slot_id[:, 0:E], top_f[:, t, rank:rank + 1], None,
                                         ALU.is_equal))
            v.tensor_tensor(sel[:], chosen[:, 0, :, :], chosen[:, 1, :, :], ALU.add).then_inc(sel_ready, 1)
            dve.wait_ge(gate_exp, 1)
            step(v.tensor_scalar(weight[:, 2, :], weight[:, 1, :], 1.0, None, ALU.add))
            step(v.reciprocal(weight[:, 3, :], weight[:, 2, :]))
            step(v.tensor_tensor(weight[:, 2, :], weight[:, 1, :], weight[:, 3, :], ALU.mult))
            for t in range(TT):
                step(v.tensor_scalar(place[:, t, :], chosen[:, 0, t, :], weight[:, 3, t:t + 1], None, ALU.mult))
                step(v.scalar_tensor_tensor(out=gate_of[:, t, 1:E + 1], in0=chosen[:, 1, t, :],
                                            scalar=weight[:, 2, t:t + 1], in1=place[:, t, :],
                                            op0=ALU.mult, op1=ALU.add))
            v.tensor_copy(gate_of[:, :, E + 1:JOBS + 1], gate_of[:, :, 1:E + 1])
            dve.wait_ge(count_done, 1)
            step(v.scalar_tensor_tensor(out=place[:], in0=psum[:, 6, 0:TT * E].rearrange("p (t e) -> p t e", t=TT),
                                        scalar=1.0, in1=sel[:], op0=ALU.add, op1=ALU.mult))
            v.memset(slot_of[:, :, JOBS:JOBS + 1], -1.0)
            v.memset(gate_of[:, :, 0:1], 0.0)
            v.tensor_scalar(slot_of[:, :, 0:E], place[:], -1.0, None, ALU.add)
            v.tensor_scalar(slot_of[:, :, E:JOBS], place[:], -1.0 - P, None, ALU.add)
            step(v.tensor_reduce(busiest[:, 0:1], psum[:, 6, 2 * E:3 * E], AX.X, ALU.max))
            step(v.tensor_scalar(busiest[:, 1:2], busiest[:, 0:1], float(P), float(E), ALU.is_gt, ALU.mult))
            v.tensor_scalar(jobs_n[:], busiest[:, 1:2], float(E), None, ALU.add).then_inc(tables_ready, 1)
            dve.wait_ge(tables_ready, 1)
            jobs = dve.value_load(jobs_n[0:1, 0:1], min_val=E, max_val=JOBS)

            def moe_mult(n, p, turns):
                dve.wait_ge(moe_silu, n + 1)
                dve.wait_ge(piece_used, turns * RAW_RING + (p + 1))
                v.tensor_tensor(hid, bank(1), act_sb, ALU.mult).then_inc(moe_hid, 1)

            def moe_rest(n):
                dve.wait_ge(moe_ht_hi, n + 1)
                v.tensor_tensor(ht_lo[:], bank(2), ht_hi[:].bitcast(F32), ALU.subtract).then_inc(moe_ht_lo, 1)

            def make_pick(j):
                for t in range(TT):
                    ins = v.tensor_scalar(pick[:, t, :], slot_id[:], slot_of[:, t, bass.ds(j, 1)], None, ALU.is_equal)
                ins.then_inc(pick_ready, 1)

            def gather_rest(j):
                for b in range(2):
                    dve.wait_ge(xg_hi, j * 2 + b + 1)
                    v.tensor_tensor(xt_lo[:, 4 * b:4 * b + 4, 0:P],
                                    psum[:, 3 + b, :].rearrange("p (k s) -> p k s", k=4),
                                    xt_hi[:, 4 * b:4 * b + 4, 0:P].bitcast(F32), ALU.subtract).then_inc(xg_lo, 1)

            def add_output(j):
                for t in range(TT):
                    for half in range(2):
                        i = 2 * t + half
                        dve.wait_ge(scattered, j * 4 + i + 1)
                        dve.wait_ge(acc_added, j * 4 + 1)
                        part = acc[:, t, half * BANK:(half + 1) * BANK]
                        v.scalar_tensor_tensor(out=part, in0=bank(SCATTER_BANKS[i]),
                                               scalar=gate_of[:, t, bass.ds(j, 1)], in1=part,
                                               op0=ALU.mult, op1=ALU.add).then_inc(acc_added, 1)

            def moe_rest_step(n, turns, before_up=None, before_down=None):
                for p in range(4, 8):
                    if p == 6 and before_up:
                        before_up()
                    lo(MOE + p, turns)
                moe_rest(n)
                if before_down:
                    before_down()
                for p in range(8, 10):
                    lo(MOE + p, turns)
                moe_mult(n + 1, MOE + 7, turns)

            make_pick(0)
            gather_rest(0)
            with dve.Fori(0, jobs) as j:
                turns = j * EXPERT_TURNS
                n = j * MOE_STEPS

                def next_pick():
                    dve.wait_ge(pick_turned, j + 1)
                    make_pick(j + 1)

                for p in range(4):
                    lo(MOE + p, turns)
                add_output(j)
                moe_rest_step(n, turns, lambda: moe_mult(n, MOE + 3, turns), next_pick)
                with dve.Fori(1, MOE_STEPS - 1) as c:
                    moe_rest_step(n + c, turns + c)
                for p in range(2):
                    lo(MOE + 4 + p, turns + (MOE_STEPS - 1))
                moe_rest(n + (MOE_STEPS - 1))
                gather_rest(j + 1)
            add_output(jobs)
            v.memset(tick[:], 0.0).then_inc(moe_done, 1)
            dve.wait_ge(moe_done, 1)
            post_norm(lambda t: acc[:, t, :], 3, 7)


_INS = ["x", "norm_g", "conv_w_in", "conv_b_in", "conv_dw_w", "conv_dw_b", "conv_ln_g", "conv_ln_b", "conv_w_out",
        "conv_b_out", "hgrn_w_in", "hgrn_lower_bounds", "hgrn_norm_g", "hgrn_w_out", "ffn_w_gu", "ffn_w_down",
        "moe_router", "moe_w_gu", "moe_w_down"]


def kernel(**inputs):
    import numpy as np
    from concourse import bacc
    from concourse.bass_utils import run_bass_kernel_spmd

    nc = bacc.Bacc("TRN2", target_bir_lowering=False, num_devices=1)
    arrays, args = {}, []
    for name in _INS:
        a = np.ascontiguousarray(inputs[name])
        arrays[f"in_{name}"] = a
        args.append(nc.dram_tensor(f"in_{name}", a.shape, mybir.dt.from_np(a.dtype), kind="ExternalInput").ap())
    out = nc.dram_tensor("out", inputs["x"].shape, F32, kind="ExternalOutput").ap()
    trunk(nc, *args, out)
    r = run_bass_kernel_spmd(nc, [arrays], core_ids=[0])
    return r.results[0]["out"]
```

```python
from contextlib import ExitStack

import concourse.bass as bass
from concourse import mybir

F32 = mybir.dt.float32
F32R = mybir.dt.float32r
I32 = mybir.dt.int32
U32 = mybir.dt.uint32
ACT = mybir.ActivationFunctionType
ALU = mybir.AluOpType
AX = mybir.AxisListType

P = 128
EPS = 1e-6
BANK = 512
PIECE = 2048
SCATTER_BANKS = (3, 4, 7, 2)
RAW_RING = 6
EARLY = 4
SPLIT_RING = 3


def trunk(nc, x, norm_g, conv_w_in, conv_b_in, conv_dw_w, conv_dw_b, conv_ln_g, conv_ln_b,
          conv_w_out, conv_b_out, hgrn_w_in, hgrn_lower_bounds, hgrn_norm_g, hgrn_w_out,
          ffn_w_gu, ffn_w_down, moe_router, moe_w_gu, moe_w_down, out):
    _, S, D = x.shape
    TT = S // P
    KT = D // P
    W = conv_dw_w.shape[1]
    FFN = ffn_w_down.shape[1]
    E = moe_router.shape[2]
    ED = moe_w_down.shape[2]
    HEADS = D // P
    HB = HEADS * TT
    FFN_CHUNK = 256
    FFN_STEPS = FFN // FFN_CHUNK
    MOE_CHUNK = 512
    MOE_STEPS = ED // MOE_CHUNK
    JOBS = 2 * E
    LEVELS = [64, 32, 16, 8, 4, 2, 1]
    assert TT == 2 and KT == 8 and FFN % FFN_CHUNK == 0 and ED % MOE_CHUNK == 0 and FFN_STEPS % 2 == 1

    CONV_IN = 0
    CONV_OUT = CONV_IN + 2 * D * KT * P // (P * PIECE)
    FFN0 = CONV_OUT + D * D // (P * PIECE)
    HGRN_QF = FFN0 + 3 * FFN_STEPS
    HGRN_VG = HGRN_QF + 2 * D * D // (P * PIECE)
    HGRN_OUT = HGRN_VG + 2 * D * D // (P * PIECE)
    MOE = HGRN_OUT + D * D // (P * PIECE)
    EXPERT_PIECES = 6 * MOE_STEPS
    EXPERT_TURNS = EXPERT_PIECES // RAW_RING

    with ExitStack() as ctx:
        def sb(name, shape, dt=F32):
            return ctx.enter_context(nc.sbuf_tensor(name, shape, dt))

        def sem(name):
            return ctx.enter_context(nc.semaphore(name))

        raw = sb("raw", [P, RAW_RING, PIECE])
        w_hi = sb("w_hi", [P, SPLIT_RING, PIECE], F32R)
        w_lo = sb("w_lo", [P, SPLIT_RING, PIECE], F32R)
        xt_hi = sb("xt_hi", [P, KT, S], F32R)
        xt_lo = sb("xt_lo", [P, KT, S], F32R)
        ht_hi = sb("ht_hi", [P, 512], F32R)
        ht_lo = sb("ht_lo", [P, 512], F32R)
        pick_t = sb("pick_t", [P, TT * P], F32R)
        y_hi, y_lo = xt_hi[:, :, P:2 * P], xt_lo[:, :, P:2 * P]
        h = sb("h", [P, TT, D])
        row = sb("row", [P, 2, D])
        scratch = sb("scratch", [P, 17408])
        cols = sb("cols", [P, 376])
        ident = sb("ident", [P, P])
        ones = sb("ones", [P, P])
        before = sb("before", [P, P])
        slot_i = scratch[:, 17000:17000 + P].bitcast(I32)
        slot_p = sb("slot_p", [P, 1], I32)
        slot_id = sb("slot_id", [P, P])
        ssq = sb("ssq", [P, TT])
        var = sb("var", [P, HB])
        root = sb("root", [P, HB])
        rstd = sb("rstd", [P, HB])
        newton = sb("newton", [P, 2, HB])
        lb_t = sb("lb_t", [P, 6, KT])
        lb_c = sb("lb_c", [P, 2, KT])
        logits = sb("logits", [P, TT, E])
        top = sb("top", [P, TT, 8])
        top_i = sb("top_i", [P, TT, 8], U32)
        top_f = sb("top_f", [P, TT, 8])
        chosen = sb("chosen", [P, 2, TT, E])
        sel = sb("sel", [P, TT, E])
        weight = sb("weight", [P, 4, TT])
        place = sb("place", [P, TT, E])
        busiest = sb("busiest", [P, 2])
        router = sb("router", [P, KT, E])
        router_hi = sb("router_hi", [P, KT, E], F32R)
        router_lo = sb("router_lo", [P, KT, E], F32R)
        slot_of = sb("slot_of", [P, TT, JOBS + 1])
        gate_of = sb("gate_of", [P, TT, JOBS + 1])
        warm = sb("warm", [P, 16])
        eps = sb("eps", [P, 1])
        tick = sb("tick", [P, 1])
        jobs_n = sb("jobs_n", [P, 1], I32)

        class Cut:
            at = 0

            @classmethod
            def take(cls, n):
                cls.at += n
                assert cls.at <= 17408, cls.at
                return scratch[:, cls.at - n:cls.at]

        Cut.at = 0
        tok = Cut.take(TT * D).rearrange("p (t d) -> p t d", t=TT)
        junk = Cut.take(TT * D)
        Cut.at = 3 * TT * D
        biased = Cut.take(TT * D).rearrange("p (t d) -> p t d", t=TT)
        Cut.at = 0
        conv_u = Cut.take(KT * (S + W - 1)).rearrange("p (k s) -> p k s", k=KT)
        conv_y = Cut.take(KT * S).rearrange("p (k s) -> p k s", k=KT)
        conv_sq = Cut.take(KT * S).rearrange("p (k s) -> p k s", k=KT)
        conv_sig = Cut.take(4 * S).rearrange("p (k s) -> p k s", k=4)
        conv_mean = Cut.take(S)
        conv_var = Cut.take(S)
        conv_r = Cut.take(S)
        conv_t = Cut.take(S)
        diag = Cut.take(W * P).rearrange("p (w c) -> p w c", w=W)
        Cut.at = 2 * TT * D
        act_sb = Cut.take(512)
        hid = Cut.take(512)
        logits_t = hid[0:E, 0:S]
        Cut.at = 0
        hq = Cut.take(HEADS * S)
        hk = Cut.take(HEADS * S)
        hg = Cut.take(HEADS * S)
        lev = [Cut.take(HEADS * S) for _ in range(2)]
        hv = Cut.take(TT * D)
        hog = Cut.take(TT * D)
        s_same = Cut.take(HB * P)
        s_cross = Cut.take(HEADS * P)
        ho = hq.rearrange("p (t d) -> p t d", t=TT)
        hsq = hk
        Cut.at = 0
        mx = Cut.take(TT * D).rearrange("p (t d) -> p t d", t=TT)
        Cut.at += TT * D + 2 * 512
        acc = Cut.take(TT * D).rearrange("p (t d) -> p t d", t=TT)
        pick = Cut.take(TT * P).rearrange("p (t s) -> p t s", t=TT)
        early = Cut.take(EARLY * PIECE).rearrange("p (n c) -> p n c", n=EARLY)
        level_mask = sb("level_mask", [P, len(LEVELS), P], mybir.dt.uint8)
        prow = s_same[:, 0:3 * P].rearrange("p (a b) -> p a b", a=3)

        psum = ctx.enter_context(nc.psum_tensor("psum", [P, 8, BANK], F32))

        LBD = hgrn_lower_bounds.shape[0]
        NG = 0
        B_IN = NG + 8 * KT
        DW_B = B_IN + 2 * KT
        LN_G = DW_B + KT
        LN_B = LN_G + KT
        LB = LN_B + KT
        ROWS0 = LB + LBD * KT
        TAPS = P
        HALF_W = (W + 1) // 2
        PE_CONV = (3, 5, 7)
        DVE_CONV = (0, 1, 2, 4, 6)
        SHARED = 6
        SHARED_TAP = 13
        TAP_JOBS = [(k, range(W)) for k in PE_CONV] + [(SHARED, range(SHARED_TAP, W))]

        def tap_col(w, k):
            a, b = divmod(w, HALF_W)
            return TAPS + a * (HALF_W * KT) + b * KT + k

        def group_bank(n):
            return 4 + 2 * (n % 2)

        EARLY0 = MOE + RAW_RING

        def is_early(p, turns):
            return isinstance(turns, int) and turns == 0 and EARLY0 <= p < EARLY0 + EARLY

        def ring_place(p, turns=0):
            return p if p < MOE or (isinstance(turns, int) and turns == 0) else p - EARLY

        def raw_piece(p, turns=0):
            if is_early(p, turns):
                return early[:, p - EARLY0, :]
            return raw[:, ring_place(p, turns) % RAW_RING, :]

        def norm_no(n, t, pre):
            if n < 0:
                return t
            return TT + 2 * TT * n + (t if n == 3 else 2 * t + pre)

        TURN_BEHIND = (1, 1, 2)

        raw_loaded = [sem(f"raw_loaded{i}") for i in range(RAW_RING)]
        early_loaded = [sem(f"early_loaded{i}") for i in range(EARLY)]
        hi_ready = sem("hi_ready")
        lo_ready = sem("lo_ready")
        piece_used = sem("piece_used")
        x_loaded = [sem(f"x_loaded{t}") for t in range(TT)]
        gains_loaded = sem("gains_loaded")
        rows_loaded = sem("rows_loaded")
        gains_turned = sem("gains_turned")
        gains_ready = sem("gains_ready")
        small_loaded = sem("small_loaded")
        row_loaded = [sem(f"row_loaded{i}") for i in range(2)]
        row_used = [sem(f"row_used{i}") for i in range(2)]
        consts_ready = sem("consts_ready")
        cols_turned = sem("cols_turned")
        cols_ready = sem("cols_ready")
        lb_arg = sem("lb_arg")
        lb_exp = sem("lb_exp")
        dve_step = sem("dve_step")
        squares_ready = sem("squares_ready")
        gained = sem("gained")
        tile_done = sem("tile_done")
        variance_ready = sem("variance_ready")
        conv_root = sem("conv_root")
        head_root = sem("head_root")
        root_ready = sem("root_ready")
        normed = sem("normed")
        turned = sem("turned")
        turn_hi = sem("turn_hi")
        turn_lo = sem("turn_lo")
        source_ready = sem("source_ready")
        residual_ready = sem("residual_ready")
        glu_sig = sem("glu_sig")
        glu_out = sem("glu_out")
        conv_done = sem("conv_done")
        mean_sum = sem("mean_sum")
        centred = sem("centred")
        conv_squared = sem("conv_squared")
        var_sum = sem("var_sum")
        conv_scaled = sem("conv_scaled")
        conv_act = sem("conv_act")
        conv_hi = sem("conv_hi")
        conv_lo = sem("conv_lo")
        tap_added = sem("tap_added")
        diag_ready = sem("diag_ready")
        diag_used = sem("diag_used")
        tensor_conv_done = sem("tensor_conv_done")
        ffn_silu = sem("ffn_silu")
        ffn_hid = sem("ffn_hid")
        ffn_turned = sem("ffn_turned")
        ffn_ht_hi = sem("ffn_ht_hi")
        ffn_ht_lo = sem("ffn_ht_lo")
        qf_sig = sem("qf_sig")
        q_ready = sem("q_ready")
        forget_ready = sem("forget_ready")
        k_ready = sem("k_ready")
        log_ready = sem("log_ready")
        level_arg = sem("level_arg")
        level_exp = sem("level_exp")
        level_factors = sem("level_factors")
        level_scores = sem("level_scores")
        level_taken = sem("level_taken")
        vg_out = sem("vg_out")
        o_proj = sem("o_proj")
        o_squared = sem("o_squared")
        og_ready = sem("og_ready")
        router_split = sem("router_split")
        router_hi_ready = sem("router_hi_ready")
        logits_done = sem("logits_done")
        logits_moved = sem("logits_moved")
        logits_turned = sem("logits_turned")
        sel_ready = sem("sel_ready")
        count_done = sem("count_done")
        gate_arg = sem("gate_arg")
        gate_exp = sem("gate_exp")
        tables_ready = sem("tables_ready")
        pick_ready = sem("pick_ready")
        gathered = sem("gathered")
        pick_turned = sem("pick_turned")
        pick_t_ready = sem("pick_t_ready")
        xg_hi = sem("xg_hi")
        xg_lo = sem("xg_lo")
        moe_silu = sem("moe_silu")
        moe_hid = sem("moe_hid")
        moe_turned = sem("moe_turned")
        moe_ht_hi = sem("moe_ht_hi")
        moe_ht_lo = sem("moe_ht_lo")
        y_rounded = sem("y_rounded")
        y_ready = sem("y_ready")
        scattered = sem("scattered")
        acc_added = sem("acc_added")
        moe_done = sem("moe_done")
        out_stored = sem("out_stored")

        block = ctx.enter_context(nc.Block())

        def bank(i, n=1):
            return psum[:, i:i + n, :].rearrange("p b c -> p (b c)")

        @block.sync
        def _(sp):
            def load(p, parts, turns=0, lag=RAW_RING):
                if p >= RAW_RING and not is_early(p, turns):
                    sp.wait_ge(lo_ready, turns * RAW_RING + (p - lag + 1))
                for dst, src in parts:
                    loaded = (early_loaded[p - EARLY0] if is_early(p, turns)
                              else raw_loaded[ring_place(p, turns) % RAW_RING])
                    sp.dma_start(dst, src).then_inc(loaded, 32 // len(parts))

            def by_channel(dst, w, k0, c0, c1=None):
                r = w.rearrange("(k p) n -> p k n", p=P)[:, k0:k0 + 4, :]
                d = dst.rearrange("p (k n) -> p k n", k=4)
                if c1 is None:
                    return [(d, r[:, :, bass.ds(c0, 512)])]
                return [(d[:, :, 0:256], r[:, :, bass.ds(c0, 256)]), (d[:, :, 256:512], r[:, :, bass.ds(c1, 256)])]

            def by_row(dst, w, r0):
                d = dst.rearrange("p (k n) -> p k n", k=2)
                return [(d, w[bass.ds(r0, 2 * P), :].rearrange("(k p) n -> p k n", p=P))]

            for t in range(TT):
                sp.dma_start(h[:, t, :], x[0, t * P:(t + 1) * P, :]).then_inc(x_loaded[t], 16)
                if t == 0:
                    sp.dma_start(prow[0:B_IN, 0, :], norm_g.rearrange("l n (k c) -> (l n k) c", c=P)).then_inc(
                        gains_loaded, 16)
            w = conv_w_in[0]
            order = [(c, kh) for c in range(4) for kh in range(2)]
            pieces = [by_channel(raw_piece(CONV_IN + n), w, 4 * kh, 256 * c, D + 256 * c)
                      for n, (c, kh) in enumerate(order)]
            load(0, pieces[0])
            for a, b, src in (
                (B_IN, DW_B, conv_b_in.rearrange("l (k c) -> (l k) c", c=P)),
                (DW_B, LN_G, conv_dw_b.rearrange("l (k c) -> (l k) c", c=P)),
                (LN_G, LN_B, conv_ln_g.rearrange("l (k c) -> (l k) c", c=P)),
                (LN_B, LB, conv_ln_b.rearrange("l (k c) -> (l k) c", c=P)),
                (LB, ROWS0, hgrn_lower_bounds.rearrange("l (k c) -> (l k) c", c=P)),
            ):
                sp.dma_start(prow[a:b, 0, :], src).then_inc(rows_loaded, 16)
            taps = conv_dw_w[0].rearrange("w (k c) -> (w k) c", c=P)
            sp.dma_start(prow[0:HALF_W * KT, 1, :], taps[0:HALF_W * KT, :]).then_inc(rows_loaded, 16)
            sp.dma_start(prow[0:(W - HALF_W) * KT, 2, :], taps[HALF_W * KT:W * KT, :]).then_inc(rows_loaded, 16)
            for p in range(1, CONV_OUT):
                load(p, pieces[p])
            for n in range(4):
                load(CONV_OUT + n, by_row(raw_piece(CONV_OUT + n), conv_w_out[0], 256 * n))
            gu, dn = ffn_w_gu[0], ffn_w_down[0]
            for kh in range(2):
                load(FFN0 + kh, by_channel(raw_piece(FFN0 + kh), gu, 4 * kh, 0, FFN))
            with sp.Fori(0, FFN_STEPS // 2) as i:
                for j in range(2):
                    p = FFN0 + 2 + 3 * j
                    col = (i * 2 + (1 + j)) * FFN_CHUNK
                    for kh in range(2):
                        load(p + kh, by_channel(raw_piece(p + kh), gu, 4 * kh, col, col + FFN), i)
                    load(p + 2, by_row(raw_piece(p + 2), dn, (i * 2 + j) * FFN_CHUNK), i)
            p = HGRN_QF - 1
            load(p, by_row(raw_piece(p), dn, (FFN_STEPS - 1) * FFN_CHUNK))
            w = hgrn_w_in[0]
            for n, (c, kh) in enumerate(order):
                load(HGRN_QF + n, by_channel(raw_piece(HGRN_QF + n), w, 4 * kh, 256 * c, D + 256 * c))
            for n, (c, kh) in enumerate(order):
                load(HGRN_VG + n, by_channel(raw_piece(HGRN_VG + n), w, 4 * kh, 2 * D + 512 * c))
            for n in range(4):
                load(HGRN_OUT + n, by_row(raw_piece(HGRN_OUT + n), hgrn_w_out[0], 256 * n))

            def expert(e, turns, first=False):
                gu, dn = moe_w_gu[0][e, :, :], moe_w_down[0][e, :, :]
                for g in range(2):
                    for kh in range(2):
                        p = MOE + 2 * g + kh
                        load(p, by_channel(raw_piece(p, turns), gu, 4 * kh, g * ED), turns)

                def step(c, t, lag=RAW_RING):
                    for g in range(2):
                        for kh in range(2):
                            p = MOE + 4 + 2 * g + kh
                            if is_early(p, t) and p == EARLY0:
                                sp.wait_ge(normed, 4 * TT)
                            load(p, by_channel(raw_piece(p, t), gu, 4 * kh, c * MOE_CHUNK + g * ED), t, lag)
                    for n in range(2):
                        p = MOE + 8 + n
                        load(p, by_row(raw_piece(p, t), dn, (c - 1) * MOE_CHUNK + 256 * n), t, lag)

                if first:
                    step(1, 0)
                    step(2, 1, RAW_RING + EARLY)
                with sp.Fori(3 if first else 1, MOE_STEPS) as c:
                    step(c, turns + (c - 1))
                for n in range(2):
                    p, t = MOE + 4 + n, turns + (MOE_STEPS - 1)
                    load(p, by_row(raw_piece(p, t), dn, (MOE_STEPS - 1) * MOE_CHUNK + 256 * n), t)

            expert(0, 0, True)
            with sp.Fori(1, E) as e:
                expert(e, e * EXPERT_TURNS)
            sp.wait_ge(tables_ready, 1)
            jobs = sp.value_load(jobs_n[0:1, 0:1], min_val=E, max_val=JOBS)
            with sp.If(jobs > E):
                with sp.Fori(0, E) as e:
                    expert(e, (e + E) * EXPERT_TURNS)
            for t in range(TT):
                sp.wait_ge(residual_ready, 3 * TT + t + 1)
                sp.dma_start(out[0, t * P:(t + 1) * P, :], h[:, t, :]).then_inc(out_stored, 16)
            sp.wait_ge(out_stored, TT * 16)

        @block.gpsimd
        def _(pool):
            nc.gpsimd.memset(eps[:], EPS)
            nc.gpsimd.memset(ones[:], 1.0).then_inc(consts_ready, 1)
            nc.gpsimd.iota(slot_i, pattern=[[1, P]], base=0, channel_multiplier=0)
            nc.gpsimd.iota(slot_p[:], pattern=[[0, 1]], base=0, channel_multiplier=1).then_inc(consts_ready, 1)
            pool.wait_ge(consts_ready, 2)
            nc.gpsimd.affine_select(out=ident[:], in_=ones[:], compare_op=ALU.is_equal, fill=0.0, base=0,
                                    pattern=[[-1, P]], channel_multiplier=1).then_inc(consts_ready, 1)
            nc.gpsimd.affine_select(out=before[:], in_=ones[:], compare_op=ALU.is_gt, fill=0.0, base=0,
                                    pattern=[[1, P]], channel_multiplier=-1).then_inc(consts_ready, 1)

            def load_row(i, src, n):
                if n:
                    pool.wait_ge(row_used[i], n)
                pool.dma_start(row[:, i, 0:src.shape[-1]], src.partition_broadcast(P)).then_inc(row_loaded[i], 16)

            load_row(0, conv_b_out[0], 0)
            load_row(1, norm_g[0, 1], 0)
            pool.dma_start(router[:], moe_router[0].rearrange("(k p) e -> p k e", p=P)).then_inc(small_loaded, 16)
            load_row(0, hgrn_norm_g[0], 1)
            load_row(1, norm_g[0, 3], 1)
            load_row(1, norm_g[1, 1], 2)
            load_row(0, norm_g[1, 2], 2)
            load_row(1, norm_g[1, 3], 3)

        @block.tensor
        def _(pe):
            mm = nc.tensor.matmul

            def keep_clock(b, n):
                for _ in range(n):
                    mm(psum[:, b, 0:P], ones[:], before[:], start=True, stop=True)

            def wait_hi(p, turns=0):
                pe.wait_ge(hi_ready, turns * RAW_RING + (p + 1))

            def wait_lo(p, turns=0):
                pe.wait_ge(lo_ready, turns * RAW_RING + (p + 1))

            def turn(n, t, src):
                pe.wait_ge(normed, TT * n + t + 1)
                for k in range(KT):
                    last = nc.tensor.transpose(psum[:, 2 * t + k // 4, (k % 4) * P:(k % 4 + 1) * P],
                                               src[:, t, k * P:(k + 1) * P], ident[:])
                    if k % 4 == 3:
                        last.then_inc(turned, 1)

            def tile_turned(n, t):
                pe.wait_ge(turn_lo, 4 * n + 2 * t + 2)

            def channel_out(p, kh, banks):
                for part, rhss in ((w_hi, (xt_hi, xt_lo)), (w_lo, (xt_hi,))):
                    (wait_hi if part is w_hi else wait_lo)(p)
                    wv = part[:, p % SPLIT_RING, :].rearrange("p (k n) -> p k n", k=4)
                    for kk in range(4):
                        for b in range(4):
                            for rhs in rhss:
                                first = kh == 0 and kk == 0 and b % 2 == 0 and part is w_hi and rhs is xt_hi
                                last = mm(psum[:, banks + b // 2, (b % 2) * S:(b % 2 + 1) * S],
                                          wv[:, kk, b * P:(b + 1) * P], rhs[:, 4 * kh + kk, :],
                                          start=first, stop=kh == 1 and kk == 3 and part is w_lo,
                                          skip_group_check=True)
                last.then_inc(piece_used, 1)

            def token_cols(p, kh, banks, tiles, turns=0, signal=piece_used):
                for part, lhss in ((w_hi, (xt_hi, xt_lo)), (w_lo, (xt_hi,))):
                    (wait_hi if part is w_hi else wait_lo)(p, turns)
                    wv = part[:, p % SPLIT_RING, :].rearrange("p (k n) -> p k n", k=4)
                    for kk in range(4):
                        for t in tiles:
                            for lhs in lhss:
                                last = mm(psum[:, banks[t], :], lhs[:, 4 * kh + kk, t * P:(t + 1) * P], wv[:, kk, :],
                                          start=kh == 0 and kk == 0 and part is w_hi and lhs is xt_hi,
                                          stop=kh == 1 and kk == 3 and part is w_lo)
                if signal is not None:
                    last.then_inc(signal, 1)

            def token_rows(p, operands, banks, tiles, first, final, turns=0, signal=piece_used):
                for part in (w_hi, w_lo):
                    (wait_hi if part is w_hi else wait_lo)(p, turns)
                    wv = part[:, p % SPLIT_RING, :].rearrange("p (k n) -> p k n", k=2)
                    for kk in range(2):
                        for t in tiles:
                            for i, lhs in enumerate(operands(kk, t)[:2 if part is w_hi else 1]):
                                for half in range(2):
                                    last = mm(psum[:, banks + 2 * t + half, :], lhs,
                                              wv[:, kk, half * BANK:(half + 1) * BANK],
                                              start=first and kk == 0 and part is w_hi and i == 0,
                                              stop=final and kk == 1 and part is w_lo)
                if signal is not None:
                    last.then_inc(signal, 1)

            both = tuple(range(TT))

            def last_rows(p0, n0, count):
                for t in both:
                    for n in range(count):
                        done = piece_used if t else (tile_done if n == count - 1 else None)
                        token_rows(p0 + n0 + n, from_xt(2 * (n0 + n)), 4, (t,), False, n == count - 1, signal=done)

            def from_xt(k0):
                return lambda k, t: (xt_hi[:, k0 + k, t * P:(t + 1) * P], xt_lo[:, k0 + k, t * P:(t + 1) * P])

            def conv_taps(i):
                k, taps = TAP_JOBS[i]
                pe.wait_ge(glu_out, k // 2 + 1)
                if i >= 2:
                    pe.wait_ge(tensor_conv_done, i - 1)
                for n, w in enumerate(taps):
                    pe.wait_ge(diag_ready, W * i + n + 1)
                    mm(psum[:, 6 + i % 2, 0:S], diag[:, w, :], conv_u[:, k, w:w + S],
                       start=n == 0, stop=w == W - 1).then_inc(diag_used, 1)

            def channel_sum(k):
                if k in PE_CONV:
                    pe.wait_ge(tensor_conv_done, PE_CONV.index(k) + 1)
                else:
                    pe.wait_ge(conv_done, DVE_CONV.index(k) + 1)
                return mm(psum[:, 4, 0:S], ones[:], conv_y[:, k, :], start=k == 0, stop=k == KT - 1)

            pe.wait_ge(consts_ready, 4)
            keep_clock(5, 6)
            pe.wait_ge(gains_loaded, 16)
            nc.tensor.transpose(psum[:, 4, 0:B_IN], prow[0:B_IN, 0, :], ident[0:B_IN, 0:B_IN]).then_inc(
                gains_turned, 1)
            for t in both:
                turn(0, t, tok)

            def turn_rows():
                pe.wait_ge(rows_loaded, 7 * 16)
                n = (W - HALF_W) * KT
                nc.tensor.transpose(psum[:, 5, 0:ROWS0], prow[0:ROWS0, 0, :], ident[0:ROWS0, 0:ROWS0])
                nc.tensor.transpose(psum[:, 5, P:P + HALF_W * KT], prow[0:HALF_W * KT, 1, :],
                                    ident[0:HALF_W * KT, 0:HALF_W * KT])
                nc.tensor.transpose(psum[:, 5, P + HALF_W * KT:P + HALF_W * KT + n], prow[0:n, 2, :],
                                    ident[0:n, 0:n]).then_inc(cols_turned, 1)

            for c in range(4):
                if c >= 2:
                    pe.wait_ge(glu_out, c - 1)
                for kh in range(2):
                    if c == 0:
                        if kh == 0:
                            keep_clock(5, 18)
                        tile_turned(0, 1)
                    channel_out(CONV_IN + 2 * c + kh, kh, 2 * (c % 2))
                    if c == 0 and kh == 0:
                        turn_rows()
                if c == 2:
                    conv_taps(0)
            conv_taps(1)
            for k in range(4):
                channel_sum(k)
            conv_taps(2)
            conv_taps(3)
            for k in range(4, KT):
                if k == 6:
                    keep_clock(0, 8)
                last = channel_sum(k)
            last.then_inc(mean_sum, 1)
            for k in range(KT):
                pe.wait_ge(conv_squared, k + 1)
                last = mm(psum[:, 5, 0:S], ones[:], conv_sq[:, k, :], start=k == 0, stop=k == KT - 1)
            last.then_inc(var_sum, 1)
            keep_clock(0, 28)
            for n in range(2):
                pe.wait_ge(conv_lo, n + 1)
                token_rows(CONV_OUT + n, from_xt(2 * n), 4, both, n == 0, False)
            pe.wait_ge(conv_lo, 4)
            last_rows(CONV_OUT, 2, 2)

            def ffn_turn(c):
                pe.wait_ge(ffn_hid, c + 1)
                for k in range(2):
                    for t in range(TT):
                        last = nc.tensor.transpose(psum[:, 2, k * S + t * P:k * S + (t + 1) * P],
                                                   hid[:, t * 256 + k * P:t * 256 + (k + 1) * P], ident[:])
                last.then_inc(ffn_turned, 1)

            def ffn_hidden(k, t):
                return ht_hi[:, k * S + t * P:k * S + (t + 1) * P], ht_lo[:, k * S + t * P:k * S + (t + 1) * P]

            def ffn_step(j, c, i, opens=False):
                p = FFN0 + 2 + 3 * j
                pe.wait_ge(ffn_hid, c + 1)
                token_cols(p, 0, (0, 1), both, i)
                ffn_turn(c)
                token_cols(p + 1, 1, (0, 1), both, i)
                pe.wait_ge(ffn_ht_lo, c + 1)
                token_rows(p + 2, ffn_hidden, 4, both, opens, False, i)

            keep_clock(3, 14)
            turn(1, 0, tok)
            keep_clock(3, 14)
            tile_turned(1, 0)
            token_cols(FFN0, 0, (0, 1), (0,), signal=None)
            turn(1, 1, tok)
            token_cols(FFN0 + 1, 1, (0, 1), (0,), signal=None)
            tile_turned(1, 1)
            for kh in range(2):
                token_cols(FFN0 + kh, kh, (0, 1), (1,))
            for j in range(2):
                ffn_step(j, j, 0, j == 0)
            with pe.Fori(1, FFN_STEPS // 2) as i:
                for j in range(2):
                    ffn_step(j, i * 2 + j, i)
            ffn_turn(FFN_STEPS - 1)
            pe.wait_ge(ffn_ht_lo, FFN_STEPS)
            for t in both:
                token_rows(HGRN_QF - 1, ffn_hidden, 4, (t,), False, True, signal=piece_used if t else tile_done)

            for t in both:
                keep_clock(3, 18)
                turn(2, t, tok)
            keep_clock(4, 9)
            tile_turned(2, 1)
            for c in range(4):
                if c >= 2:
                    pe.wait_ge(q_ready, c - 1)
                for kh in range(2):
                    channel_out(HGRN_QF + 2 * c + kh, kh, 2 * (c % 2))

            def scores(n):
                f = lev[n % 2]
                if n == 0:
                    pe.wait_ge(k_ready, 4)
                    pe.wait_ge(q_ready, 4)
                else:
                    pe.wait_ge(level_factors, n)
                    pe.wait_ge(level_taken, max(n - 1, 1))
                for b in range(HEADS if n == len(LEVELS) + 1 else HB):
                    if n == 0:
                        out_b, keys, queries = psum[:, 4 + b // 4, (b % 4) * P:(b % 4 + 1) * P], hk, hq
                        queries = queries[:, b * P:(b + 1) * P]
                        keys = keys[:, b * P:(b + 1) * P]
                    elif n == len(LEVELS) + 1:
                        out_b = psum[:, group_bank(n) + b // 4, (b % 4) * P:(b % 4 + 1) * P]
                        keys, queries = f[:, 2 * b * P:(2 * b + 1) * P], f[:, (2 * b + 1) * P:(2 * b + 2) * P]
                    else:
                        out_b = psum[:, group_bank(n) + b // 8, (b % 8) * (P // 2):(b % 8 + 1) * (P // 2)]
                        keys = f[:, b * P:(b + 1) * P]
                        queries = keys.rearrange("p (x two l) -> p x two l", two=2, l=LEVELS[n - 1])[:, :, 1, :]
                        out_b = out_b.rearrange("p (x l) -> p x l", l=LEVELS[n - 1])
                    last = mm(out_b, keys, queries, start=True, stop=True)
                last.then_inc(level_scores, 1)

            pe.wait_ge(q_ready, 3)
            for n in range(8):
                c, kh = divmod(n, 2)
                if n == 2:
                    pe.wait_ge(q_ready, 4)
                if c >= 2:
                    pe.wait_ge(vg_out, c - 1)
                token_cols(HGRN_VG + n, kh, (2 * (c % 2), 2 * (c % 2) + 1), both)
                if n:
                    scores(n - 1)
            scores(len(LEVELS))
            scores(len(LEVELS) + 1)
            pe.wait_ge(level_taken, len(LEVELS) + 2)
            pe.wait_ge(vg_out, 4)
            for t in range(TT):
                for hd in range(HEADS):
                    o = psum[:, 4 + 2 * t + hd // 4, (hd % 4) * P:(hd % 4 + 1) * P]
                    b = (hd * TT + t) * P
                    if t:
                        mm(o, s_cross[:, hd * P:(hd + 1) * P], hv[:, hd * P:(hd + 1) * P], start=True, stop=False)
                    last = mm(o, s_same[:, b:b + P], hv[:, t * D + hd * P:t * D + (hd + 1) * P],
                              start=t == 0, stop=True)
                last.then_inc(o_proj, 1)
            keep_clock(3, 12)
            turn(3, 0, ho)
            keep_clock(3, 8)
            tile_turned(3, 0)
            token_rows(HGRN_OUT, from_xt(0), 4, (0,), True, False, signal=None)
            turn(3, 1, ho)
            token_rows(HGRN_OUT + 1, from_xt(2), 4, (0,), False, False, signal=None)
            tile_turned(3, 1)
            for n in range(2):
                token_rows(HGRN_OUT + n, from_xt(2 * n), 4, (1,), n == 0, False)
            last_rows(HGRN_OUT, 2, 2)

            for t in both:
                keep_clock(3, (10, 18)[t])
                turn(4, t, mx)
            keep_clock(5, 12)
            pe.wait_ge(router_split, 1)
            tile_turned(4, 1)
            ops = ((router_hi, xt_hi), (router_hi, xt_lo), (router_lo, xt_hi))
            for i, (a, b) in enumerate(ops):
                for k in range(KT):
                    last = mm(psum[0:E, 7, 0:S], a[:, k, :], b[:, k, :], start=i == 0 and k == 0,
                              stop=i == 2 and k == KT - 1)
            last.then_inc(logits_done, 1)
            pe.wait_ge(logits_moved, 1)
            for t in both:
                last = nc.tensor.transpose(psum[:, 7, S + t * E:S + (t + 1) * E], logits_t[:, t * P:(t + 1) * P],
                                           ident[0:E, 0:E])
            last.then_inc(logits_turned, 1)
            keep_clock(5, 9)
            pe.wait_ge(sel_ready, 1)
            mm(psum[:, 6, 0:E], before[:], sel[:, 0, :], start=True, stop=True)
            mm(psum[:, 6, E:2 * E], before[:], sel[:, 1, :], start=True, stop=False)
            mm(psum[:, 6, E:2 * E], ones[:], sel[:, 0, :], start=False, stop=True)
            mm(psum[:, 6, 2 * E:3 * E], ones[:], sel[:, 0, :], start=True, stop=False)
            mm(psum[:, 6, 2 * E:3 * E], ones[:], sel[:, 1, :], start=False, stop=True).then_inc(count_done, 1)

            keep_clock(5, 7)
            pe.wait_ge(tables_ready, 1)
            jobs = pe.value_load(jobs_n[0:1, 0:1], min_val=E, max_val=JOBS)

            def moe_turn(n):
                pe.wait_ge(moe_hid, n + 2)
                for k in range(4):
                    last = nc.tensor.transpose(psum[:, 2, k * P:(k + 1) * P], hid[:, k * P:(k + 1) * P], ident[:])
                last.then_inc(moe_turned, 1)

            def slot_hidden(k0):
                return lambda k, t: (ht_hi[:, (k0 + k) * P:(k0 + k + 1) * P],
                                     ht_lo[:, (k0 + k) * P:(k0 + k + 1) * P])

            def moe_step(n, turns, opens=False):
                pe.wait_ge(moe_silu, n + 1)
                for kh in range(2):
                    token_cols(MOE + 4 + kh, kh, (0,), (0,), turns)
                moe_turn(n)
                for kh in range(2):
                    token_cols(MOE + 6 + kh, kh, (1,), (0,), turns)
                pe.wait_ge(moe_ht_lo, n + 1)
                for kk in range(2):
                    token_rows(MOE + 8 + kk, slot_hidden(2 * kk), 5, (0,), opens and kk == 0, False, turns)

            def gather(j):
                pe.wait_ge(pick_ready, j + 1)
                for k in range(KT):
                    for t in range(TT):
                        last = mm(psum[:, 3 + k // 4, (k % 4) * P:(k % 4 + 1) * P], mx[:, t, k * P:(k + 1) * P],
                                  pick[:, t, :], start=t == 0, stop=t == TT - 1)
                    if k % 4 == 3:
                        last.then_inc(gathered, 1)

            def scatter(j):
                pe.wait_ge(y_ready, j + 1)
                pe.wait_ge(pick_t_ready, j + 1)
                for t in range(TT):
                    for half in range(2):
                        four = slice(4 * half, 4 * half + 4)
                        dst = bank(SCATTER_BANKS[2 * t + half]).rearrange("p (k s) -> p k s", k=4)
                        token = pick_t[:, t * P:(t + 1) * P]
                        mm(dst, token, y_hi[:, four, :], start=True, stop=False)
                        mm(dst, token, y_lo[:, four, :], start=False, stop=True).then_inc(scattered, 1)

            gather(0)
            with pe.Fori(0, jobs) as j:
                turns = j * EXPERT_TURNS
                pe.wait_ge(xg_lo, j * 2 + 2)
                for kh in range(2):
                    token_cols(MOE + kh, kh, (0,), (0,), turns)
                scatter(j)
                for kh in range(2):
                    token_cols(MOE + 2 + kh, kh, (1,), (0,), turns)
                pe.wait_ge(acc_added, j * 4 + 5)
                for t in range(TT):
                    last = nc.tensor.transpose(psum[:, 7, t * P:(t + 1) * P], pick[:, t, :], ident[:])
                last.then_inc(pick_turned, 1)
                moe_step(j * MOE_STEPS, turns, True)
                with pe.Fori(1, MOE_STEPS - 1) as c:
                    moe_step(j * MOE_STEPS + c, turns + c)
                n = j * MOE_STEPS + (MOE_STEPS - 1)
                moe_turn(n)
                gather(j + 1)
                pe.wait_ge(moe_ht_lo, n + 1)
                for kk in range(2):
                    token_rows(MOE + 4 + kk, slot_hidden(2 * kk), 5, (0,), False, kk == 1, turns + (MOE_STEPS - 1))
            pe.wait_ge(xg_lo, jobs * 2 + 2)
            scatter(jobs)

        @block.scalar
        def _(act):
            fn = nc.scalar.activation
            warmed = [0]

            def hi(p, turns=0):
                if is_early(p, turns):
                    act.wait_ge(early_loaded[p - EARLY0], 32)
                else:
                    slot_turn, slot = divmod(ring_place(p, turns), RAW_RING)
                    act.wait_ge(raw_loaded[slot], turns * 32 + 32 * (slot_turn + 1))
                if p >= SPLIT_RING:
                    act.wait_ge(piece_used, turns * RAW_RING + (p - SPLIT_RING + 1))
                fn(w_hi[:, p % SPLIT_RING, :], raw_piece(p, turns), ACT.Copy).then_inc(hi_ready, 1)

            def load_table(func):
                fn(warm[:, warmed[0]:warmed[0] + 1], ones[:, 0:1], func)
                warmed[0] += 1

            def squares(t, src):
                fn(junk[:, t * D:(t + 1) * D], src, ACT.Square, accum_out=ssq[:, t:t + 1]).then_inc(squares_ready, 1)

            def row_root(n, t, pre):
                act.wait_ge(squares_ready, norm_no(n, t, pre) + 1)
                fn(root[:, t:t + 1], ssq[:, t:t + 1], ACT.Sqrt, scale=1.0 / D, bias=eps[:]).then_inc(root_ready, 1)

            def norm_roots(n, source, gain=None):
                for t in range(TT):
                    if n == 0:
                        act.wait_ge(source_ready, t + 1)
                    elif n < 3:
                        act.wait_ge(tile_done, n + 1) if t == 0 else used((0, HGRN_QF - 1, MOE - 1)[n])
                    squares(t, source(t))
                    row_root(n, t, 0)
                    if n < 3:
                        if t:
                            turn_hi_part(n + TURN_BEHIND[n], 0, gain)
                        act.wait_ge(residual_ready, TT * n + t + 1)
                        squares(t, h[:, t, :])
                        row_root(n, t, 1)

            def turn_hi_part(n, t, gain):
                for kh in range(2):
                    act.wait_ge(turned, 4 * n + 2 * t + kh + 1)
                    tokens = slice(t * P, (t + 1) * P)
                    if gain is None:
                        fn(xt_hi[:, 4 * kh:4 * kh + 4, tokens], bank(2 * t + kh).rearrange("p (k s) -> p k s", k=4),
                           ACT.Copy).then_inc(turn_hi, 4)
                    else:
                        for k in range(4 * kh, 4 * kh + 4):
                            fn(xt_hi[:, k, tokens], psum[:, 2 * t + kh, (k % 4) * P:(k % 4 + 1) * P], ACT.Copy,
                               scale=cols[:, gain + k:gain + k + 1]).then_inc(turn_hi, 1)

            def used(p):
                act.wait_ge(piece_used, p + 1)

            act.wait_ge(consts_ready, 4)
            load_table(ACT.Sqrt)
            for t in range(TT):
                act.wait_ge(x_loaded[t], 16)
                squares(t, h[:, t, :])
                row_root(-1, t, 1)
            act.wait_ge(gains_ready, 1)
            turn_hi_part(0, 0, NG)
            hi(0)
            turn_hi_part(0, 1, NG)
            for p in range(1, 3):
                hi(p)
            act.wait_ge(cols_ready, 1)
            load_table(ACT.Sigmoid)

            def build_diag(i, taps=range(W)):
                for w in taps:
                    if i:
                        act.wait_ge(diag_used, W * (i - 1) + w + 1)
                    col = tap_col(w, TAP_JOBS[i][0])
                    fn(diag[:, w, :], ident[:], ACT.Copy, scale=cols[:, col:col + 1]).then_inc(diag_ready, 1)

            def gate_sigmoid(c):
                used(2 * c + 1)
                if c >= 2:
                    act.wait_ge(glu_out, c - 1)
                for b in range(2):
                    k = 2 * c + b
                    fn(conv_sig[:, 2 * (c % 2) + b, :], psum[:, 2 * (c % 2) + 1, b * S:(b + 1) * S], ACT.Sigmoid,
                       bias=cols[:, B_IN + KT + k:B_IN + KT + k + 1]).then_inc(glu_sig, 1)

            def take_conv(i):
                k = PE_CONV[i]
                act.wait_ge(diag_used, W * (i + 1))
                fn(conv_y[:, k, :], psum[:, 6 + i % 2, 0:S], ACT.Identity,
                   bias=cols[:, DW_B + k:DW_B + k + 1]).then_inc(tensor_conv_done, 1)

            hi(3)
            gate_sigmoid(0)
            hi(4)
            build_diag(0, range(0, 8))
            hi(5)
            build_diag(0, range(8, 20))
            gate_sigmoid(1)
            hi(6)
            build_diag(0, range(20, W))
            hi(7)
            gate_sigmoid(2)
            hi(8)
            build_diag(1)
            take_conv(0)
            hi(9)
            gate_sigmoid(3)
            hi(10)
            build_diag(2)
            take_conv(1)
            build_diag(3, TAP_JOBS[3][1])
            take_conv(2)
            for k in range(KT):
                act.wait_ge(centred, k + 1)
                fn(conv_sq[:, k, :], conv_y[:, k, :], ACT.Square).then_inc(conv_squared, 1)
            load_table(ACT.Sqrt)
            act.wait_ge(variance_ready, 1)
            fn(conv_t, conv_var, ACT.Sqrt).then_inc(conv_root, 1)
            load_table(ACT.Silu)
            for k in range(KT):
                act.wait_ge(conv_scaled, k + 1)
                fn(conv_sq[:, k, :], conv_y[:, k, :], ACT.Silu, scale=cols[:, LN_G + k:LN_G + k + 1],
                   bias=cols[:, LN_B + k:LN_B + k + 1]).then_inc(conv_act, 1)
                if k % 2:
                    act.wait_ge(conv_act, k + 1)
                    fn(xt_hi[:, k - 1:k + 1, :], conv_sq[:, k - 1:k + 1, :], ACT.Copy).then_inc(conv_hi, 1)
            act.wait_ge(lb_arg, 1)
            fn(lb_t[:, 2:4, :], lb_t[:, 0:2, :], ACT.Exp).then_inc(lb_exp, 1)
            hi(CONV_OUT + 3)
            hi(FFN0)
            load_table(ACT.Sqrt)
            norm_roots(0, lambda t: biased[:, t, :], NG + 2 * KT)
            hi(FFN0 + 1)
            turn_hi_part(1, 1, NG + 2 * KT)
            load_table(ACT.Silu)

            def ffn_act():
                fn(act_sb.rearrange("p (t n) -> p t n", t=TT), psum[:, 0:TT, 0:FFN_CHUNK], ACT.Silu).then_inc(
                    ffn_silu, 1)

            def ffn_round(c):
                act.wait_ge(ffn_turned, c + 1)
                fn(ht_hi[:], bank(2), ACT.Copy).then_inc(ffn_ht_hi, 1)

            with act.Fori(0, FFN_STEPS // 2) as i:
                for j in range(2):
                    p = FFN0 + 2 + 3 * j
                    c = i * 2 + j
                    hi(p, i)
                    act.wait_ge(piece_used, i * RAW_RING + (p - 1))
                    act.wait_ge(piece_used, FFN0 + 2)
                    ffn_act()
                    hi(p + 1, i)
                    hi(p + 2, i)
                    ffn_round(c)
            hi(HGRN_QF - 1)
            used(HGRN_QF - 3)
            ffn_act()
            hi(HGRN_QF)
            ffn_round(FFN_STEPS - 1)
            hi(HGRN_QF + 1)
            load_table(ACT.Sqrt)
            norm_roots(1, lambda t: bank(4 + 2 * t, 2), NG + 4 * KT)
            turn_hi_part(2, 1, NG + 4 * KT)
            load_table(ACT.Sigmoid)
            hi(HGRN_QF + 2)
            hi(HGRN_QF + 3)
            for c in range(4):
                used(HGRN_QF + 2 * c + 1)
                fn(hk[:, c * 512:(c + 1) * 512], bank(2 * (c % 2) + 1), ACT.Sigmoid).then_inc(qf_sig, 1)
                fn(hq[:, c * 512:(c + 1) * 512], bank(2 * (c % 2)), ACT.Sigmoid).then_inc(qf_sig, 1)
                for p in (HGRN_QF + 4 + 2 * c, HGRN_QF + 5 + 2 * c)[:2 * (c < 3)]:
                    hi(p)
            load_table(ACT.Ln)
            for c, part in enumerate((slice(0, 1536), slice(1536, 2048))):
                act.wait_ge(k_ready, 3 + c)
                fn(lev[0][:, part], lev[0][:, part], ACT.Ln).then_inc(log_ready, 1)
            load_table(ACT.Exp)
            hi(HGRN_VG + 2)

            def level(n):
                act.wait_ge(level_arg, n)
                fn(lev[n % 2], lev[n % 2], ACT.Exp).then_inc(level_exp, 1)

            level(1)
            for n in range(1, 8):
                if HGRN_VG + 2 + n < HGRN_OUT:
                    hi(HGRN_VG + 2 + n)
                level(n + 1)
                if n % 2:
                    c = n // 2
                    used(HGRN_VG + 2 * c + 1)
                    dst = (hv if c < 2 else hog).rearrange("p (t d) -> p t d", t=TT)
                    fn(dst[:, :, (c % 2) * 512:(c % 2 + 1) * 512], psum[:, 2 * (c % 2):2 * (c % 2) + 2, :],
                       ACT.Copy).then_inc(vg_out, 1)
            act.wait_ge(vg_out, 4)
            fn(hog, hog, ACT.Silu).then_inc(og_ready, 1)
            hi(HGRN_OUT)
            hi(HGRN_OUT + 1)
            load_table(ACT.Sqrt)
            for t in range(TT):
                act.wait_ge(o_proj, t + 1)
                fn(hsq[:, t * D:(t + 1) * D], bank(4 + 2 * t, 2), ACT.Square).then_inc(o_squared, 1)
                act.wait_ge(variance_ready, 2 + t)
                one = slice(t * HEADS, (t + 1) * HEADS)
                fn(root[:, one], var[:, one], ACT.Sqrt).then_inc(head_root, 1)
            turn_hi_part(3, 0, None)
            hi(HGRN_OUT + 2)
            turn_hi_part(3, 1, None)
            hi(HGRN_OUT + 3)
            hi(MOE)
            load_table(ACT.Sqrt)
            norm_roots(2, lambda t: bank(4 + 2 * t, 2))
            act.wait_ge(small_loaded, 16)
            fn(router_hi[:], router[:], ACT.Copy).then_inc(router_hi_ready, 1)
            hi(MOE + 1)
            turn_hi_part(4, 1, None)
            hi(MOE + 2)
            act.wait_ge(gate_arg, 1)
            fn(weight[:, 1, :], weight[:, 0, :], ACT.Exp).then_inc(gate_exp, 1)
            act.wait_ge(tables_ready, 1)
            jobs = act.value_load(jobs_n[0:1, 0:1], min_val=E, max_val=JOBS)

            def moe_act(n, p, turns):
                act.wait_ge(piece_used, turns * RAW_RING + (p + 1))
                act.wait_ge(moe_hid, n + 1)
                fn(act_sb, bank(0), ACT.Silu).then_inc(moe_silu, 1)

            def moe_round(n):
                act.wait_ge(moe_turned, n + 1)
                fn(ht_hi[:], bank(2), ACT.Copy).then_inc(moe_ht_hi, 1)

            def gather_round(j):
                for b in range(2):
                    act.wait_ge(gathered, j * 2 + b + 1)
                    fn(xt_hi[:, 4 * b:4 * b + 4, 0:P], psum[:, 3 + b, :].rearrange("p (k s) -> p k s", k=4),
                       ACT.Copy).then_inc(xg_hi, 1)

            def take_output(j):
                act.wait_ge(piece_used, j * EXPERT_PIECES + MOE)
                fn(y_hi, bank(5, 2).rearrange("p (k s) -> p k s", k=KT), ACT.Copy).then_inc(y_rounded, 1)

            def moe_split_step(n, turns, between=None):
                for p in range(4, 8):
                    if p == 6 and between:
                        between()
                    hi(MOE + p, turns)
                moe_round(n)
                moe_act(n + 1, MOE + 5, turns)
                for p in range(8, 10):
                    hi(MOE + p, turns)

            def job(j, peeled=False):
                turns = j * EXPERT_TURNS
                n = j * MOE_STEPS

                def turned_pick():
                    act.wait_ge(pick_turned, j + 1)
                    fn(pick_t[:], bank(7)[:, 0:TT * P], ACT.Copy).then_inc(pick_t_ready, 1)

                for p in range(4):
                    if p == 2:
                        take_output(j)
                    if not peeled or p >= SPLIT_RING:
                        hi(MOE + p, turns)
                moe_act(n, MOE + 1, turns)
                moe_split_step(n, turns, turned_pick)
                with act.Fori(1, MOE_STEPS - 1) as c:
                    moe_split_step(n + c, turns + c)
                for p in range(2):
                    hi(MOE + 4 + p, turns + (MOE_STEPS - 1))
                moe_round(n + (MOE_STEPS - 1))
                gather_round(j + 1)

            gather_round(0)
            job(0, True)
            with act.Fori(1, jobs) as j:
                job(j)
            take_output(jobs)
            act.wait_ge(moe_done, 1)
            norm_roots(3, lambda t: acc[:, t, :])

        @block.vector
        def _(dve):
            v = nc.vector
            steps = [0]

            def step(ins):
                steps[0] += 1
                ins.then_inc(dve_step, 1)
                dve.wait_ge(dve_step, steps[0])

            def lo(p, turns=0):
                dve.wait_ge(hi_ready, turns * RAW_RING + (p + 1))
                v.tensor_tensor(w_lo[:, p % SPLIT_RING, :], raw_piece(p, turns),
                                w_hi[:, p % SPLIT_RING, :].bitcast(F32), ALU.subtract).then_inc(lo_ready, 1)

            def inverse_root(r, va, ro, nw):
                step(v.reciprocal(ro, ro))
                step(v.tensor_tensor(nw, ro, ro, ALU.mult))
                step(v.tensor_tensor(nw, nw, va, ALU.mult))
                step(v.scalar_tensor_tensor(out=r, in0=nw, scalar=-3.0, in1=ro, op0=ALU.add, op1=ALU.mult))

            def row_factor(n, t, pre):
                one = slice(t, t + 1)
                dve.wait_ge(squares_ready, norm_no(n, t, pre) + 1)
                step(v.tensor_scalar(var[:, one], ssq[:, one], 1.0 / D, EPS, ALU.mult, ALU.add))
                dve.wait_ge(root_ready, norm_no(n, t, pre) + 1)
                inverse_root(rstd[:, one], var[:, one], root[:, one], newton[:, 0, one])

            def pre_norm(n, t):
                row_factor(n, t, 1)
                v.tensor_scalar(tok[:, t, :], h[:, t, :], rstd[:, t:t + 1], -0.5, ALU.mult, ALU.mult).then_inc(
                    normed, 1)

            def post_norm(n, t, src):
                dve.wait_ge(row_loaded[1], 16 * (n + 1))
                dve.wait_ge(squares_ready, norm_no(n, t, 0) + 1)
                v.scalar_tensor_tensor(out=tok[:, t, :], in0=src, scalar=-0.5, in1=row[:, 1, :],
                                       op0=ALU.mult, op1=ALU.mult).then_inc(gained, 1)
                row_factor(n, t, 0)
                dve.wait_ge(gained, TT * n + t + 1)
                v.scalar_tensor_tensor(out=h[:, t, :], in0=tok[:, t, :], scalar=rstd[:, t:t + 1],
                                       in1=h[:, t, :], op0=ALU.mult, op1=ALU.add).then_inc(residual_ready, 1)
                if t == TT - 1:
                    v.memset(tick[:], 0.0).then_inc(row_used[1], 1)
                dve.wait_ge(residual_ready, TT * n + t + 1)

            def turn_lo_part(n, t, gain):
                tokens = slice(t * P, (t + 1) * P)
                for kh in range(2):
                    dve.wait_ge(turn_hi, 4 * (4 * n + 2 * t + kh + 1))
                    four = slice(4 * kh, 4 * kh + 4)
                    if gain is None:
                        ins = v.tensor_tensor(xt_lo[:, four, tokens],
                                              bank(2 * t + kh).rearrange("p (k s) -> p k s", k=4),
                                              xt_hi[:, four, tokens].bitcast(F32), ALU.subtract)
                    else:
                        for k in range(4 * kh, 4 * kh + 4):
                            ins = v.scalar_tensor_tensor(
                                out=xt_lo[:, k, tokens], in0=psum[:, 2 * t + kh, (k % 4) * P:(k % 4 + 1) * P],
                                scalar=cols[:, gain + k:gain + k + 1], in1=xt_hi[:, k, tokens].bitcast(F32),
                                op0=ALU.mult, op1=ALU.subtract)
                    ins.then_inc(turn_lo, 1)

            pre_norm(-1, 0)
            dve.wait_ge(gains_turned, 1)
            v.tensor_copy(cols[:, 0:B_IN], psum[:, 4, 0:B_IN]).then_inc(gains_ready, 1)
            pre_norm(-1, 1)
            dve.wait_ge(gains_ready, 1)
            for t in range(TT):
                turn_lo_part(0, t, NG)
            lo(0)
            lo(1)
            dve.wait_ge(cols_turned, 1)
            v.tensor_copy(cols[:, B_IN:ROWS0], psum[:, 5, B_IN:ROWS0])
            v.tensor_copy(cols[:, TAPS:TAPS + W * KT], psum[:, 5, P:P + W * KT]).then_inc(cols_ready, 1)
            dve.wait_ge(cols_ready, 1)
            lo(2)

            step(v.memset(conv_u[:, :, 0:W - 1], 0.0))
            UNROLL = 6

            def glu(c):
                for b in range(2):
                    k = 2 * c + b
                    dve.wait_ge(glu_sig, k + 1)
                    ins = v.scalar_tensor_tensor(
                        out=conv_u[:, k, W - 1:], in0=psum[:, 2 * (c % 2), b * S:(b + 1) * S],
                        scalar=cols[:, B_IN + k:B_IN + k + 1], in1=conv_sig[:, 2 * (c % 2) + b, :],
                        op0=ALU.add, op1=ALU.mult)
                ins.then_inc(glu_out, 1)
                dve.wait_ge(glu_out, c + 1)

            def conv_part(i, part):
                k = DVE_CONV[i]
                even, odd = conv_y[:, k, :], conv_sq[:, k, :]
                if part == 0:
                    v.memset(odd, 0.0).then_inc(tap_added, 1)
                    v.tensor_scalar(even, conv_u[:, k, 0:S], cols[:, tap_col(0, k):tap_col(0, k) + 1],
                                    cols[:, DW_B + k:DW_B + k + 1], ALU.mult, ALU.add).then_inc(tap_added, 1)
                first, end = (0, (SHARED_TAP - 1) // UNROLL) if k == SHARED else ((0, 3), (3, 5))[part]
                with dve.Fori(first, end) as turn:
                    for u in range(UNROLL):
                        acc_buf = even if u % 2 else odd
                        dve.wait_ge(tap_added, turn * UNROLL + ((W + 1) * i + 1 + u))
                        v.scalar_tensor_tensor(
                            out=acc_buf, in0=conv_u[:, k, bass.ds(turn * UNROLL + (1 + u), S)],
                            scalar=cols[:, bass.ds(turn * (UNROLL * KT) + (TAPS + KT * (1 + u) + k), 1)],
                            in1=acc_buf, op0=ALU.mult, op1=ALU.add).then_inc(tap_added, 1)
                if k == SHARED:
                    dve.wait_ge(tap_added, (W + 1) * i + SHARED_TAP + 1)
                    v.tensor_tensor(even, even, odd, ALU.add).then_inc(tap_added, 1)
                    dve.wait_ge(tap_added, (W + 1) * i + SHARED_TAP + 2)
                    dve.wait_ge(diag_used, W * len(PE_CONV) + W - SHARED_TAP)
                    v.tensor_tensor(even, even, bank(7)[:, 0:S], ALU.add).then_inc(conv_done, 1)
                elif part:
                    dve.wait_ge(tap_added, (W + 1) * (i + 1))
                    v.tensor_tensor(even, even, odd, ALU.add).then_inc(conv_done, 1)

            assert W == 5 * UNROLL + 1 and (SHARED_TAP - 1) % UNROLL == 0 and DVE_CONV[-1] == SHARED
            lo(3)
            glu(0)
            lo(4)
            conv_part(0, 0)
            lo(5)
            conv_part(0, 1)
            glu(1)
            lo(6)
            conv_part(1, 0)
            lo(7)
            conv_part(1, 1)
            glu(2)
            lo(8)
            conv_part(2, 0)
            conv_part(2, 1)
            glu(3)
            conv_part(3, 0)
            conv_part(3, 1)
            conv_part(4, 0)
            lo(CONV_OUT + 1)
            dve.wait_ge(mean_sum, 1)
            step(v.tensor_scalar(conv_mean, psum[:, 4, 0:S], 1.0 / D, None, ALU.mult))
            for k in range(KT):
                v.tensor_tensor(conv_y[:, k, :], conv_y[:, k, :], conv_mean, ALU.subtract).then_inc(centred, 1)
            lo(CONV_OUT + 2)
            dve.wait_ge(var_sum, 1)
            v.tensor_scalar(conv_var, psum[:, 5, 0:S], 1.0 / D, EPS, ALU.mult, ALU.add).then_inc(variance_ready, 1)
            dve.wait_ge(conv_root, 1)
            inverse_root(conv_r, conv_var, conv_t, conv_mean)
            for k in range(KT):
                v.scalar_tensor_tensor(out=conv_y[:, k, :], in0=conv_y[:, k, :], scalar=-0.5, in1=conv_r,
                                       op0=ALU.mult, op1=ALU.mult).then_inc(conv_scaled, 1)
            for n in range(4):
                dve.wait_ge(conv_hi, n + 1)
                pair = slice(2 * n, 2 * n + 2)
                v.tensor_tensor(xt_lo[:, pair, :], conv_sq[:, pair, :], xt_hi[:, pair, :].bitcast(F32),
                                ALU.subtract).then_inc(conv_lo, 1)
            b0, b1 = cols[:, LB:LB + KT], cols[:, LB + KT:LB + 2 * KT]
            step(v.tensor_tensor(lb_t[:, 4, :], b0, b1, ALU.max))
            v.tensor_tensor(lb_t[:, 0, :], b0, lb_t[:, 4, :], ALU.subtract)
            v.tensor_tensor(lb_t[:, 1, :], b1, lb_t[:, 4, :], ALU.subtract).then_inc(lb_arg, 1)
            dve.wait_ge(lb_exp, 1)
            step(v.tensor_tensor(lb_t[:, 4, :], lb_t[:, 2, :], lb_t[:, 3, :], ALU.add))
            step(v.reciprocal(lb_t[:, 5, :], lb_t[:, 4, :]))
            step(v.tensor_tensor(lb_c[:, 0, :], lb_t[:, 3, :], lb_t[:, 5, :], ALU.mult))
            step(v.tensor_scalar(lb_c[:, 1, :], lb_c[:, 0, :], -1.0, 1.0, ALU.mult, ALU.add))
            dve.wait_ge(consts_ready, 4)
            xor_t, xor_f, mask_f = scratch[:, 15000:15128], scratch[:, 15128:15256], scratch[:, 15256:15384]
            step(v.tensor_copy(slot_id[:], slot_i))
            step(v.tensor_tensor(xor_t.bitcast(I32), slot_i, slot_p[:].to_broadcast([P, P]), ALU.bitwise_xor))
            step(v.tensor_copy(xor_f, xor_t.bitcast(I32)))
            step(v.tensor_tensor(xor_f, xor_f, before[:], ALU.mult))
            for i, length in enumerate(LEVELS):
                step(v.tensor_scalar(mask_f, xor_f, float(length), None, ALU.is_ge))
                step(v.scalar_tensor_tensor(out=level_mask[:, i, :], in0=xor_f, scalar=float(2 * length),
                                            in1=mask_f, op0=ALU.is_lt, op1=ALU.mult))
            lo(CONV_OUT + 3)
            lo(FFN0)
            dve.wait_ge(row_loaded[0], 16)
            def add_bias(t):
                dve.wait_ge(tile_done, 1) if t == 0 else dve.wait_ge(piece_used, CONV_OUT + 4)
                v.tensor_tensor(biased[:, t, :], bank(4 + 2 * t, 2), row[:, 0, :], ALU.add).then_inc(source_ready, 1)
                dve.wait_ge(source_ready, t + 1)

            add_bias(0)
            post_norm(0, 0, biased[:, 0, :])
            add_bias(1)
            v.memset(tick[:], 0.0).then_inc(row_used[0], 1)
            pre_norm(0, 0)
            post_norm(0, 1, biased[:, 1, :])
            turn_lo_part(1, 0, NG + 2 * KT)
            pre_norm(0, 1)
            lo(FFN0 + 1)
            turn_lo_part(1, 1, NG + 2 * KT)

            def ffn_mult(c):
                dve.wait_ge(ffn_silu, c + 1)
                v.tensor_tensor(hid.rearrange("p (t n) -> p t n", t=TT), psum[:, 0:TT, FFN_CHUNK:2 * FFN_CHUNK],
                                act_sb.rearrange("p (t n) -> p t n", t=TT), ALU.mult).then_inc(ffn_hid, 1)

            def ffn_rest(c):
                dve.wait_ge(ffn_ht_hi, c + 1)
                v.tensor_tensor(ht_lo[:], bank(2), ht_hi[:].bitcast(F32), ALU.subtract).then_inc(ffn_ht_lo, 1)

            with dve.Fori(0, FFN_STEPS // 2) as i:
                for j in range(2):
                    p = FFN0 + 2 + 3 * j
                    c = i * 2 + j
                    lo(p, i)
                    ffn_mult(c)
                    lo(p + 1, i)
                    lo(p + 2, i)
                    ffn_rest(c)
            lo(HGRN_QF - 1)
            ffn_mult(FFN_STEPS - 1)
            lo(HGRN_QF)
            ffn_rest(FFN_STEPS - 1)
            lo(HGRN_QF + 1)
            for t in range(TT):
                post_norm(1, t, bank(4 + 2 * t, 2))
                if t:
                    turn_lo_part(2, 0, NG + 4 * KT)
                pre_norm(1, t)
            turn_lo_part(2, 1, NG + 4 * KT)
            lo(HGRN_QF + 2)
            lo(HGRN_QF + 3)

            for c in range(4):
                part = slice(c * 512, (c + 1) * 512)
                dve.wait_ge(qf_sig, 2 * c + 1)
                for k in (2 * c, 2 * c + 1):
                    one = slice(k * S, (k + 1) * S)
                    ins = v.tensor_scalar(lev[0][:, one], hk[:, one], lb_c[:, 1, k:k + 1], lb_c[:, 0, k:k + 1],
                                          ALU.mult, ALU.add)
                ins.then_inc(forget_ready, 1)
                dve.wait_ge(forget_ready, c + 1)
                v.tensor_scalar(hk[:, part], lev[0][:, part], -1.0, 1.0, ALU.mult, ALU.add).then_inc(k_ready, 1)
                dve.wait_ge(qf_sig, 2 * c + 2)
                v.tensor_tensor(hq[:, part], bank(2 * (c % 2)), hq[:, part], ALU.mult).then_inc(q_ready, 1)
                for p in (HGRN_QF + 4 + 2 * c, HGRN_QF + 5 + 2 * c)[:2 * (c < 3)]:
                    lo(p)
            dve.wait_ge(k_ready, 4)
            dve.wait_ge(q_ready, 4)
            for b in range(HB):
                if b * P in (0, 1536):
                    dve.wait_ge(log_ready, 1 + b * P // 1536)
                one = slice(b * P, (b + 1) * P)
                ins = v.tensor_tensor_scan(hg[:, one], ones[:], lev[0][:, one], 0.0, ALU.mult, ALU.add)
            step(ins)

            def halves(buf, n):
                length = P if n == len(LEVELS) + 1 else LEVELS[n - 1]
                w = buf.rearrange("p (x two l) -> p x two l", two=2, l=length)
                return w[:, :, 0, :], w[:, :, 1, :], length

            def level_diff(n):
                if n > 2:
                    dve.wait_ge(level_scores, n - 1)
                left, right, length = halves(lev[n % 2], n)
                g_left, g_right, _ = halves(hg, n)
                end = g_left[:, :, length - 1:length].to_broadcast([P, HEADS * S // (2 * length), length])
                v.tensor_tensor(left, end, g_left, ALU.subtract)
                if n == len(LEVELS) + 1:
                    v.tensor_copy(right, g_right).then_inc(level_arg, 1)
                else:
                    v.tensor_tensor(right, g_right, end, ALU.subtract).then_inc(level_arg, 1)

            def level_mult(n):
                dve.wait_ge(level_exp, n)
                left, right, _ = halves(lev[n % 2], n)
                v.tensor_tensor(left, left, halves(hk, n)[0], ALU.mult)
                v.tensor_tensor(right, right, halves(hq, n)[1], ALU.mult).then_inc(level_factors, 1)

            def level_take(n):
                dve.wait_ge(level_scores, n + 1)
                if n:
                    dve.wait_ge(level_taken, n)
                by_pair = s_same.rearrange("p (b t) -> p b t", b=HB)
                if n == 0:
                    v.tensor_tensor(by_pair, bank(4, 4).rearrange("p (b t) -> p b t", b=HB),
                                    ident[:].rearrange("p (a t) -> p a t", a=1).to_broadcast([P, HB, P]),
                                    ALU.mult).then_inc(level_taken, 1)
                elif n == len(LEVELS) + 1:
                    v.tensor_copy(s_cross, bank(group_bank(n), 2)).then_inc(level_taken, 1)
                else:
                    length = LEVELS[n - 1]
                    blocks = P // (2 * length)
                    right = "p b (x two l) -> p b x two l"
                    dst = by_pair.rearrange(right, two=2, l=length)[:, :, :, 1, :]
                    mask = level_mask[:, n - 1:n, :].rearrange(right, two=2, l=length)[:, :, :, 1, :]
                    src = bank(group_bank(n), 2).rearrange("p (b x l) -> p b x l", b=HB, l=length)
                    v.copy_predicated(dst, mask.to_broadcast([P, HB, blocks, length]), src).then_inc(level_taken, 1)

            level_diff(1)
            lo(HGRN_VG + 2)
            level_mult(1)
            for n in range(1, 8):
                level_diff(n + 1)
                level_take(n - 1)
                if HGRN_VG + 2 + n < HGRN_OUT:
                    lo(HGRN_VG + 2 + n)
                level_mult(n + 1)
            level_take(7)
            level_take(8)
            dve.wait_ge(og_ready, 1)
            dve.wait_ge(row_loaded[0], 32)
            gain = row[:, 0:1, 0:P].to_broadcast([P, HB, P])
            by_head = "p (b c) -> p b c"
            step(v.scalar_tensor_tensor(out=hog.rearrange(by_head, b=HB), in0=hog.rearrange(by_head, b=HB),
                                        scalar=-0.5, in1=gain, op0=ALU.mult, op1=ALU.mult))
            v.memset(tick[:], 0.0).then_inc(row_used[0], 1)
            dve.wait_ge(row_used[0], 2)
            for t in range(TT):
                one = slice(t * HEADS, (t + 1) * HEADS)
                dve.wait_ge(o_squared, t + 1)
                step(v.tensor_reduce(var[:, one], hsq[:, t * D:(t + 1) * D].rearrange(by_head, b=HEADS), AX.X,
                                     ALU.add))
                v.tensor_scalar(var[:, one], var[:, one], 1.0 / P, EPS, ALU.mult, ALU.add).then_inc(
                    variance_ready, 1)
                cut = slice(t * D, (t + 1) * D)
                dve.wait_ge(variance_ready, 2 + t)
                dve.wait_ge(head_root, t + 1)
                inverse_root(rstd[:, one], var[:, one], root[:, one], newton[:, 0, one])
                scale = rstd[:, one].rearrange("p (b a) -> p b a", a=1).to_broadcast([P, HEADS, P])
                step(v.tensor_tensor(hq[:, cut].rearrange(by_head, b=HEADS),
                                     bank(4 + 2 * t, 2).rearrange(by_head, b=HEADS), scale, ALU.mult))
                v.tensor_tensor(hq[:, cut], hq[:, cut], hog[:, cut], ALU.mult).then_inc(normed, 1)
            turn_lo_part(3, 0, None)
            lo(HGRN_OUT)
            lo(HGRN_OUT + 1)
            turn_lo_part(3, 1, None)
            lo(HGRN_OUT + 2)
            lo(HGRN_OUT + 3)
            lo(MOE)
            dve.wait_ge(row_loaded[0], 48)
            for t in range(TT):
                post_norm(2, t, bank(4 + 2 * t, 2))
                if t:
                    turn_lo_part(4, 0, None)
                row_factor(2, t, 1)
                step(v.tensor_scalar(rstd[:, t:t + 1], rstd[:, t:t + 1], -0.5, None, ALU.mult))
                v.scalar_tensor_tensor(out=mx[:, t, :], in0=h[:, t, :], scalar=rstd[:, t:t + 1],
                                       in1=row[:, 0, :], op0=ALU.mult, op1=ALU.mult).then_inc(normed, 1)
            dve.wait_ge(router_hi_ready, 1)
            v.tensor_tensor(router_lo[:], router[:], router_hi[:].bitcast(F32), ALU.subtract).then_inc(router_split, 1)
            v.memset(acc[:, :, :], 0.0).then_inc(acc_added, 1)
            v.memset(tick[:], 0.0).then_inc(moe_hid, 1)
            v.tensor_scalar(pick_t[:].rearrange("p (t s) -> p t s", t=TT),
                            ones[:].rearrange("p (a s) -> p a s", a=1).to_broadcast([P, TT, P]), 0.0, None,
                            ALU.mult).then_inc(pick_t_ready, 1)
            lo(MOE + 1)
            turn_lo_part(4, 1, None)
            lo(MOE + 2)
            dve.wait_ge(logits_done, 1)
            v.tensor_copy(logits_t, psum[0:E, 7, 0:S]).then_inc(logits_moved, 1)
            dve.wait_ge(logits_turned, 1)
            step(v.tensor_copy(logits[:], psum[:, 7, S:S + TT * E].rearrange("p (t e) -> p t e", t=TT)))
            for t in range(TT):
                step(v.max(top[:, t, :], logits[:, t, :]))
                step(v.max_index(top_i[:, t, :], top[:, t, :], logits[:, t, :]))
            step(v.tensor_copy(top_f[:], top_i[:]))
            v.tensor_tensor(weight[:, 0, :], top[:, :, 1], top[:, :, 0], ALU.subtract).then_inc(gate_arg, 1)
            for t in range(TT):
                for rank in range(2):
                    step(v.tensor_scalar(chosen[:, rank, t, :], slot_id[:, 0:E], top_f[:, t, rank:rank + 1], None,
                                         ALU.is_equal))
            v.tensor_tensor(sel[:], chosen[:, 0, :, :], chosen[:, 1, :, :], ALU.add).then_inc(sel_ready, 1)
            dve.wait_ge(gate_exp, 1)
            step(v.tensor_scalar(weight[:, 2, :], weight[:, 1, :], 1.0, None, ALU.add))
            step(v.reciprocal(weight[:, 3, :], weight[:, 2, :]))
            step(v.tensor_tensor(weight[:, 2, :], weight[:, 1, :], weight[:, 3, :], ALU.mult))
            for t in range(TT):
                step(v.tensor_scalar(place[:, t, :], chosen[:, 0, t, :], weight[:, 3, t:t + 1], None, ALU.mult))
                step(v.scalar_tensor_tensor(out=gate_of[:, t, 1:E + 1], in0=chosen[:, 1, t, :],
                                            scalar=weight[:, 2, t:t + 1], in1=place[:, t, :],
                                            op0=ALU.mult, op1=ALU.add))
            v.tensor_copy(gate_of[:, :, E + 1:JOBS + 1], gate_of[:, :, 1:E + 1])
            dve.wait_ge(count_done, 1)
            step(v.scalar_tensor_tensor(out=place[:], in0=psum[:, 6, 0:TT * E].rearrange("p (t e) -> p t e", t=TT),
                                        scalar=1.0, in1=sel[:], op0=ALU.add, op1=ALU.mult))
            v.memset(slot_of[:, :, JOBS:JOBS + 1], -1.0)
            v.memset(gate_of[:, :, 0:1], 0.0)
            v.tensor_scalar(slot_of[:, :, 0:E], place[:], -1.0, None, ALU.add)
            v.tensor_scalar(slot_of[:, :, E:JOBS], place[:], -1.0 - P, None, ALU.add)
            step(v.tensor_reduce(busiest[:, 0:1], psum[:, 6, 2 * E:3 * E], AX.X, ALU.max))
            step(v.tensor_scalar(busiest[:, 1:2], busiest[:, 0:1], float(P), float(E), ALU.is_gt, ALU.mult))
            v.tensor_scalar(jobs_n[:], busiest[:, 1:2], float(E), None, ALU.add).then_inc(tables_ready, 1)
            dve.wait_ge(tables_ready, 1)
            jobs = dve.value_load(jobs_n[0:1, 0:1], min_val=E, max_val=JOBS)

            def moe_mult(n, p, turns):
                dve.wait_ge(moe_silu, n + 1)
                dve.wait_ge(piece_used, turns * RAW_RING + (p + 1))
                v.tensor_tensor(hid, bank(1), act_sb, ALU.mult).then_inc(moe_hid, 1)

            def moe_rest(n):
                dve.wait_ge(moe_ht_hi, n + 1)
                v.tensor_tensor(ht_lo[:], bank(2), ht_hi[:].bitcast(F32), ALU.subtract).then_inc(moe_ht_lo, 1)

            def make_pick(j):
                for t in range(TT):
                    ins = v.tensor_scalar(pick[:, t, :], slot_id[:], slot_of[:, t, bass.ds(j, 1)], None, ALU.is_equal)
                ins.then_inc(pick_ready, 1)

            def gather_rest(j):
                for b in range(2):
                    dve.wait_ge(xg_hi, j * 2 + b + 1)
                    v.tensor_tensor(xt_lo[:, 4 * b:4 * b + 4, 0:P],
                                    psum[:, 3 + b, :].rearrange("p (k s) -> p k s", k=4),
                                    xt_hi[:, 4 * b:4 * b + 4, 0:P].bitcast(F32), ALU.subtract).then_inc(xg_lo, 1)

            def add_output(j):
                for t in range(TT):
                    for half in range(2):
                        i = 2 * t + half
                        dve.wait_ge(scattered, j * 4 + i + 1)
                        dve.wait_ge(acc_added, j * 4 + 1)
                        part = acc[:, t, half * BANK:(half + 1) * BANK]
                        v.scalar_tensor_tensor(out=part, in0=bank(SCATTER_BANKS[i]),
                                               scalar=gate_of[:, t, bass.ds(j, 1)], in1=part,
                                               op0=ALU.mult, op1=ALU.add).then_inc(acc_added, 1)

            def output_rest(j):
                dve.wait_ge(y_rounded, j + 1)
                v.tensor_tensor(y_lo, bank(5, 2).rearrange("p (k s) -> p k s", k=KT), y_hi.bitcast(F32),
                                ALU.subtract).then_inc(y_ready, 1)

            def moe_rest_step(n, turns, before_up=None, before_down=None):
                for p in range(4, 8):
                    if p == 6 and before_up:
                        before_up()
                    lo(MOE + p, turns)
                moe_rest(n)
                if before_down:
                    before_down()
                for p in range(8, 10):
                    lo(MOE + p, turns)
                moe_mult(n + 1, MOE + 7, turns)

            def job(j, peeled=False):
                turns = j * EXPERT_TURNS
                n = j * MOE_STEPS

                def next_pick():
                    dve.wait_ge(pick_turned, j + 1)
                    make_pick(j + 1)

                for p in range(4):
                    if p == 2:
                        output_rest(j)
                    if not peeled or p >= SPLIT_RING:
                        lo(MOE + p, turns)
                add_output(j)
                moe_rest_step(n, turns, lambda: moe_mult(n, MOE + 3, turns), next_pick)
                with dve.Fori(1, MOE_STEPS - 1) as c:
                    moe_rest_step(n + c, turns + c)
                for p in range(2):
                    lo(MOE + 4 + p, turns + (MOE_STEPS - 1))
                moe_rest(n + (MOE_STEPS - 1))
                gather_rest(j + 1)

            make_pick(0)
            gather_rest(0)
            job(0, True)
            with dve.Fori(1, jobs) as j:
                job(j)
            output_rest(jobs)
            add_output(jobs)
            v.memset(tick[:], 0.0).then_inc(moe_done, 1)
            dve.wait_ge(moe_done, 1)
            for t in range(TT):
                post_norm(3, t, acc[:, t, :])


_INS = ["x", "norm_g", "conv_w_in", "conv_b_in", "conv_dw_w", "conv_dw_b", "conv_ln_g", "conv_ln_b", "conv_w_out",
        "conv_b_out", "hgrn_w_in", "hgrn_lower_bounds", "hgrn_norm_g", "hgrn_w_out", "ffn_w_gu", "ffn_w_down",
        "moe_router", "moe_w_gu", "moe_w_down"]


def kernel(**inputs):
    import numpy as np
    from concourse import bacc
    from concourse.bass_utils import run_bass_kernel_spmd

    nc = bacc.Bacc("TRN2", target_bir_lowering=False, num_devices=1)
    arrays, args = {}, []
    for name in _INS:
        a = np.ascontiguousarray(inputs[name])
        arrays[f"in_{name}"] = a
        args.append(nc.dram_tensor(f"in_{name}", a.shape, mybir.dt.from_np(a.dtype), kind="ExternalInput").ap())
    out = nc.dram_tensor("out", inputs["x"].shape, F32, kind="ExternalOutput").ap()
    trunk(nc, *args, out)
    r = run_bass_kernel_spmd(nc, [arrays], core_ids=[0])
    return r.results[0]["out"]
```
